# Optimizing a Trainium2 kernel written in Bass

```python
import math
import jax, jax.numpy as jnp
from jax import lax
import numpy as np

D_MODEL = 2048
BATCH = 1
SEQ = 256
DEPTH = 2
DEC_BATCH = 8
DEC_SEQ = 8
PAST_LEN = 2048
PAGE_SIZE = 128

N_EVEN = (DEPTH + 1) // 2
N_ODD = DEPTH // 2
EPS = 1e-6
CONV_W = 4
W_LRU = D_MODEL // 2
LRU_BLOCKS = 16
LRU_BS = W_LRU // LRU_BLOCKS
LRU_C = 8.0
H_GLA = 4
DK_GLA = D_MODEL // (4 * H_GLA)
DV_GLA = D_MODEL // (2 * H_GLA)
GLA_RANK = 16
GLA_TAU = 16.0
GLA_CHUNK = 64
_HK = H_GLA * DK_GLA
_HV = H_GLA * DV_GLA
SPLIT0 = (W_LRU, 2 * W_LRU, 2 * W_LRU + _HK, 2 * W_LRU + 2 * _HK, 2 * W_LRU + 2 * _HK + _HV, 2 * W_LRU + 2 * _HK + 2 * _HV)
IN0_COLS = 2 * W_LRU + 2 * _HK + 2 * _HV + GLA_RANK
MIX0 = W_LRU + _HV
M_PROJ = 2
D_INNER = M_PROJ * D_MODEL
H_M = 4
DH_M = D_INNER // H_M
QKV_BS = 4
M_CHUNK = 64
N_GROUPS = 4
E_PER_GROUP = 4
N_EXPERTS = N_GROUPS * E_PER_GROUP
TOP_K_FINE = 2
D_EXPERT = 256

kernel_name = 'hawk_gla_mlstm_hmoe_step'

def rmsnorm(x, g):
    xf = x.astype(jnp.float32)
    y = xf * lax.rsqrt(jnp.mean(xf * xf, axis=-1, keepdims=True) + EPS)
    return (y * g.astype(jnp.float32)).astype(x.dtype)

def causal_conv(x, buf, w, b):
    T = x.shape[1]
    xp = jnp.concatenate([buf.astype(x.dtype), x], axis=1)
    y = b.astype(x.dtype)
    for j in range(CONV_W):
        y = y + xp[:, j:j + T] * w[j]
    return y, xp[:, T:]

def blockdiag(x, w):
    nb, bi, bo = w.shape
    xb = x.reshape(x.shape[:-1] + (nb, bi))
    return jnp.einsum('btni,nio->btno', xb, w).reshape(x.shape[:-1] + (nb * bo,))

def to_chunks(a, L):
    nc = a.shape[2] // L
    return jnp.moveaxis(a.reshape(a.shape[:2] + (nc, L) + a.shape[3:]), 2, 0)

def from_chunks(a):
    a = jnp.moveaxis(a, 0, 2)
    return a.reshape(a.shape[:2] + (a.shape[2] * a.shape[3],) + a.shape[4:])

def head_rmsnorm(o, g):
    B, H, T, Dh = o.shape
    on = o * lax.rsqrt(jnp.mean(o * o, axis=-1, keepdims=True) + EPS)
    return jnp.transpose(on, (0, 2, 1, 3)).reshape(B, T, H * Dh) * g.astype(jnp.float32)

def head_layernorm(h, g):
    B, H, T, Dh = h.shape
    mu = jnp.mean(h, axis=-1, keepdims=True)
    hc = h - mu
    hn = hc * lax.rsqrt(jnp.mean(hc * hc, axis=-1, keepdims=True) + EPS)
    return jnp.transpose(hn, (0, 2, 1, 3)).reshape(B, T, H * Dh) * g.astype(jnp.float32)

def rg_lru(xc, h0, wa, ba, wx, bx, lam):
    xf = xc.astype(jnp.float32)
    r = jax.nn.sigmoid(blockdiag(xc, wa).astype(jnp.float32) + ba.astype(jnp.float32))
    i = jax.nn.sigmoid(blockdiag(xc, wx).astype(jnp.float32) + bx.astype(jnp.float32))
    log_a = -LRU_C * r * jax.nn.softplus(-lam.astype(jnp.float32))
    a = jnp.exp(log_a)
    b = jnp.sqrt(-jnp.expm1(2.0 * log_a)) * (i * xf)
    b = b.at[:, 0].add(a[:, 0] * h0.astype(jnp.float32))

    def combine(left, right):
        a1, b1 = left
        a2, b2 = right
        return a1 * a2, a2 * b1 + b2

    _, h = lax.associative_scan(combine, (a, b), axis=1)
    return h, h[:, -1]

def gla_chunked(q, k, v, lg, S0):
    T = q.shape[2]
    L = math.gcd(T, GLA_CHUNK)
    mask = jnp.tril(jnp.ones((L, L), dtype=bool))[:, :, None]

    def step(S, inp):
        qc, kc, vc, gc = inp
        bc = jnp.cumsum(gc, axis=2)
        o = jnp.einsum('bhtd,bhde->bhte', qc * jnp.exp(bc), S)
        decay = jnp.exp(jnp.where(mask, bc[:, :, :, None, :] - bc[:, :, None, :, :], -jnp.inf))
        att = jnp.einsum('bhtd,bhsd,bhtsd->bhts', qc, kc, decay)
        o = o + jnp.einsum('bhts,bhse->bhte', att, vc)
        bl = bc[:, :, -1:, :]
        S = jnp.exp(bl[:, :, 0, :])[..., None] * S + jnp.einsum('bhsd,bhse->bhde', kc * jnp.exp(bl - bc), vc)
        return S, o

    S, o = lax.scan(step, S0, (to_chunks(q, L), to_chunks(k, L), to_chunks(v, L), to_chunks(lg, L)))
    return from_chunks(o), S

def mlstm_chunked(q, k, v, ig, lf, C0, n0, m0):
    T = q.shape[2]
    L = math.gcd(T, M_CHUNK)
    mask = jnp.tril(jnp.ones((L, L), dtype=bool))

    def step(carry, inp):
        C, n, m = carry
        qc, kc, vc, ic, fc = inp
        F = jnp.cumsum(fc, axis=-1)
        Dm = jnp.where(mask, F[..., :, None] - F[..., None, :] + ic[..., None, :], -jnp.inf)
        prev = m[..., None] + F
        mt = jnp.maximum(prev, jnp.max(Dm, axis=-1))
        wprev = jnp.exp(prev - mt)
        s = jnp.einsum('bhtd,bhsd->bhts', qc, kc) * jnp.exp(Dm - mt[..., None])
        num = wprev[..., None] * jnp.einsum('bhtd,bhde->bhte', qc, C) + jnp.einsum('bhts,bhse->bhte', s, vc)
        den = wprev * jnp.einsum('bhtd,bhd->bht', qc, n) + jnp.sum(s, axis=-1)
        h = num / jnp.maximum(jnp.abs(den), jnp.exp(-mt))[..., None]
        mL = mt[..., -1]
        wC = jnp.exp(m + F[..., -1] - mL)
        wS = jnp.exp(F[..., -1:] - F + ic - mL[..., None])
        C = wC[..., None, None] * C + jnp.einsum('bhsd,bhse->bhde', kc * wS[..., None], vc)
        n = wC[..., None] * n + jnp.einsum('bhs,bhsd->bhd', wS, kc)
        return (C, n, mL), h

    (C, n, m), h = lax.scan(step, (C0, n0, m0), (to_chunks(q, L), to_chunks(k, L), to_chunks(v, L), to_chunks(ig, L), to_chunks(lf, L)))
    return from_chunks(h), C, n, m

def rglru_gla_mixer(xn, lru_buf, lru_h, gla_S, w_in, lru_conv_w, lru_conv_b, lru_wa, lru_ba, lru_wx, lru_bx, lru_lam, gla_wa2, gla_ba2, gla_norm_g, w_out):
    B, T, _ = xn.shape
    proj = xn @ w_in
    xa, ga, q, k, v, g, alr = jnp.split(proj, SPLIT0, axis=-1)
    xc, new_buf = causal_conv(xa, lru_buf, lru_conv_w, lru_conv_b)
    h, h_last = rg_lru(xc, lru_h, lru_wa, lru_ba, lru_wx, lru_bx, lru_lam)
    ya = h * jax.nn.gelu(ga.astype(jnp.float32))
    lg = jax.nn.log_sigmoid((alr @ gla_wa2).astype(jnp.float32) + gla_ba2.astype(jnp.float32)) / GLA_TAU

    def heads(a, d):
        return jnp.transpose(a.reshape(B, T, H_GLA, d), (0, 2, 1, 3)).astype(jnp.float32)

    o, S_new = gla_chunked(heads(q, DK_GLA) * (DK_GLA ** -0.5), heads(k, DK_GLA), heads(v, DV_GLA), heads(lg, DK_GLA), gla_S.astype(jnp.float32))
    yb = head_rmsnorm(o, gla_norm_g) * jax.nn.silu(g.astype(jnp.float32))
    y = jnp.concatenate([ya, yb], axis=-1).astype(xn.dtype) @ w_out
    return y, new_buf.astype(lru_buf.dtype), h_last.astype(lru_h.dtype), S_new.astype(gla_S.dtype)

def mlstm_mixer(xn, conv_buf, C0, n0, m0, w_up, conv_w, conv_b, wq, wk, wv, w_ig, b_ig, w_fg, b_fg, skip, norm_g, w_down):
    B, T, _ = xn.shape
    xm, z = jnp.split(xn @ w_up, 2, axis=-1)
    xc, new_buf = causal_conv(xm, conv_buf, conv_w, conv_b)
    xc = jax.nn.silu(xc)
    q = blockdiag(xc, wq)
    k = blockdiag(xc, wk)
    v = blockdiag(xm, wv)
    qkv = jnp.concatenate([q, k, v], axis=-1)
    ig = (qkv @ w_ig).astype(jnp.float32) + b_ig.astype(jnp.float32)
    lf = jax.nn.log_sigmoid((qkv @ w_fg).astype(jnp.float32) + b_fg.astype(jnp.float32))

    def heads(a):
        return jnp.transpose(a.reshape(B, T, H_M, DH_M), (0, 2, 1, 3)).astype(jnp.float32)

    h, C, n, m = mlstm_chunked(heads(q), heads(k) * (DH_M ** -0.5), heads(v), jnp.transpose(ig, (0, 2, 1)), jnp.transpose(lf, (0, 2, 1)), C0.astype(jnp.float32), n0.astype(jnp.float32), m0.astype(jnp.float32))
    hn = head_layernorm(h, norm_g)
    out = (hn + skip.astype(jnp.float32) * xc.astype(jnp.float32)) * jax.nn.silu(z.astype(jnp.float32))
    y = out.astype(xn.dtype) @ w_down
    return y, new_buf.astype(conv_buf.dtype), C.astype(C0.dtype), n.astype(n0.dtype), m.astype(m0.dtype)

def hier_moe(xn, w_rg, b_rg, w_re, b_re, w_gate, w_up, w_down):
    B, T, D = xn.shape
    xf = xn.reshape(B * T, D)
    gp = jax.nn.softmax((xf @ w_rg).astype(jnp.float32) + b_rg.astype(jnp.float32), axis=-1)
    p_g, g_idx = lax.top_k(gp, 1)
    g_oh = jax.nn.one_hot(g_idx[:, 0], N_GROUPS, dtype=jnp.float32)
    el = ((xf @ w_re).astype(jnp.float32) + b_re.astype(jnp.float32)).reshape(B * T, N_GROUPS, E_PER_GROUP)
    el_sel = jnp.einsum('nge,ng->ne', el, g_oh)
    ep = jax.nn.softmax(el_sel, axis=-1)
    tv, ti = lax.top_k(ep, TOP_K_FINE)
    tv = tv / jnp.sum(tv, axis=-1, keepdims=True) * p_g
    eid = g_idx * E_PER_GROUP + ti
    gates = jnp.sum(jax.nn.one_hot(eid, N_EXPERTS, dtype=jnp.float32) * tv[..., None], axis=1)
    h = jax.nn.silu(jnp.einsum('nd,edf->nef', xf, w_gate)) * jnp.einsum('nd,edf->nef', xf, w_up)
    y = jnp.einsum('nef,efd->nd', h * gates[:, :, None].astype(h.dtype), w_down)
    return y.reshape(B, T, D)

def trunk(x, st_lru_conv, st_lru_h, st_gla_S, st_m_conv, st_m_C, st_m_n, st_m_m,
          norm_mix_g, norm_ffn_g, norm_final_g,
          l0_w_in, l0_lru_conv_w, l0_lru_conv_b, l0_lru_wa, l0_lru_ba, l0_lru_wx, l0_lru_bx, l0_lru_lam, l0_gla_wa2, l0_gla_ba2, l0_gla_norm_g, l0_w_out,
          l1_w_up, l1_conv_w, l1_conv_b, l1_wq, l1_wk, l1_wv, l1_w_ig, l1_b_ig, l1_w_fg, l1_b_fg, l1_skip, l1_norm_g, l1_w_down,
          moe_w_rg, moe_b_rg, moe_w_re, moe_b_re, moe_w_gate, moe_w_up, moe_w_down):
    o_lru_conv, o_lru_h, o_gla_S, o_m_conv, o_m_C, o_m_n, o_m_m = [], [], [], [], [], [], []
    for layer in range(DEPTH):
        j = layer // 2
        xn = rmsnorm(x, norm_mix_g[layer])
        if layer % 2 == 0:
            y, nb, nh, nS = rglru_gla_mixer(xn, st_lru_conv[j], st_lru_h[j], st_gla_S[j], l0_w_in[j], l0_lru_conv_w[j], l0_lru_conv_b[j], l0_lru_wa[j], l0_lru_ba[j], l0_lru_wx[j], l0_lru_bx[j], l0_lru_lam[j], l0_gla_wa2[j], l0_gla_ba2[j], l0_gla_norm_g[j], l0_w_out[j])
            o_lru_conv.append(nb)
            o_lru_h.append(nh)
            o_gla_S.append(nS)
        else:
            y, nb, nC, nn, nm = mlstm_mixer(xn, st_m_conv[j], st_m_C[j], st_m_n[j], st_m_m[j], l1_w_up[j], l1_conv_w[j], l1_conv_b[j], l1_wq[j], l1_wk[j], l1_wv[j], l1_w_ig[j], l1_b_ig[j], l1_w_fg[j], l1_b_fg[j], l1_skip[j], l1_norm_g[j], l1_w_down[j])
            o_m_conv.append(nb)
            o_m_C.append(nC)
            o_m_n.append(nn)
            o_m_m.append(nm)
        x = x + y.astype(x.dtype)
        x = x + hier_moe(rmsnorm(x, norm_ffn_g[layer]), moe_w_rg[layer], moe_b_rg[layer], moe_w_re[layer], moe_b_re[layer], moe_w_gate[layer], moe_w_up[layer], moe_w_down[layer]).astype(x.dtype)
    y = rmsnorm(x, norm_final_g)
    return (y, jnp.stack(o_lru_conv), jnp.stack(o_lru_h), jnp.stack(o_gla_S), jnp.stack(o_m_conv), jnp.stack(o_m_C), jnp.stack(o_m_n), jnp.stack(o_m_m))

def setup_inputs(seed: int = 0) -> dict:
    key = jax.random.key(seed)
    ks = iter(jax.random.split(key, 64))
    f32 = jnp.float32

    def nrm(shape, s):
        return jax.random.normal(next(ks), shape, f32) * s

    u = jax.random.uniform(next(ks), (N_EVEN, W_LRU), f32, minval=0.9, maxval=0.999)
    sa = u ** (1.0 / LRU_C)
    lam = jnp.log(sa) - jnp.log1p(-sa)
    return {
        'x_prompt': nrm((BATCH, SEQ, D_MODEL), 1.0),
        'x_sample': nrm((DEC_BATCH, DEC_SEQ, D_MODEL), 1.0),
        'state_lru_conv': nrm((N_EVEN, DEC_BATCH, CONV_W - 1, W_LRU), 1.0),
        'state_lru_h': nrm((N_EVEN, DEC_BATCH, W_LRU), 0.5),
        'state_gla_S': nrm((N_EVEN, DEC_BATCH, H_GLA, DK_GLA, DV_GLA), 1.0),
        'state_mlstm_conv': nrm((N_ODD, DEC_BATCH, CONV_W - 1, D_INNER), 1.0),
        'state_mlstm_C': nrm((N_ODD, DEC_BATCH, H_M, DH_M, DH_M), 1.0),
        'state_mlstm_n': nrm((N_ODD, DEC_BATCH, H_M, DH_M), 1.0),
        'state_mlstm_m': nrm((N_ODD, DEC_BATCH, H_M), 2.0),
        'norm_mix_g': 1.0 + nrm((DEPTH, D_MODEL), 0.02),
        'norm_ffn_g': 1.0 + nrm((DEPTH, D_MODEL), 0.02),
        'norm_final_g': 1.0 + nrm((D_MODEL,), 0.02),
        'l0_w_in': nrm((N_EVEN, D_MODEL, IN0_COLS), D_MODEL ** -0.5),
        'l0_lru_conv_w': nrm((N_EVEN, CONV_W, W_LRU), CONV_W ** -0.5),
        'l0_lru_conv_b': nrm((N_EVEN, W_LRU), 0.01),
        'l0_lru_wa': nrm((N_EVEN, LRU_BLOCKS, LRU_BS, LRU_BS), LRU_BS ** -0.5),
        'l0_lru_ba': nrm((N_EVEN, W_LRU), 0.01),
        'l0_lru_wx': nrm((N_EVEN, LRU_BLOCKS, LRU_BS, LRU_BS), LRU_BS ** -0.5),
        'l0_lru_bx': nrm((N_EVEN, W_LRU), 0.01),
        'l0_lru_lam': lam,
        'l0_gla_wa2': nrm((N_EVEN, GLA_RANK, _HK), GLA_RANK ** -0.5),
        'l0_gla_ba2': nrm((N_EVEN, _HK), 0.1),
        'l0_gla_norm_g': 1.0 + nrm((N_EVEN, _HV), 0.02),
        'l0_w_out': nrm((N_EVEN, MIX0, D_MODEL), MIX0 ** -0.5),
        'l1_w_up': nrm((N_ODD, D_MODEL, 2 * D_INNER), D_MODEL ** -0.5),
        'l1_conv_w': nrm((N_ODD, CONV_W, D_INNER), CONV_W ** -0.5),
        'l1_conv_b': nrm((N_ODD, D_INNER), 0.01),
        'l1_wq': nrm((N_ODD, D_INNER // QKV_BS, QKV_BS, QKV_BS), QKV_BS ** -0.5),
        'l1_wk': nrm((N_ODD, D_INNER // QKV_BS, QKV_BS, QKV_BS), QKV_BS ** -0.5),
        'l1_wv': nrm((N_ODD, D_INNER // QKV_BS, QKV_BS, QKV_BS), QKV_BS ** -0.5),
        'l1_w_ig': nrm((N_ODD, 3 * D_INNER, H_M), 0.1 * (3 * D_INNER) ** -0.5),
        'l1_b_ig': nrm((N_ODD, H_M), 0.1),
        'l1_w_fg': nrm((N_ODD, 3 * D_INNER, H_M), 0.1 * (3 * D_INNER) ** -0.5),
        'l1_b_fg': jnp.linspace(3.0, 6.0, H_M, dtype=f32)[None, :] + nrm((N_ODD, H_M), 0.1),
        'l1_skip': 1.0 + nrm((N_ODD, D_INNER), 0.02),
        'l1_norm_g': 1.0 + nrm((N_ODD, D_INNER), 0.02),
        'l1_w_down': nrm((N_ODD, D_INNER, D_MODEL), D_INNER ** -0.5),
        'moe_w_rg': nrm((DEPTH, D_MODEL, N_GROUPS), D_MODEL ** -0.5),
        'moe_b_rg': nrm((DEPTH, N_GROUPS), 0.01),
        'moe_w_re': nrm((DEPTH, D_MODEL, N_EXPERTS), D_MODEL ** -0.5),
        'moe_b_re': nrm((DEPTH, N_EXPERTS), 0.01),
        'moe_w_gate': nrm((DEPTH, N_EXPERTS, D_MODEL, D_EXPERT), D_MODEL ** -0.5),
        'moe_w_up': nrm((DEPTH, N_EXPERTS, D_MODEL, D_EXPERT), D_MODEL ** -0.5),
        'moe_w_down': nrm((DEPTH, N_EXPERTS, D_EXPERT, D_MODEL), D_EXPERT ** -0.5),
    }

def reference(x_prompt, x_sample, state_lru_conv, state_lru_h, state_gla_S, state_mlstm_conv, state_mlstm_C, state_mlstm_n, state_mlstm_m,
              norm_mix_g, norm_ffn_g, norm_final_g,
              l0_w_in, l0_lru_conv_w, l0_lru_conv_b, l0_lru_wa, l0_lru_ba, l0_lru_wx, l0_lru_bx, l0_lru_lam, l0_gla_wa2, l0_gla_ba2, l0_gla_norm_g, l0_w_out,
              l1_w_up, l1_conv_w, l1_conv_b, l1_wq, l1_wk, l1_wv, l1_w_ig, l1_b_ig, l1_w_fg, l1_b_fg, l1_skip, l1_norm_g, l1_w_down,
              moe_w_rg, moe_b_rg, moe_w_re, moe_b_re, moe_w_gate, moe_w_up, moe_w_down):
    weights = (norm_mix_g, norm_ffn_g, norm_final_g,
               l0_w_in, l0_lru_conv_w, l0_lru_conv_b, l0_lru_wa, l0_lru_ba, l0_lru_wx, l0_lru_bx, l0_lru_lam, l0_gla_wa2, l0_gla_ba2, l0_gla_norm_g, l0_w_out,
               l1_w_up, l1_conv_w, l1_conv_b, l1_wq, l1_wk, l1_wv, l1_w_ig, l1_b_ig, l1_w_fg, l1_b_fg, l1_skip, l1_norm_g, l1_w_down,
               moe_w_rg, moe_b_rg, moe_w_re, moe_b_re, moe_w_gate, moe_w_up, moe_w_down)
    bp = x_prompt.shape[0]

    def zero_state(s):
        return jnp.zeros((s.shape[0], bp) + s.shape[2:], s.dtype)

    (y_prompt, p_lru_conv, p_lru_h, p_gla_S, p_m_conv, p_m_C, p_m_n, p_m_m) = trunk(
        x_prompt, zero_state(state_lru_conv), zero_state(state_lru_h), zero_state(state_gla_S), zero_state(state_mlstm_conv),
        zero_state(state_mlstm_C), zero_state(state_mlstm_n), zero_state(state_mlstm_m), *weights)
    (y_sample, s_lru_conv, s_lru_h, s_gla_S, s_m_conv, s_m_C, s_m_n, s_m_m) = trunk(
        x_sample, state_lru_conv, state_lru_h, state_gla_S, state_mlstm_conv, state_mlstm_C, state_mlstm_n, state_mlstm_m, *weights)
    return (y_prompt, y_sample, p_lru_conv, p_lru_h, p_gla_S, p_m_conv, p_m_C, p_m_n, p_m_m, s_lru_conv, s_lru_h, s_gla_S, s_m_conv, s_m_C, s_m_n, s_m_m)


_drawn_inputs = setup_inputs


def setup_inputs(seed=0):
    import zlib

    import numpy as np

    out = dict(_drawn_inputs(seed))
    spreads = {}
    factors = {'norm_final_g': 24.375,
     'l0_lru_ba': 22.797,
     'l0_lru_bx': 8.0,
     'l1_conv_b': 2.689,
     'l1_w_fg': 6.203,
     'l1_skip': 105.928,
     'l1_norm_g': 66.177,
     'moe_b_re': 2.999,
     'moe_b_rg': 3.979,
     'l0_gla_norm_g': 3.479}
    for name, (base, spread) in spreads.items():
        noise = np.random.default_rng([zlib.crc32(name.encode()), seed]).standard_normal(out[name].shape)
        drawn = base * np.exp(spread * noise) if base else spread * noise
        out[name] = __import__('jax').numpy.asarray(drawn.astype(out[name].dtype))
    for name, factor in factors.items():
        out[name] = (out[name] * factor).astype(out[name].dtype)
    return out
```

```python
from contextlib import ExitStack, contextmanager

import concourse.bass as bass
from concourse import mybir

ALU = mybir.AluOpType
ACT = mybir.ActivationFunctionType
AX_X = mybir.AxisListType.X
F32 = mybir.dt.float32
BF16 = mybir.dt.bfloat16

P = 128
D = 2048
T_P = 256
B = 8
T_S = 8
T = T_P + B * T_S
TILES = [(0, 128), (128, 128), (256, 64)]
EPS = 1e-6
CW = 4
DC = D // P
W_LRU = 1024
LC = W_LRU // P
H = 4
DK, DV = 128, 256
IN0 = 5136
IN0C = IN0 // P
RANK = 16
XA, GA, QA, KA, VA, GG, AL = 0, 8, 16, 20, 24, 32, 40
DI = 4096
QB = 4
IC = DI // P
DH = DI // H
HC = DH // P
NE, NG, EG = 16, 4, 4
FE = 256
GC = 32
NCH = T_P // GC
SLOT = 2048
NSLOT = 8
KPS = 4
TPB = 4
SPL = 3
ROWS72 = SPL * SPL * T_S
NEG = -1.0e30

PARAM_TILES = [
    [("norm_mix_g", 2 * DC), ("norm_ffn_g", 2 * DC), ("norm_final_g", DC)],
    [("l0_lru_conv_w", CW * LC), ("l0_lru_conv_b", LC), ("l0_lru_ba", LC), ("l0_lru_bx", LC), ("l0_lru_lam", LC),
     ("l0_gla_ba2", H), ("l0_gla_norm_g", 8)],
    [("state_lru_h", B * LC)],
    [("l1_conv_w", CW * IC)],
    [("l1_conv_b", IC), ("l1_skip", IC), ("l1_norm_g", IC)],
]
PCOL = {}
for _i, _tile in enumerate(PARAM_TILES):
    _at = 0
    for _n, _k in _tile:
        PCOL[_n] = _i * P + _at
        _at += _k


class Signals:

    MOST = 30

    def __init__(self, nc, count=120):
        self.nc = nc
        self.sems = [nc.alloc_semaphore(f"signal{i}") for i in range(count)]
        self.next = 0
        self.held = 0

    def take(self):
        if not self.held and self.next > len(self.sems) - self.MOST:
            numbers = [s.num for s in self.sems]
            with self.nc.Block() as block:
                @block.gpsimd
                def _(pool):
                    pool.sem_clear(range(min(numbers), max(numbers) + 1))
            self.next = 0
        self.next += 1
        self.held += 1
        return self.sems[self.next - 1]


@contextmanager
def signal(m, name):
    yield m.signals.take()
    m.signals.held -= 1


class Mem:

    def __init__(self, nc, ctx):
        self.signals = Signals(nc)

        def sb(name, shape, dt=F32):
            return ctx.enter_context(nc.sbuf_tensor(name, shape, dt))

        self.x = sb("x_resid", [P, DC, T])
        self.xn = sb("x_norm", [P, DC * T])
        self.ring = sb("ring", [P, NSLOT * SLOT])
        self.arena = sb("arena", [P, 21600])
        self.ident = sb("ident", [P, P])
        self.identb = sb("identb", [P, P], BF16)
        self.ones = sb("ones", [P, P])
        self.causal = sb("causal", [P, P])
        self.causal32 = sb("causal32", [P, P])
        self.causal8 = sb("causal8", [64, 64])
        self.prm = sb("params", [P, len(PARAM_TILES) * P])
        self.neg = sb("negated", [P, 2 * LC])
        self.keep32 = sb("keep32", [P, T])
        self.small = sb("small", [P, 1088])
        self.rows = sb("gate_rows", [4, 7 * T])
        self.psum = ctx.enter_context(nc.psum_tensor("psum", [P, 8, 512], F32))
        self.XN = self.xn[:, :].rearrange("p (c t) -> p c t", t=T)


def view(buf, at, *shape):
    n = 1
    for s in shape:
        n *= s
    v = buf[:, at:at + n]
    if len(shape) == 1:
        return v
    names = "abcd"[:len(shape)]
    return v.rearrange(f"p ({' '.join(names)}) -> p {' '.join(names)}", **dict(zip(names[1:], shape[1:])))


def param(m, name, i=0):
    return m.prm[:, PCOL[name] + i:PCOL[name] + i + 1]


def setup(nc, m, I):
    x_tok = view(m.arena, 0, 3, D)
    prow = view(m.arena, 3 * D, len(PARAM_TILES), P)
    with signal(m, "rows_in") as rows_in, signal(m, "consts") as consts, signal(m, "turned") as turned, \
            signal(m, "copied") as copied, nc.Block() as block:
        @block.sync
        def _(sp):
            sp.dma_start(x_tok[:, 0:2, :], I["x_prompt"].rearrange("a (j p) d -> p (a j) d", p=P)).then_inc(rows_in, 16)
            sp.dma_start(x_tok[0:64, 2, :], I["x_sample"].rearrange("b t d -> (b t) d")).then_inc(rows_in, 16)
            for i, tile in enumerate(PARAM_TILES):
                at = 0
                for name, k in tile:
                    src = I[name]
                    letters = " ".join("abcd"[:len(src.shape)])
                    src = src.rearrange(f"{letters} -> ({letters})") if len(src.shape) > 1 else src
                    sp.dma_start(prow[at:at + k, i, :], src.rearrange("(k p) -> k p", p=P)).then_inc(rows_in, 16)
                    at += k

        @block.gpsimd
        def _(pool):
            pool.memset(m.ones[:, :], 1.0)
            pool.memset(m.causal32[:, :], 1.0)
            pool.drain()
            pool.affine_select(m.ident[:, :], m.ones[:, :], [[1, P]], ALU.is_equal, 0.0, base=0, channel_multiplier=-1)
            pool.affine_select(m.causal[:, :], m.ones[:, :], [[1, P]], ALU.is_ge, 0.0, base=0, channel_multiplier=-1)
            pool.drain()
            pool.affine_select(m.causal32[:, :].rearrange("p (a b) -> p a b", b=GC),
                               m.causal[:, :].rearrange("p (a b) -> p a b", b=GC),
                               [[-GC, P // GC], [0, GC]], ALU.is_ge, 0.0, base=0, channel_multiplier=1)
            pool.affine_select(m.causal8[:, :].rearrange("p (a b) -> p a b", b=T_S),
                               m.causal[0:64, 0:64].rearrange("p (a b) -> p a b", b=T_S),
                               [[-T_S, B], [0, T_S]], ALU.is_ge, 0.0, base=0, channel_multiplier=1)
            pool.memset(m.keep32[:, :], 1.0)
            pool.drain()
            pool.memset(m.keep32[:, 0:T_P:GC], 0.0)
            pool.memset(m.keep32[:, T_P:T:T_S], 0.0)
            pool.tensor_copy(m.identb[:, :], m.ident[:, :])
            pool.drain().then_inc(consts, 1)

        @block.tensor
        def _(pe):
            pe.wait_ge(consts, 1)
            pe.wait_ge(rows_in, 16 * (2 + sum(len(t) for t in PARAM_TILES)))
            for c in range(DC):
                if c >= 8:
                    pe.wait_ge(copied, c - 7)
                for j, (t0, n) in enumerate(TILES):
                    last = pe.transpose(m.psum[:, c % 8, t0:t0 + n], x_tok[0:n, j, c * P:(c + 1) * P],
                                        m.ident[0:n, 0:n])
                last.then_inc(turned, 1)
            for i, tile in enumerate(PARAM_TILES):
                k = sum(n for _, n in tile)
                pe.wait_ge(copied, DC - 8 + i + 1)
                pe.transpose(m.psum[:, i, 0:k], prow[0:k, i, :], m.ident[0:k, 0:k]).then_inc(turned, 1)

        @block.scalar
        def _(act):
            for c in range(DC):
                act.wait_ge(turned, c + 1)
                act.copy(m.x[:, c, :], m.psum[:, c % 8, 0:T]).then_inc(copied, 1)
            for i, tile in enumerate(PARAM_TILES):
                k = sum(n for _, n in tile)
                act.wait_ge(turned, DC + i + 1)
                act.copy(m.prm[:, i * P:i * P + k], m.psum[:, i, 0:k]).then_inc(copied, 1)


def rmsnorm(nc, m, gain, at, out):
    sq = view(m.ring, 0, 2, T)
    rstd = view(m.ring, 2 * T, T)
    with signal(m, "squared") as squared, signal(m, "summed") as summed, signal(m, "root") as root, \
            nc.Block() as block:
        @block.scalar
        def _(act):
            for c in range(DC):
                if c >= 2:
                    act.wait_ge(summed, c - 1)
                act.activation(sq[:, c % 2, :], m.x[:, c, :], ACT.Square).then_inc(squared, 1)
            act.wait_ge(root, 1)
            act.activation(rstd, rstd, ACT.Sqrt).then_inc(root, 1)

        @block.tensor
        def _(pe):
            for c in range(DC):
                pe.wait_ge(squared, c + 1)
                pe.matmul(m.psum[:, 0, 0:T], m.ones[:, :], sq[:, c % 2, :], start=(c == 0),
                          stop=(c == DC - 1)).then_inc(summed, 1)

        @block.vector
        def _(dve):
            dve.wait_ge(summed, DC)
            dve.tensor_scalar(rstd, m.psum[:, 0, 0:T], 1.0 / D, EPS, ALU.mult, ALU.add).then_inc(root, 1)
            dve.wait_ge(root, 2)
            dve.reciprocal(rstd, rstd)
            dve.drain()
            for c in range(DC):
                dve.scalar_tensor_tensor(out[:, c, :], m.x[:, c, :], param(m, gain, at + c), rstd,
                                         ALU.mult, ALU.mult)


def linear(nc, m, weights, kc, rhs, copy_to=None, gate=None):
    kg = kc // KPS
    cbs = NSLOT // kg
    width = TPB * P
    passes = weights.shape[1] // width // cbs
    w = weights.rearrange("(g k p) n -> p g k n", k=KPS, p=P)
    slots = view(m.ring, 0, NSLOT, KPS, 512)
    e = view(m.arena, 20480, 2, T)
    with ExitStack() as ctx:
        def signals(name, n):
            return [ctx.enter_context(signal(m, f"{name}{i}")) for i in range(n)]

        landed = signals("landed", NSLOT)
        used = signals("used", NSLOT)
        tile_done = signals("tile_done", cbs)
        by_act = signals("by_act", cbs)
        by_dve = signals("by_dve", cbs)
        block = ctx.enter_context(nc.Block())

        @block.sync
        def _(sp):
            def load(i, s):
                col = (i * cbs + s // kg) * width
                sp.dma_start(slots[:, s, :, :], w[:, s % kg, :, bass.ds(col, width)]).then_inc(landed[s], 16)

            for s in range(NSLOT):
                load(0, s)
            with sp.Fori(1, passes) as i:
                for s in range(NSLOT):
                    if s % kg < kg - 1:
                        sp.wait_ge(used[s], i)
                    else:
                        sp.wait_ge(tile_done[s // kg], i * TPB)
                    load(i, s)

        @block.tensor
        def _(pe):
            with pe.Fori(0, passes) as i:
                for s in range(NSLOT):
                    cb, g = s // kg, s % kg
                    pe.wait_ge(landed[s], i * 16 + 16)
                    if g == 0:
                        if copy_to is not None:
                            pe.wait_ge(by_act[cb], i * 2 + 2)
                        pe.wait_ge(by_dve[cb], i * TPB + TPB)
                    for k in range(KPS):
                        for t in range(TPB):
                            mm = pe.matmul(m.psum[:, cb * TPB + t, 0:T], slots[:, s, k, t * P:(t + 1) * P],
                                           rhs(g * KPS + k), start=(g == 0 and k == 0),
                                           stop=(g == kg - 1 and k == KPS - 1))
                            if g == kg - 1 and k == KPS - 1:
                                mm.then_inc(tile_done[cb], 1)
                    if g < kg - 1:
                        mm.then_inc(used[s], 1)

        @block.scalar
        def _(act):
            if copy_to is not None:
                for cb in range(cbs):
                    act.sem_inc(by_act[cb], 2)
                with act.Fori(0, passes) as i:
                    for cb in range(cbs):
                        for t in range(0, TPB, 2):
                            act.wait_ge(tile_done[cb], i * TPB + (t + 1))
                            act.copy(copy_to((i * cbs + cb) * TPB + t),
                                     m.psum[:, cb * TPB + t, 0:T]).then_inc(by_act[cb], 1)
            elif gate is not None:
                with act.Fori(0, passes) as i:
                    for cb in range(cbs):
                        for t in range(TPB):
                            act.wait_ge(tile_done[cb], i * TPB + (t + 1))
                            if t >= 2:
                                act.wait_ge(by_dve[cb], i * TPB + (TPB + t - 1))
                            elif cb:
                                act.wait_ge(by_dve[cb - 1], i * TPB + (TPB + t + 3))
                            else:
                                act.wait_ge(by_dve[cbs - 1], i * TPB + TPB)
                            act.activation(e[:, t % 2, :], m.psum[:, cb * TPB + t, 0:T], ACT.Silu).then_inc(by_act[cb], 1)

        @block.vector
        def _(dve):
            for cb in range(cbs):
                dve.sem_inc(by_dve[cb], TPB)
            with dve.Fori(0, passes) as i:
                for cb in range(cbs):
                    for t in range(TPB):
                        n = (i * cbs + cb) * TPB + t
                        ps = m.psum[:, cb * TPB + t, 0:T]
                        if copy_to is not None:
                            if t % 2:
                                dve.wait_ge(tile_done[cb], i * TPB + (t + 1))
                                dve.tensor_copy(copy_to(n), ps).then_inc(by_dve[cb], 2)
                        elif gate is not None:
                            dve.wait_ge(by_act[cb], i * TPB + (t + 1))
                            gate(dve, e[:, t % 2, :], n).then_inc(by_dve[cb], 1)
                        else:
                            dve.wait_ge(tile_done[cb], i * TPB + (t + 1))
                            x = m.x[:, bass.ds(n, 1), :].squeeze(1)
                            dve.tensor_tensor(x, x, ps, ALU.add).then_inc(by_dve[cb], 1)


def moe(nc, m, I, layer):
    xn = m.XN
    logit = view(m.small, 0, 3, 20)
    rank = view(m.small, 64, 4)
    bias = view(m.small, 72, 20)
    wr = view(m.ring, 0, DC, 20)
    tmp = [view(m.small, 96 + 16 * i, 3, 4) for i in range(10)]
    mx, s1 = view(m.small, 280, 3, 1), view(m.small, 284, 3, 1)
    m1, pg = view(m.small, 288, 3, 1), view(m.small, 292, 3, 1)
    prod = view(m.small, 300, 3, NG, EG)
    gates = view(m.small, 352, 3, NG, EG)
    gt16 = view(m.ring, 4096, T)
    gb = view(m.arena, 0, NE, T)
    hid = view(m.arena, NE * T, NE, 2, T)
    ex = view(m.arena, 3 * NE * T, 2, T)
    up = view(m.arena, 3 * NE * T + 2 * T, 2, T)
    with signal(m, "w_in") as w_in, signal(m, "init") as init, signal(m, "logits") as logits, \
            signal(m, "to_exp") as to_exp, signal(m, "expd") as expd, signal(m, "gated") as gated, \
            signal(m, "turned") as turned, signal(m, "gt_done") as gt_done, signal(m, "spread") as spread, \
            signal(m, "kept") as kept, nc.Block() as block:
        @block.sync
        def _(sp):
            sp.dma_start(wr[:, :, 0:NG], I["moe_w_rg"][layer].rearrange("(c p) g -> p c g", p=P)).then_inc(w_in, 16)
            sp.dma_start(wr[:, :, NG:20], I["moe_w_re"][layer].rearrange("(c p) g -> p c g", p=P)).then_inc(w_in, 16)
            sp.dma_start(bias[:, 0:NG], I["moe_b_rg"][layer].partition_broadcast(P)).then_inc(w_in, 16)
            sp.dma_start(bias[:, NG:20], I["moe_b_re"][layer].partition_broadcast(P)).then_inc(w_in, 16)

        @block.gpsimd
        def _(pool):
            for g in range(4):
                pool.memset(rank[:, g:g + 1], float(4 - g))
            pool.memset(logit[:, :, :], 0.0)
            pool.drain().then_inc(init, 1)

        @block.tensor
        def _(pe):
            pe.wait_ge(w_in, 64)
            for j, (t0, n) in enumerate(TILES):
                for c in range(DC):
                    mm = pe.matmul(m.psum[0:n, j, 0:20], xn[:, c, t0:t0 + n], wr[:, c, :], start=(c == 0),
                                   stop=(c == DC - 1))
            mm.then_inc(logits, 1)
            pe.wait_ge(gated, 1)
            for j, (t0, n) in enumerate(TILES):
                mm = pe.transpose(m.psum[0:NE, 3, t0:t0 + n], gates[0:n, j, :, :].rearrange("p g e -> p (g e)"),
                                  m.ident[0:n, 0:n])
            mm.then_inc(turned, 1)
            pe.wait_ge(gt_done, 1)
            for e in range(NE):
                if e >= 4:
                    pe.wait_ge(kept, e - 3)
                pe.matmul(m.psum[:, 4 + e % 4, 0:T], m.ident[0:NE, e:e + 1].to_broadcast([NE, P]), gt16[0:NE, :],
                          start=True, stop=True).then_inc(spread, 1)

        @block.scalar
        def _(act):
            act.wait_ge(to_exp, 1)
            act.activation(tmp[3], tmp[3], ACT.Exp).then_inc(expd, 1)
            act.wait_ge(to_exp, 2)
            act.activation(tmp[9], tmp[9], ACT.Exp).then_inc(expd, 1)
            for e in range(NE):
                act.wait_ge(spread, e + 1)
                act.copy(gb[:, e, :], m.psum[:, 4 + e % 4, 0:T]).then_inc(kept, 1)

        @block.vector
        def _(dve):
            bc = [P, 3, 4]
            rk = rank.unsqueeze(1).to_broadcast(bc)

            def first_largest(values, largest, ranked, onehot):
                dve.tensor_reduce(largest, values, AX_X, ALU.max)
                dve.drain()
                dve.tensor_tensor(ranked, values, largest.to_broadcast(bc), ALU.is_ge)
                dve.drain()
                dve.tensor_tensor(ranked, ranked, rk, ALU.mult)
                dve.drain()
                dve.tensor_reduce(s1, ranked, AX_X, ALU.max)
                dve.drain()
                dve.tensor_tensor(onehot, ranked, s1.to_broadcast(bc), ALU.is_equal)
                dve.drain()

            dve.wait_ge(init, 1)
            dve.wait_ge(logits, 1)
            for j, (t0, n) in enumerate(TILES):
                dve.tensor_tensor(logit[0:n, j, :], m.psum[0:n, j, 0:20], bias[0:n, :], ALU.add)
            dve.drain()
            lg = logit[:, :, 0:NG]
            first_largest(lg, mx, tmp[0], tmp[1])
            dve.tensor_tensor(tmp[3], lg, mx.to_broadcast(bc), ALU.subtract)
            dve.drain().then_inc(to_exp, 1)
            el4 = logit[:, :, NG:20].rearrange("p j (g e) -> p j g e", g=NG)
            for g in range(NG):
                dve.tensor_tensor(prod[:, :, g, :], el4[:, :, g, :], tmp[1][:, :, g:g + 1].to_broadcast(bc), ALU.mult)
            dve.drain()
            dve.tensor_tensor(tmp[4], prod[:, :, 0, :], prod[:, :, 1, :], ALU.add)
            dve.tensor_tensor(tmp[5], prod[:, :, 2, :], prod[:, :, 3, :], ALU.add)
            dve.drain()
            dve.tensor_tensor(tmp[4], tmp[4], tmp[5], ALU.add)
            dve.drain()
            first_largest(tmp[4], m1, tmp[0], tmp[6])
            dve.scalar_tensor_tensor(tmp[5], tmp[6], NEG, tmp[4], ALU.mult, ALU.add)
            dve.drain()
            first_largest(tmp[5], mx, tmp[0], tmp[7])
            dve.tensor_tensor(tmp[9], tmp[4], m1.to_broadcast(bc), ALU.subtract)
            dve.drain().then_inc(to_exp, 1)
            dve.tensor_tensor(tmp[7], tmp[7], tmp[6], ALU.add)
            dve.wait_ge(expd, 2)
            dve.drain()
            dve.tensor_tensor(tmp[8], tmp[9], tmp[7], ALU.mult)
            dve.tensor_reduce(pg, tmp[3], AX_X, ALU.add)
            dve.drain()
            dve.tensor_reduce(s1, tmp[8], AX_X, ALU.add)
            dve.drain()
            dve.tensor_tensor(s1, s1, pg, ALU.mult)
            dve.drain()
            dve.reciprocal(s1, s1)
            dve.drain()
            dve.tensor_tensor(tmp[8], tmp[8], s1.to_broadcast(bc), ALU.mult)
            dve.drain()
            for g in range(NG):
                dve.tensor_tensor(gates[:, :, g, :], tmp[8], tmp[1][:, :, g:g + 1].to_broadcast(bc), ALU.mult)
            dve.drain().then_inc(gated, 1)
            dve.wait_ge(turned, 1)
            dve.tensor_copy(gt16[0:NE, :], m.psum[0:NE, 3, 0:T]).then_inc(gt_done, 1)

    wg = I["moe_w_gate"][layer].rearrange("e (g k p) f -> e p g k f", k=KPS, p=P)
    wu = I["moe_w_up"][layer].rearrange("e (g k p) f -> e p g k f", k=KPS, p=P)
    wd = I["moe_w_down"][layer].rearrange("e (k p) n -> e p k n", p=P)
    slots = view(m.ring, 0, NSLOT, KPS, 512)
    down = view(m.ring, 4 * SLOT, 2, D)
    with ExitStack() as ctx:
        landed = [ctx.enter_context(signal(m, f"gate_up_landed{s}")) for s in range(4)]
        used = [ctx.enter_context(signal(m, f"gate_up_used{s}")) for s in range(3)]
        down_landed = ctx.enter_context(signal(m, "down_landed"))
        hidden_raw = ctx.enter_context(signal(m, "hidden_raw"))
        expd = ctx.enter_context(signal(m, "expd"))
        up_kept = ctx.enter_context(signal(m, "up_kept"))
        hidden = ctx.enter_context(signal(m, "hidden"))
        down_done = ctx.enter_context(signal(m, "down_done"))
        added = ctx.enter_context(signal(m, "added"))
        block = ctx.enter_context(nc.Block())

        @block.sync
        def _(sp):
            def load_gate_up(e):
                fixed = isinstance(e, int)
                for s in range(4):
                    if not (fixed and e == 0):
                        sp.wait_ge(used[s] if s < 3 else hidden_raw, e)
                    for at, w in ((0, wg), (FE, wu)):
                        src = w[e, :, s, :, :] if fixed else w[bass.ds(e, 1), :, s, :, :].squeeze(0)
                        sp.dma_start(slots[:, s, :, at:at + FE], src).then_inc(landed[s], 16)

            def load_down(e):
                fixed = isinstance(e, int)
                if not (fixed and e == 0):
                    sp.wait_ge(down_done, e * DC)
                sp.dma_start(down, wd[e] if fixed else wd[bass.ds(e, 1), :, :, :].squeeze(0)).then_inc(down_landed, 16)

            load_gate_up(0)
            load_down(0)
            load_gate_up(1)
            with sp.Fori(2, NE) as e:
                load_gate_up(e)
                load_down(e - 1)
            load_down(NE - 1)

        @block.tensor
        def _(pe):
            def gate_up(e):
                for s in range(4):
                    pe.wait_ge(landed[s], e * 32 + 32)
                    if s == 0 and not (isinstance(e, int) and e == 0):
                        pe.wait_ge(hidden, e * 2)
                    for k in range(KPS):
                        for t in range(TPB):
                            mm = pe.matmul(m.psum[:, t, 0:T], slots[:, s, k, t * P:(t + 1) * P], xn[:, s * KPS + k, :],
                                           start=(s == 0 and k == 0), stop=(s == 3 and k == KPS - 1))
                    if s < 3:
                        mm.then_inc(used[s], 1)
                mm.then_inc(hidden_raw, 1)

            def project_down(e):
                pe.wait_ge(hidden, e * 2 + 2)
                pe.wait_ge(down_landed, e * 16 + 16)
                for n in range(DC):
                    if isinstance(e, int) and e == 0 and n < 4:
                        pass
                    else:
                        pe.wait_ge(added, e * DC + (n - 3))
                    for k in range(2):
                        rhs = hid[:, e, k, :] if isinstance(e, int) else hid[:, bass.ds(e, 1), k, :].squeeze(1)
                        mm = pe.matmul(m.psum[:, 4 + n % 4, 0:T], down[:, k, n * P:(n + 1) * P], rhs, start=(k == 0),
                                       stop=(k == 1))
                    mm.then_inc(down_done, 1)

            gate_up(0)
            gate_up(1)
            project_down(0)
            with pe.Fori(2, NE) as e:
                gate_up(e)
                project_down(e - 1)
            project_down(NE - 1)

        @block.scalar
        def _(act):
            act.wait_ge(hidden_raw, 1)
            for f in range(2):
                act.activation(ex[:, f, :], m.psum[:, f, 0:T], ACT.Silu).then_inc(expd, 1)
            with act.Fori(1, NE) as e:
                act.wait_ge(hidden_raw, e + 1)
                act.wait_ge(hidden, e * 2)
                for f in range(2):
                    act.activation(ex[:, f, :], m.psum[:, f, 0:T], ACT.Silu).then_inc(expd, 1)

        @block.vector
        def _(dve):
            def hidden_values(e):
                dve.wait_ge(hidden_raw, e + 1)
                g = gb[:, e, :] if isinstance(e, int) else gb[:, bass.ds(e, 1), :].squeeze(1)
                for f in range(2):
                    dve.tensor_tensor(up[:, f, :], m.psum[:, 2 + f, 0:T], g, ALU.mult)
                dve.drain()
                for f in range(2):
                    dve.wait_ge(expd, e * 2 + (f + 1))
                    h = hid[:, e, f, :] if isinstance(e, int) else hid[:, bass.ds(e, 1), f, :].squeeze(1)
                    dve.tensor_tensor(h, up[:, f, :], ex[:, f, :], ALU.mult).then_inc(hidden, 1)

            def add_down(e):
                for n in range(DC):
                    dve.wait_ge(down_done, e * DC + (n + 1))
                    dve.tensor_tensor(m.x[:, n, :], m.x[:, n, :], m.psum[:, 4 + n % 4, 0:T], ALU.add).then_inc(added, 1)

            hidden_values(0)
            hidden_values(1)
            add_down(0)
            with dve.Fori(2, NE) as e:
                hidden_values(e)
                add_down(e - 1)
            add_down(NE - 1)


def store_columns(nc, m, columns, n, dram_rows):
    stage = view(m.xn, 0, 8, P)
    tiles = [(i, min(P, n - i)) for i in range(0, n, P)]
    with signal(m, "turned") as turned, signal(m, "copied") as copied, signal(m, "stored") as stored, \
            nc.Block() as block:
        @block.tensor
        def _(pe):
            for i, (a, k) in enumerate(tiles):
                pe.transpose(m.psum[0:k, i, 0:P], columns[:, a:a + k], m.ident[:, :]).then_inc(turned, 1)

        @block.scalar
        def _(act):
            for i, (a, k) in enumerate(tiles):
                act.wait_ge(turned, i + 1)
                act.copy(stage[0:k, i, :], m.psum[0:k, i, 0:P]).then_inc(copied, 1)

        @block.sync
        def _(sp):
            stores = 0
            for i, (a, k) in enumerate(tiles):
                sp.wait_ge(copied, i + 1)
                for lo, hi, rows in dram_rows:
                    f, t = max(lo, a), min(hi, a + k)
                    if f < t:
                        sp.dma_start(rows[f - lo:t - lo, :], stage[f - a:t - a, i, :]).then_inc(stored, 16)
                        stores += 1
            sp.wait_ge(stored, 16 * stores)


def convolve(nc, m, xin, xout, pad, rows, state, chunks, w_name, b_name, cols, ctx_name):
    with signal(m, "state_in") as state_in, signal(m, "turned") as turned, signal(m, "copied") as copied, \
            nc.Block() as block:
        @block.sync
        def _(sp):
            sp.dma_start(rows[0:24, :], state.rearrange("a b r d -> (a b r) d")).then_inc(state_in, 16)

        @block.tensor
        def _(pe):
            pe.wait_ge(state_in, 16)
            for c in range(chunks):
                if c >= 8:
                    pe.wait_ge(copied, c - 7)
                pe.transpose(m.psum[:, c % 8, 0:24], rows[0:24, c * P:(c + 1) * P], m.ident[0:24, 0:24]).then_inc(turned, 1)

        @block.vector
        def _(dve):
            for c in range(chunks):
                dve.tensor_copy(pad[:, c, :, 3:11], xin[:, c, T_P:T].rearrange("p (b t) -> p b t", b=B))
            dve.tensor_copy(cols[:, 0:3 * chunks].rearrange("p (r c) -> p c r", r=3), xin[:, :, T_P - 3:T_P])
            dve.drain()
            for c in range(chunks):
                dve.wait_ge(turned, c + 1)
                dve.tensor_copy(pad[:, c, :, 0:3],
                                m.psum[:, c % 8, 0:24].rearrange("p (b r) -> p b r", b=B)).then_inc(copied, 1)
            for b in range(B):
                at = 3 * chunks + b * 3 * chunks
                dve.tensor_copy(cols[:, at:at + 3 * chunks].rearrange("p (r c) -> p c r", r=3), pad[:, :, b, 8:11])
            dve.drain()
            for j in reversed(range(CW)):
                d = CW - 1 - j
                with dve.Fori(0, chunks) as c:
                    def at(v):
                        return v[:, bass.ds(c, 1)].squeeze(1)
                    w = m.prm[:, bass.ds(c + (PCOL[w_name] + j * chunks), 1)]
                    s_out = at(xout[:, :, T_P:T]).rearrange("p (b t) -> p b t", b=B)
                    if d == 0:
                        bias = m.prm[:, bass.ds(c + PCOL[b_name], 1)]
                        dve.tensor_scalar(at(xout[:, :, 0:T_P]), at(xin[:, :, 0:T_P]), w, bias, ALU.mult, ALU.add)
                        dve.tensor_scalar(s_out, at(pad[:, :, :, 3:11]), w, bias, ALU.mult, ALU.add)
                    else:
                        dve.scalar_tensor_tensor(at(xout[:, :, d:T_P]), at(xin[:, :, 0:T_P - d]), w,
                                                 at(xout[:, :, d:T_P]), ALU.mult, ALU.add)
                        dve.scalar_tensor_tensor(s_out, at(pad[:, :, :, j:j + 8]), w, s_out, ALU.mult, ALU.add)
                dve.drain()


def rg_lru(nc, m, I, O):
    proj = view(m.arena, 0, IN0C + 1, T)
    pad = view(m.arena, 13120, LC, B, 11)
    wa = view(m.arena, 14000, LC, P)
    wx = view(m.arena, 15100, LC, P)
    rows = view(m.arena, 16200, W_LRU)
    cols = view(m.arena, 17300, 27 * LC)
    xc, r, g, a, b, h = (view(m.ring, 2560 * i, LC, T) for i in range(6))
    convolve(nc, m, proj[:, XA:XA + LC], xc, pad, rows, I["state_lru_conv"], LC, "l0_lru_conv_w", "l0_lru_conv_b", cols, "l0")
    store_columns(nc, m, cols, 27 * LC, [
        (0, 3 * LC, O["p_lru_conv"].rearrange("a b r (c p) -> (a b r c) p", p=P)),
        (3 * LC, 27 * LC, O["s_lru_conv"].rearrange("a b r (c p) -> (a b r c) p", p=P))])
    c8 = m.neg[:, 0:LC]
    tl = m.neg[:, LC:2 * LC]
    lam = m.prm[:, PCOL["l0_lru_lam"]:PCOL["l0_lru_lam"] + LC]
    h0 = m.prm[:, PCOL["state_lru_h"]:PCOL["state_lru_h"] + B * LC].rearrange("p (b c) -> p c b", b=B)
    hl = view(m.small, 0, 9 * LC)
    add0 = view(m.small, 96, LC, B)
    with signal(m, "blank") as blank, signal(m, "w_in") as w_in, signal(m, "negs") as negs, \
            signal(m, "prod") as prod, signal(m, "expd") as expd, signal(m, "sig") as sig, \
            signal(m, "pwr") as pwr, signal(m, "om") as om, signal(m, "ge") as ge, nc.Block() as block:
        @block.gpsimd
        def _(pool):
            pool.memset(wa, 0.0)
            pool.memset(wx, 0.0)
            pool.drain().then_inc(blank, 1)

        @block.sync
        def _(sp):
            sp.wait_ge(blank, 1)
            for w, name in ((wa, "l0_lru_wa"), (wx, "l0_lru_wx")):
                src = I[name].rearrange("a (c two) i o -> two i (a c) o", two=2)
                sp.dma_start(w[0:64, :, 0:64], src[0]).then_inc(w_in, 16)
                sp.dma_start(w[64:128, :, 64:128], src[1]).then_inc(w_in, 16)

        @block.tensor
        def _(pe):
            pe.wait_ge(w_in, 64)
            for q, w in enumerate((wa, wx)):
                for c in range(LC):
                    if q:
                        pe.wait_ge(expd, 2 + c + 1)
                    pe.matmul(m.psum[:, c, 0:T], w[:, c, :], xc[:, c, :], start=True, stop=True).then_inc(prod, 1)

        @block.scalar
        def _(act):
            act.wait_ge(negs, 1)
            act.activation(tl, tl, ACT.Exp, scale=-1.0).then_inc(expd, 1)
            act.drain()
            act.activation(tl, tl, ACT.Ln, bias=1.0).then_inc(expd, 1)
            for q, dst in enumerate((r, g)):
                for c in range(LC):
                    act.wait_ge(prod, q * LC + c + 1)
                    act.activation(dst[:, c, :], m.psum[:, c, 0:T], ACT.Sigmoid,
                                   bias=param(m, ("l0_lru_ba", "l0_lru_bx")[q], c)).then_inc(expd, 1)
            act.wait_ge(sig, 1)
            for c in range(LC):
                act.activation(a[:, c, :], r[:, c, :], ACT.Exp, scale=c8[:, c:c + 1]).then_inc(pwr, 1)
            for c in range(LC):
                act.activation(b[:, c, :], r[:, c, :], ACT.Tanh, scale=c8[:, c:c + 1]).then_inc(pwr, 1)
            act.drain()
            act.activation(r, proj[:, GA:GA + LC], ACT.Gelu_apprx_tanh).then_inc(ge, 1)
            act.wait_ge(om, 1)
            act.activation(b, b, ACT.Sqrt, scale=-1.0).then_inc(om, 1)

        @block.vector
        def _(dve):
            dve.scalar_tensor_tensor(tl, lam, -1.0, lam, ALU.mult, ALU.max)
            dve.drain().then_inc(negs, 1)
            dve.wait_ge(expd, 2)
            dve.tensor_scalar(c8, lam, -1.0, 0.0, ALU.mult, ALU.max)
            dve.drain()
            dve.tensor_tensor(c8, c8, tl, ALU.add)
            dve.drain()
            dve.tensor_scalar(c8, c8, -8.0, None, ALU.mult)
            dve.wait_ge(expd, 2 + 2 * LC)
            dve.drain().then_inc(sig, 1)
            dve.tensor_tensor(g, g, xc, ALU.mult)
            dve.wait_ge(pwr, LC)
            dve.tensor_tensor(h, a, a, ALU.mult)
            dve.drain()
            dve.wait_ge(pwr, 2 * LC)
            dve.scalar_tensor_tensor(b, h, 1.0, b, ALU.add, ALU.mult)
            dve.drain().then_inc(om, 1)
            dve.wait_ge(om, 2)
            dve.tensor_tensor(b, b, g, ALU.mult)
            dve.tensor_tensor(add0, a[:, :, T_P:T:T_S], h0, ALU.mult)
            dve.drain()
            dve.tensor_tensor(b[:, :, T_P:T:T_S], b[:, :, T_P:T:T_S], add0, ALU.add)
            dve.memset(a[:, :, T_P:T:T_S], 0.0)
            dve.memset(a[:, :, 0:1], 0.0)
            dve.drain()
            flat = "p c t -> p (c t)"
            dve.tensor_tensor_scan(h.rearrange(flat), a.rearrange(flat), b.rearrange(flat), 0.0, ALU.mult, ALU.add)
            dve.wait_ge(ge, 1)
            dve.drain()
            dve.tensor_copy(hl[:, 0:LC], h[:, :, T_P - 1:T_P].squeeze(2))
            dve.tensor_copy(hl[:, LC:9 * LC].rearrange("p (b c) -> p c b", b=B), h[:, :, T_P + T_S - 1:T:T_S])
            dve.drain()
            dve.tensor_tensor(proj[:, GA:GA + LC], h, r, ALU.mult)
    store_columns(nc, m, hl, 9 * LC, [(0, LC, O["p_lru_h"].rearrange("a b (c p) -> (a b c) p", p=P)),
                                      (LC, 9 * LC, O["s_lru_h"].rearrange("a b (c p) -> (a b c) p", p=P))])


def gla(nc, m, I, O):
    proj = view(m.arena, 0, IN0C + 1, T)
    bc, t1, qe, ke, qi, kh, ab = (view(m.ring, 1280 * i, H, T) for i in range(7))
    vt = view(m.ring, 8960, 3, H, DV)
    kt = view(m.ring, 12032, 3, H, DK)
    att = view(m.ring, 13568, H, 3, P)
    sp_ = view(m.ring, 15104, H, DV)
    ebl = view(m.small, 0, H, 16)
    wa2 = view(m.small, 64, 512)
    ss = view(m.arena, 13200, B, H, DV)
    km = view(m.arena, 0, 2, B, DK)
    osb = proj[:, QA:QA + 8]

    def cut(v, w):
        return (v[:, :, 0:T_P].rearrange("p h (c l) -> p h c l", l=GC) if w == 0 else
                v[:, :, T_P:T].rearrange("p h (c l) -> p h c l", l=T_S))

    with signal(m, "w_in") as w_in, signal(m, "prod") as prod, signal(m, "zd") as zd, \
            signal(m, "lnd") as lnd, signal(m, "dd") as dd, signal(m, "ee") as ee, nc.Block() as block:
        @block.sync
        def _(sp):
            sp.dma_start(wa2[0:RANK, :], I["l0_gla_wa2"].rearrange("a r n -> (a r) n")).then_inc(w_in, 16)
            sp.wait_ge(w_in, 16)

        @block.tensor
        def _(pe):
            pe.wait_ge(w_in, 16)
            for h in range(H):
                pe.matmul(m.psum[:, h, 0:T], wa2[0:RANK, h * DK:(h + 1) * DK], proj[0:RANK, AL, :], start=True,
                          stop=True).then_inc(prod, 1)

        @block.scalar
        def _(act):
            act.wait_ge(zd, 1)
            act.activation(ab, ab, ACT.Exp, scale=-1.0)
            act.drain()
            act.activation(ab, ab, ACT.Ln, bias=1.0).then_inc(lnd, 1)
            act.wait_ge(dd, 1)
            act.activation(qe, t1, ACT.Exp)
            act.activation(ke, t1, ACT.Exp, scale=-1.0)
            act.activation(qi, bc, ACT.Exp).then_inc(ee, 1)
            act.wait_ge(dd, 2)
            act.activation(kh, t1, ACT.Exp)
            act.activation(ebl, ebl, ACT.Exp).then_inc(ee, 1)

        @block.vector
        def _(dve):
            for h in range(H):
                dve.wait_ge(prod, h + 1)
                dve.tensor_scalar(t1[:, h, :], m.psum[:, h, 0:T], param(m, "l0_gla_ba2", h), None, ALU.add)
            dve.drain()
            dve.scalar_tensor_tensor(ab, t1, -1.0, t1, ALU.mult, ALU.max).then_inc(zd, 1)
            dve.wait_ge(lnd, 1)
            dve.scalar_tensor_tensor(t1, t1, 0.0, ab, ALU.min, ALU.subtract)
            dve.drain()
            dve.tensor_scalar(t1, t1, 1.0 / 16.0, None, ALU.mult)
            dve.drain()
            for h in range(H):
                dve.tensor_tensor_scan(bc[:, h, :], m.keep32[:, :], t1[:, h, :], 0.0, ALU.mult, ALU.add)
            dve.drain()
            for w, (l, ref) in enumerate(((GC, GC // 2 - 1), (T_S, T_S // 2 - 1))):
                b4 = cut(bc, w)
                dve.tensor_tensor(cut(t1, w), b4, b4[:, :, :, ref:ref + 1].to_broadcast([P, H, 8, l]), ALU.subtract)
                dve.tensor_copy(ebl[:, :, 8 * w:8 * w + 8], b4[:, :, :, l - 1:l].squeeze(3))
            dve.drain().then_inc(dd, 1)
            dve.wait_ge(ee, 1)
            for w, l in ((0, GC), (1, T_S)):
                b4 = cut(bc, w)
                dve.tensor_tensor(cut(t1, w), b4[:, :, :, l - 1:l].to_broadcast([P, H, 8, l]), b4, ALU.subtract)
            dve.drain().then_inc(dd, 1)
            q, k = proj[:, QA:QA + H], proj[:, KA:KA + H]
            dve.scalar_tensor_tensor(qe, q, DK ** -0.5, qe, ALU.mult, ALU.mult)
            dve.scalar_tensor_tensor(qi, q, DK ** -0.5, qi, ALU.mult, ALU.mult)
            dve.tensor_tensor(ke, ke, k, ALU.mult)
            dve.wait_ge(ee, 2)
            dve.tensor_tensor(kh, kh, k, ALU.mult)
    with signal(m, "turned") as turned, signal(m, "st_in") as st_in, nc.Block() as block:
        @block.sync
        def _(sp):
            for b in range(B):
                sp.dma_start(ss[:, b, :, :], I["state_gla_S"][0, b].rearrange("h d e -> d h e")).then_inc(st_in, 16)
            sp.wait_ge(st_in, 16 * B)

        @block.tensor
        def _(pe):
            for j, (t0, n) in enumerate(TILES):
                for c in range(8):
                    mm = pe.transpose(m.psum[0:n, 2 * j + c // 4, (c % 4) * P:(c % 4 + 1) * P], proj[:, VA + c, t0:t0 + n],
                                      m.ident[:, :])
                mm.then_inc(turned, 1)
            for j, (t0, n) in enumerate(TILES[0:2]):
                for h in range(H):
                    mm = pe.transpose(m.psum[0:n, 6 + j, h * P:(h + 1) * P], kh[:, h, t0:t0 + n], m.ident[:, :])
                mm.then_inc(turned, 1)

        @block.vector
        def _(dve):
            for j, (t0, n) in enumerate(TILES):
                dve.wait_ge(turned, j + 1)
                dve.tensor_copy(vt[0:n, j].rearrange("p h e -> p (h e)"),
                                m.psum[0:n, 2 * j:2 * j + 2, :].rearrange("p a b -> p (a b)"))
            for j, (t0, n) in enumerate(TILES[0:2]):
                dve.wait_ge(turned, 4 + j)
                dve.tensor_copy(kt[0:n, j].rearrange("p h e -> p (h e)"), m.psum[0:n, 6 + j, :])
    with signal(m, "turned") as turned, signal(m, "scored") as scored, nc.Block() as block:
        @block.tensor
        def _(pe):
            t0, n = TILES[2]
            for h in range(H):
                mm = pe.transpose(m.psum[0:n, 4, h * P:(h + 1) * P], kh[:, h, t0:t0 + n], m.ident[:, :])
            mm.then_inc(turned, 1)
            for h in range(H):
                for j, (t0, n) in enumerate(TILES):
                    mm = pe.matmul(m.psum[0:n, h, j * P:j * P + n], ke[:, h, t0:t0 + n], qe[:, h, t0:t0 + n], start=True,
                                   stop=True)
                mm.then_inc(scored, 1)

        @block.vector
        def _(dve):
            dve.wait_ge(turned, 1)
            dve.tensor_copy(kt[0:64, 2].rearrange("p h e -> p (h e)"), m.psum[0:64, 4, :])
            for h in range(H):
                dve.wait_ge(scored, h + 1)
                for j, (t0, n) in enumerate(TILES):
                    mask = m.causal8 if j == 2 else m.causal32
                    dve.tensor_tensor(att[0:n, h, j, 0:n], m.psum[0:n, h, j * P:j * P + n], mask[0:n, 0:n], ALU.mult)
    for pair in range(2):
        heads = (2 * pair, 2 * pair + 1)
        with signal(m, "masked") as masked, signal(m, "upd") as upd, signal(m, "new_s") as new_s, \
                signal(m, "supd") as supd, signal(m, "snew") as snew, signal(m, "o_done") as o_done, \
                nc.Block() as block:
            @block.gpsimd
            def _(pool):
                for i, h in enumerate(heads):
                    for b in range(B):
                        pool.affine_select(km[0:64, i, b, :], kt[0:64, 2, h, :], [[0, DK]], ALU.is_ge, 0.0,
                                           base=-T_S * b, channel_multiplier=1)
                pool.drain()
                for i, h in enumerate(heads):
                    for b in range(B):
                        pool.affine_select(km[0:64, i, b, :], km[0:64, i, b, :], [[0, DK]], ALU.is_ge, 0.0,
                                           base=T_S * b + T_S - 1, channel_multiplier=-1)
                pool.drain().then_inc(masked, 1)

            @block.tensor
            def _(pe):
                def o(i, e):
                    return m.psum[:, 2 * i + e]
                for i, h in enumerate(heads):
                    for e in range(2):
                        for j, (t0, n) in enumerate(TILES):
                            pe.matmul(o(i, e)[:, t0:t0 + n], vt[0:n, j, h, e * P:(e + 1) * P], att[0:n, h, j, 0:n],
                                      start=(j == 0), stop=False, skip_group_check=True)
                pe.wait_ge(masked, 1)
                for c in range(NCH):
                    j, r0 = c // 4, (c % 4) * GC
                    for i, h in enumerate(heads):
                        if c:
                            pe.wait_ge(new_s, 2 * (c - 1) + i + 1)
                            for e in range(2):
                                pe.matmul(o(i, e)[:, c * GC:(c + 1) * GC], sp_[:, h, e * P:(e + 1) * P],
                                          qi[:, h, c * GC:(c + 1) * GC], start=False, stop=False, skip_group_check=True)
                        pe.matmul(m.psum[:, 4 + i, 0:DV], kt[r0:r0 + GC, j, h, :], vt[r0:r0 + GC, j, h, :], start=True,
                                  stop=True, tile_position=(r0, 0)).then_inc(upd, 1)
                    b = c
                    for i, h in enumerate(heads):
                        for e in range(2):
                            pe.matmul(o(i, e)[:, T_P + b * T_S:T_P + (b + 1) * T_S], ss[:, b, h, e * P:(e + 1) * P],
                                      qi[:, h, T_P + b * T_S:T_P + (b + 1) * T_S], start=False, stop=False,
                                      skip_group_check=True)
                        if b:
                            pe.wait_ge(snew, 2 * (b - 1) + i + 1)
                        pe.matmul(m.psum[:, 6 + i, 0:DV], km[0:64, i, b, :], vt[0:64, 2, h, :], start=True,
                                  stop=True).then_inc(supd, 1)
                pe.drain().then_inc(o_done, 1)

            @block.vector
            def _(dve):
                for c in range(NCH):
                    for i, h in enumerate(heads):
                        dve.wait_ge(upd, 2 * c + i + 1)
                        if c == 0:
                            dve.tensor_copy(sp_[:, h, :], m.psum[:, 4 + i, 0:DV]).then_inc(new_s, 1)
                        else:
                            dve.scalar_tensor_tensor(sp_[:, h, :], sp_[:, h, :], ebl[:, h, c:c + 1], m.psum[:, 4 + i, 0:DV],
                                                     ALU.mult, ALU.add).then_inc(new_s, 1)
                    b = c
                    for i, h in enumerate(heads):
                        dve.wait_ge(supd, 2 * b + i + 1)
                        dve.scalar_tensor_tensor(ss[:, b, h, :], ss[:, b, h, :], ebl[:, h, 8 + b:9 + b],
                                                 m.psum[:, 6 + i, 0:DV], ALU.mult, ALU.add).then_inc(snew, 1)
                    dve.drain()
                dve.wait_ge(o_done, 1)
                for i, h in enumerate(heads):
                    for e in range(2):
                        dve.tensor_copy(osb[:, 2 * h + e, :], m.psum[:, 2 * i + e, 0:T])
    sq = view(m.ring, 0, 8, T)
    rs = view(m.ring, 2560, H, T)
    sg = view(m.ring, 5120, 8, T)
    with signal(m, "sqd") as sqd, signal(m, "summed") as summed, signal(m, "root") as root, \
            signal(m, "expd") as expd, signal(m, "stored") as stored, nc.Block() as block:
        @block.sync
        def _(sp):
            for b in range(B):
                sp.dma_start(O["s_gla_S"][0, b].rearrange("h d e -> d h e"), ss[:, b, :, :]).then_inc(stored, 16)
            sp.dma_start(O["p_gla_S"][0, 0].rearrange("h d e -> d h e"), sp_).then_inc(stored, 16)
            sp.wait_ge(stored, 16 * (B + 1))

        @block.scalar
        def _(act):
            act.activation(sq, osb, ACT.Square).then_inc(sqd, 1)
            act.activation(sg, proj[:, GG:GG + 8], ACT.Silu).then_inc(expd, 1)
            act.wait_ge(root, 1)
            act.activation(rs, rs, ACT.Sqrt).then_inc(root, 1)

        @block.tensor
        def _(pe):
            pe.wait_ge(sqd, 1)
            for h in range(H):
                for e in range(2):
                    mm = pe.matmul(m.psum[:, h, 0:T], m.ones[:, :], sq[:, 2 * h + e, :], start=(e == 0), stop=(e == 1))
                mm.then_inc(summed, 1)

        @block.vector
        def _(dve):
            for h in range(H):
                dve.wait_ge(summed, h + 1)
                dve.tensor_scalar(rs[:, h, :], m.psum[:, h, 0:T], 1.0 / DV, EPS, ALU.mult, ALU.add)
            dve.drain().then_inc(root, 1)
            dve.wait_ge(root, 2)
            dve.reciprocal(rs, rs)
            dve.drain()
            for c in range(8):
                dve.scalar_tensor_tensor(osb[:, c, :], osb[:, c, :], param(m, "l0_gla_norm_g", c), rs[:, c // 2, :],
                                         ALU.mult, ALU.mult)
            dve.wait_ge(expd, 1)
            dve.drain()
            dve.tensor_tensor(proj[:, GG:GG + 8], osb, sg, ALU.mult)


def first_projection(nc, m, I):
    proj = view(m.arena, 0, IN0C + 1, T)
    w_in = I["l0_w_in"][0]

    linear(nc, m, w_in[:, 0:IN0C * P], DC, lambda k: m.XN[:, k, :],
           copy_to=lambda n: proj[:, bass.ds(n, 1), :].squeeze(1))
    wt = view(m.ring, 0, DC, RANK)
    with signal(m, "tail_in") as tail_in, signal(m, "tail") as tail, nc.Block() as block:
        @block.sync
        def _(sp):
            sp.dma_start(wt, w_in[:, IN0C * P:IN0].rearrange("(k p) n -> p k n", p=P)).then_inc(tail_in, 16)

        @block.tensor
        def _(pe):
            pe.wait_ge(tail_in, 16)
            for k in range(DC):
                mm = pe.matmul(m.psum[0:RANK, 0, 0:T], wt[:, k, :], m.XN[:, k, :], start=(k == 0), stop=(k == DC - 1))
            mm.then_inc(tail, 1)

        @block.scalar
        def _(act):
            act.wait_ge(tail, 1)
            act.copy(proj[0:RANK, AL, :], m.psum[0:RANK, 0, 0:T])


def final_norm(nc, m, O):
    y = view(m.arena, 0, DC, T)
    rmsnorm(nc, m, "norm_final_g", 0, y)
    y_tok = view(m.arena, DC * T, 3, D)
    with signal(m, "turned") as turned, signal(m, "copied") as copied, signal(m, "stored") as stored, \
            nc.Block() as block:
        @block.tensor
        def _(pe):
            q = 0
            for j, (t0, n) in enumerate(TILES):
                for g in range(4):
                    if q >= 8:
                        pe.wait_ge(copied, q - 7)
                    for c in range(4):
                        mm = pe.transpose(m.psum[0:n, q % 8, c * P:(c + 1) * P], y[:, 4 * g + c, t0:t0 + n], m.ident[:, :])
                    mm.then_inc(turned, 1)
                    q += 1

        @block.scalar
        def _(act):
            q = 0
            for j, (t0, n) in enumerate(TILES):
                for g in range(4):
                    act.wait_ge(turned, q + 1)
                    act.copy(y_tok[0:n, j, g * 512:(g + 1) * 512], m.psum[0:n, q % 8, :]).then_inc(copied, 1)
                    q += 1

        @block.sync
        def _(sp):
            outs = [O["y_prompt"][0, 0:P, :], O["y_prompt"][0, P:T_P, :], O["y_sample"].rearrange("b t d -> (b t) d")]
            for j, (t0, n) in enumerate(TILES):
                sp.wait_ge(copied, 4 * (j + 1))
                sp.dma_start(outs[j], y_tok[0:n, j, :]).then_inc(stored, 16)
            sp.wait_ge(stored, 48)


def mlstm(nc, m, I, O):
    xm = view(m.arena, 0, IC, T)
    xc = view(m.arena, IC * T, IC, T)
    linear(nc, m, I["l1_w_up"][0][:, 0:DI], DC, lambda k: m.XN[:, k, :],
           copy_to=lambda n: xm[:, bass.ds(n, 1), :].squeeze(1))
    pad = view(m.ring, 0, IC, B, 11)
    state_rows = view(m.ring, 2816, DI)
    cols = view(m.ring, 7000, 27 * IC)
    convolve(nc, m, xm, xc, pad, state_rows, I["state_mlstm_conv"], IC, "l1_conv_w", "l1_conv_b", cols, "l1")
    store_columns(nc, m, cols, 27 * IC, [
        (0, 3 * IC, O["p_m_conv"].rearrange("a b r (c p) -> (a b r c) p", p=P)),
        (3 * IC, 27 * IC, O["s_m_conv"].rearrange("a b r (c p) -> (a b r c) p", p=P))])

    wq, wk, wv = (view(m.small, IC * QB * i, IC, QB) for i in range(3))
    with signal(m, "w_in") as w_in, nc.Block() as block:
        @block.sync
        def _(sp):
            for w, name in ((wq, "l1_wq"), (wk, "l1_wk"), (wv, "l1_wv")):
                sp.dma_start(w, I[name][0].rearrange("(c b) i o -> (b i) c o", c=IC)).then_inc(w_in, 16)
            sp.wait_ge(w_in, 48)

        @block.scalar
        def _(act):
            for q in range(4):
                x = xc[:, q * HC:(q + 1) * HC, :]
                act.activation(x, x, ACT.Silu)

    q_f = view(m.ring, 0, HC, T)
    k_f = view(m.ring, 2560, HC, T)
    bd = view(m.ring, 5120, 3, HC, P)
    blk = view(m.small, 384, 32)
    wg = view(m.ring, 8192, 3, IC, 8)
    bg, bgf = view(m.small, 416, 1), view(m.small, 417, 1)
    gate_tok = view(m.small, 420, 3, 8)
    u_col = view(m.small, 448, 3, H)

    def expand(dve, h, which):
        for i, w in enumerate((wq, wk, wv)[:which]):
            for c in range(HC):
                dve.tensor_tensor(bd[:, i, c, :].rearrange("p (b o) -> p b o", o=QB),
                                  w[:, h * HC + c, :].unsqueeze(1).to_broadcast([P, 32, QB]),
                                  blk.unsqueeze(2).to_broadcast([P, 32, QB]), ALU.mult)
        return dve.drain()

    with signal(m, "w_in") as w_in, signal(m, "blk_done") as blk_done, nc.Block() as block:
        @block.sync
        def _(sp):
            for i in range(3):
                for j, name in enumerate(("l1_w_ig", "l1_w_fg")):
                    src = I[name][0, i * DI:(i + 1) * DI, :].rearrange("(c p) g -> p c g", p=P)
                    sp.dma_start(wg[:, i, :, 4 * j:4 * j + 4], src).then_inc(w_in, 16)
            sp.dma_start(bg[0:4, :], I["l1_b_ig"].rearrange("a g -> g a")).then_inc(w_in, 16)
            sp.dma_start(bgf[0:4, :], I["l1_b_fg"].rearrange("a g -> g a")).then_inc(w_in, 16)
            sp.wait_ge(w_in, 8 * 16)

        @block.gpsimd
        def _(pool):
            pool.memset(blk, 1.0)
            pool.drain()
            pool.affine_select(blk, blk, [[-QB, 32]], ALU.is_ge, 0.0, base=0, channel_multiplier=1)
            pool.drain()
            pool.affine_select(blk, blk, [[QB, 32]], ALU.is_ge, 0.0, base=QB - 1, channel_multiplier=-1)

    for h in range(H):
        with signal(m, "expanded") as expanded, signal(m, "prod") as prod, signal(m, "kept") as kept, \
                signal(m, "v_kept") as v_kept, nc.Block() as block:
            @block.vector
            def _(dve):
                expand(dve, h, 3).then_inc(expanded, 1)
                for c in range(HC):
                    dve.wait_ge(prod, 3 * c + 3)
                    dve.tensor_copy(xm[:, h * HC + c, :], m.psum[:, 3 * (c % 2) + 2, 0:T]).then_inc(v_kept, 1)

            @block.scalar
            def _(act):
                for c in range(HC):
                    for i, dst in enumerate((q_f, k_f)):
                        act.wait_ge(prod, 3 * c + i + 1)
                        act.copy(dst[:, c, :], m.psum[:, 3 * (c % 2) + i, 0:T]).then_inc(kept, 1)

            @block.tensor
            def _(pe):
                pe.wait_ge(expanded, 1)
                for c in range(HC):
                    if c >= 2:
                        pe.wait_ge(kept, 2 * (c - 1))
                        pe.wait_ge(v_kept, c - 1)
                    for i, src in enumerate((xc, xc, xm)):
                        pe.matmul(m.psum[:, 3 * (c % 2) + i, 0:T], bd[:, i, c, :], src[:, h * HC + c, :], start=True,
                                  stop=True).then_inc(prod, 1)
        with signal(m, "gates_done") as gates_done, nc.Block() as block:
            @block.tensor
            def _(pe):
                for j, (t0, n) in enumerate(TILES):
                    for i in range(3):
                        for c in range(HC):
                            src = (q_f[:, c], k_f[:, c], xm[:, h * HC + c])[i]
                            mm = pe.matmul(m.psum[0:n, j, 0:8], src[:, t0:t0 + n], wg[:, i, h * HC + c, :],
                                           start=(i == 0 and c == 0), stop=(i == 2 and c == HC - 1))
                mm.then_inc(gates_done, 1)

            @block.vector
            def _(dve):
                dve.wait_ge(gates_done, 1)
                for j, (t0, n) in enumerate(TILES):
                    if h == 0:
                        dve.tensor_copy(gate_tok[0:n, j, :], m.psum[0:n, j, 0:8])
                    else:
                        dve.tensor_tensor(gate_tok[0:n, j, :], gate_tok[0:n, j, :], m.psum[0:n, j, 0:8], ALU.add)

    ig, lf, big, keep, cut, ws, wp = (m.rows[:, T * i:T * (i + 1)] for i in range(7))
    m0 = view(m.small, 464, B)
    wc_row = view(m.small, 472, B)
    ml = view(m.small, 480, 9)
    wcol = view(m.small, 496, H, B)

    def seqs(v):
        return v[:, T_P:T].rearrange("p (b t) -> p b t", b=B)

    with signal(m, "turned") as turned, signal(m, "e1") as e1, signal(m, "e2") as e2, \
            signal(m, "m_in") as m_in, signal(m, "m_out") as m_out, signal(m, "u_done") as u_done, \
            signal(m, "ends") as ends, signal(m, "m_done") as m_done, nc.Block() as block:
        @block.sync
        def _(sp):
            with nc.allow_non_contiguous_dma(reason="32 values"):
                sp.dma_start(m0[0:H, :], I["state_mlstm_m"][0].rearrange("b h -> h b")).then_inc(m_in, 16)
                sp.wait_ge(m_done, 1)
                sp.dma_start(O["p_m_m"].rearrange("a b h -> h (a b)"), ml[0:H, 0:1]).then_inc(m_out, 16)
                sp.dma_start(O["s_m_m"][0].rearrange("b h -> h b"), ml[0:H, 1:9]).then_inc(m_out, 16)
            sp.wait_ge(m_out, 32)

        @block.gpsimd
        def _(pool):
            pool.memset(keep, 1.0)
            pool.memset(cut, 0.0)
            pool.drain()
            for v, x in ((keep, 0.0), (cut, NEG)):
                pool.memset(v[:, 0:1], x)
                pool.memset(v[:, T_P:T:T_S], x)
            pool.drain().then_inc(ends, 1)

        @block.tensor
        def _(pe):
            for g in range(2):
                for j, (t0, n) in enumerate(TILES):
                    mm = pe.transpose(m.psum[0:4, g, t0:t0 + n], gate_tok[0:n, j, 4 * g:4 * g + 4], m.ident[0:n, 0:n])
                mm.then_inc(turned, 1)
            pe.wait_ge(u_done, 1)
            for j, (t0, n) in enumerate(TILES):
                mm = pe.transpose(m.psum[0:n, 2, 4 * j:4 * j + 4], ig[:, t0:t0 + n], m.ident[0:4, 0:4])
            mm.then_inc(turned, 1)
            pe.wait_ge(u_done, 2)
            for h in range(H):
                mm = pe.matmul(m.psum[:, 3, B * h:B * h + B], m.ident[0:H, h:h + 1].to_broadcast([H, P]), wc_row[0:H, :],
                               start=(h == 0), stop=(h == H - 1), skip_group_check=True)
            mm.then_inc(turned, 1)

        @block.scalar
        def _(act):
            act.wait_ge(e1, 1)
            act.activation(ws, ws, ACT.Exp, scale=-1.0)
            act.drain()
            act.activation(ws, ws, ACT.Ln, bias=1.0).then_inc(e1, 1)
            act.wait_ge(e2, 1)
            act.activation(ws, ws, ACT.Exp)
            act.activation(wp, wp, ACT.Exp)
            act.activation(wc_row[0:H, :], wc_row[0:H, :], ACT.Exp)
            act.activation(lf, lf, ACT.Exp, scale=-1.0).then_inc(e2, 1)

        @block.vector
        def _(dve):
            dve.wait_ge(turned, 2)
            dve.wait_ge(m_in, 16)
            dve.wait_ge(ends, 1)
            dve.tensor_scalar(ig, m.psum[0:4, 0, 0:T], bg[0:4, :], None, ALU.add)
            dve.tensor_scalar(lf, m.psum[0:4, 1, 0:T], bgf[0:4, :], None, ALU.add)
            dve.drain()
            dve.scalar_tensor_tensor(ws, lf, -1.0, lf, ALU.mult, ALU.max)
            dve.drain().then_inc(e1, 1)
            dve.wait_ge(e1, 2)
            dve.scalar_tensor_tensor(lf, lf, 0.0, ws, ALU.min, ALU.subtract)
            dve.drain()
            dve.tensor_tensor_scan(big, keep, lf, 0.0, ALU.mult, ALU.add)
            dve.drain()
            dve.tensor_tensor(ig, ig, big, ALU.subtract)
            dve.drain().then_inc(u_done, 1)
            dve.tensor_copy(wp, ig)
            dve.drain()
            dve.tensor_scalar(wp[:, 0:1], wp[:, 0:1], 0.0, None, ALU.max)
            dve.tensor_tensor(seqs(wp)[:, :, 0:1], seqs(wp)[:, :, 0:1], m0[0:H, :].unsqueeze(2), ALU.max)
            dve.drain()
            dve.tensor_tensor_scan(lf, cut, wp, 0.0, ALU.add, ALU.max)
            dve.drain()
            dve.tensor_copy(keep, lf)
            ends_m = lf[:, T_P + T_S - 1:T:T_S]
            dve.tensor_tensor(ws[:, 0:T_P], ig[:, 0:T_P], lf[:, T_P - 1:T_P].to_broadcast([4, T_P]), ALU.subtract)
            dve.tensor_tensor(seqs(ws), seqs(ig), ends_m.unsqueeze(2).to_broadcast([4, B, T_S]), ALU.subtract)
            dve.tensor_scalar(wp[:, 0:T_P], lf[:, 0:T_P], -1.0, None, ALU.mult)
            dve.tensor_tensor(seqs(wp), m0[0:H, :].unsqueeze(2).to_broadcast([4, B, T_S]), seqs(lf), ALU.subtract)
            dve.tensor_tensor(wc_row[0:H, :], m0[0:H, :], ends_m, ALU.subtract)
            dve.drain()
            dve.tensor_tensor(lf, lf, big, ALU.add)
            dve.drain()
            dve.tensor_copy(ml[0:H, 0:1], lf[:, T_P - 1:T_P])
            dve.tensor_copy(ml[0:H, 1:9], lf[:, T_P + T_S - 1:T:T_S])
            dve.drain().then_inc(m_done, 1)
            dve.drain().then_inc(e2, 1)
            dve.wait_ge(e2, 2)
            dve.drain().then_inc(u_done, 1)
            dve.wait_ge(turned, 4)
            for j, (t0, n) in enumerate(TILES):
                dve.tensor_copy(u_col[0:n, j, :], m.psum[0:n, 2, 4 * j:4 * j + 4])
            dve.tensor_copy(wcol.rearrange("p h b -> p (h b)"), m.psum[:, 3, 0:H * B])
    big_m = keep
    em = lf


    n0 = view(m.small, 528, B, H, HC)
    n_new = view(m.small, 784, 1 + B, H, HC)
    n_rows = view(m.arena, 20480, 2, P)
    rden = view(m.arena, 20480 + 2 * P, T)
    with signal(m, "n_in") as n_in, signal(m, "turned") as turned, nc.Block() as block:
        @block.sync
        def _(sp):
            src = I["state_mlstm_n"].rearrange("a b h (c p) -> (a b h c) p", p=P)
            for i in range(2):
                sp.dma_start(n_rows[:, i, :], src[i * P:(i + 1) * P, :]).then_inc(n_in, 16)

        @block.tensor
        def _(pe):
            pe.wait_ge(n_in, 32)
            for i in range(2):
                mm = pe.transpose(m.psum[:, 0, i * P:(i + 1) * P], n_rows[:, i, :], m.ident[:, :])
            mm.then_inc(turned, 1)

        @block.vector
        def _(dve):
            dve.wait_ge(turned, 1)
            dve.tensor_copy(n0.rearrange("p b h c -> p (b h c)"), m.psum[:, 0, 0:2 * P])

    c_slot = view(m.ring, 8192, HC, DH)
    s_t = [view(m.ring, 7424, T_P), view(m.ring, 7424 + T_P, P), view(m.ring, 7424 + T_P + P, 64)]
    vt = view(m.xn, 0, 3, DH)
    kt = view(m.xn, 3 * DH, 2, DH)
    k72 = m.xn[:, 3 * DH:3 * DH + DH // 2].bitcast(BF16)
    v72 = m.xn[:, 4 * DH:4 * DH + DH // 2].bitcast(BF16)
    rep_words = HC * B * ROWS72 // 2
    krep = m.ring[:, 5120:5120 + rep_words].bitcast(BF16).rearrange("p (c b r) -> p c b r", c=HC, b=B)
    vrep = m.ring[:, 2560:2560 + rep_words].bitcast(BF16).rearrange("p (c b r) -> p c b r", c=HC, b=B)
    qn = view(m.ring, 8192, HC, 64)
    rest = view(m.ring, 8704, HC, 64)
    p16 = m.ring[:, 9216:9216 + HC * 32].bitcast(BF16).rearrange("p (c t) -> p c t", c=HC)
    wn = view(m.ring, 9728, HC, B)
    for h in range(H):
        xm_h, xc_h = xm[:, h * HC:(h + 1) * HC], xc[:, h * HC:(h + 1) * HC]
        with signal(m, "expanded") as expanded, signal(m, "prod") as prod, signal(m, "kept") as kept, \
                nc.Block() as block:
            @block.vector
            def _(dve):
                expand(dve, h, 2).then_inc(expanded, 1)

            @block.scalar
            def _(act):
                for c in range(HC):
                    for i, dst in enumerate((q_f, k_f)):
                        act.wait_ge(prod, 2 * c + i + 1)
                        act.activation(dst[:, c, :], m.psum[:, 2 * (c % 4) + i, 0:T], ACT.Copy,
                                       scale=1.0 if i == 0 else DH ** -0.5).then_inc(kept, 1)

            @block.tensor
            def _(pe):
                pe.wait_ge(expanded, 1)
                for c in range(HC):
                    if c >= 4:
                        pe.wait_ge(kept, 2 * (c - 3))
                    for i in range(2):
                        pe.matmul(m.psum[:, 2 * (c % 4) + i, 0:T], bd[:, i, c, :], xc_h[:, c, :], start=True,
                                  stop=True).then_inc(prod, 1)
        with signal(m, "scored") as scored, signal(m, "spread") as spread, signal(m, "arg") as arg, \
                signal(m, "weight") as weight, signal(m, "st_done") as st_done, signal(m, "den") as den, \
                nc.Block() as block:
            @block.tensor
            def _(pe):
                for i, row in enumerate((big_m, em, ws, wp)):
                    mm = pe.matmul(m.psum[:, 3 + i, 0:T], m.ident[0:H, h:h + 1].to_broadcast([H, P]), row, start=True,
                                   stop=True)
                mm.then_inc(spread, 1)
                for a in range(2):
                    for c in range(HC):
                        pe.matmul(m.psum[:, a, 0:T_P - a * P], k_f[:, c, a * P:(a + 1) * P], q_f[:, c, a * P:T_P],
                                  start=(c == 0), stop=(c == HC - 1))
                for c in range(HC):
                    mm = pe.matmul(m.psum[0:64, 2, 0:64], k_f[:, c, T_P:T], q_f[:, c, T_P:T], start=(c == 0),
                                   stop=(c == HC - 1))
                mm.then_inc(scored, 1)
                pe.wait_ge(st_done, 1)
                pe.matmul(m.psum[:, 7, 0:T_P], m.ones[:, :], s_t[0], start=True, stop=False, skip_group_check=True)
                pe.matmul(m.psum[:, 7, P:T_P], m.ones[:, :], s_t[1], start=False, stop=False, skip_group_check=True)
                pe.matmul(m.psum[:, 7, T_P:T], m.ones[0:64, :], s_t[2][0:64, :], start=False, stop=False,
                          skip_group_check=True)
                for c in range(HC):
                    mm = pe.matmul(m.psum[:, 7, T_P:T], m.ones[:, :], qn[:, c, :], start=False, stop=(c == HC - 1),
                                   skip_group_check=True)
                mm.then_inc(den, 1)

            @block.scalar
            def _(act):
                for a in range(3):
                    n = TILES[a][1]
                    act.wait_ge(arg, a + 1)
                    act.activation(s_t[a][0:n, :], s_t[a][0:n, :], ACT.Exp, scale=-1.0).then_inc(weight, 1)

            @block.vector
            def _(dve):
                dve.wait_ge(spread, 1)
                for a, (t0, n) in enumerate(TILES):
                    end = T_P if a < 2 else T
                    dve.tensor_scalar(s_t[a][0:n, :], m.psum[0:n, 3, t0:end], u_col[0:n, a, h:h + 1], 0.0, ALU.subtract,
                                      ALU.max).then_inc(arg, 1)
                dve.wait_ge(scored, 1)
                for a, (t0, n) in enumerate(TILES):
                    dve.wait_ge(weight, a + 1)
                    dve.tensor_tensor(s_t[a][0:n, :], s_t[a][0:n, :], m.psum[0:n, a, 0:s_t[a].shape[1]], ALU.mult)
                dve.drain()
                for a, mask in enumerate((m.causal, m.causal, m.causal8)):
                    n = TILES[a][1]
                    dve.tensor_tensor(s_t[a][0:n, 0:n], s_t[a][0:n, 0:n], mask[0:n, 0:n], ALU.mult)
                q_s = q_f[:, :, T_P:T]
                dve.tensor_tensor(q_s, q_s, m.psum[:, 6, T_P:T].unsqueeze(1).to_broadcast([P, HC, 64]), ALU.mult)
                dve.tensor_tensor(k_f, k_f, m.psum[:, 5, 0:T].unsqueeze(1).to_broadcast([P, HC, T]), ALU.mult)
                dve.drain()
                for b in range(B):
                    dve.tensor_tensor(qn[:, :, b * T_S:(b + 1) * T_S], q_s[:, :, b * T_S:(b + 1) * T_S],
                                      n0[:, b, h, :].unsqueeze(2).to_broadcast([P, HC, T_S]), ALU.mult)
                dve.drain().then_inc(st_done, 1)
                dve.wait_ge(den, 1)
                dve.tensor_copy(rden, m.psum[:, 7, 0:T])
                dve.drain()
                dve.scalar_tensor_tensor(rden, rden, -1.0, rden, ALU.mult, ALU.max)
                dve.drain()
                dve.tensor_tensor(rden, rden, m.psum[:, 4, 0:T], ALU.max)
                dve.drain()
                dve.reciprocal(rden, rden)
        with signal(m, "turned") as turned, signal(m, "copied") as copied, nc.Block() as block:
            @block.tensor
            def _(pe):
                for j, (t0, n) in enumerate(TILES):
                    for c in range(HC):
                        mm = pe.transpose(m.psum[0:n, 2 * j + c // 4, (c % 4) * P:(c % 4 + 1) * P], xm_h[:, c, t0:t0 + n],
                                          m.ident[:, :])
                    mm.then_inc(turned, 1)
                for j, (t0, n) in enumerate(TILES[0:2]):
                    if j:
                        pe.wait_ge(copied, 1)
                    for c in range(HC):
                        bank = (6, 0)[j] + c // 4
                        mm = pe.transpose(m.psum[0:n, bank, (c % 4) * P:(c % 4 + 1) * P], k_f[:, c, t0:t0 + n],
                                          m.ident[:, :])
                    mm.then_inc(turned, 1)

            @block.scalar
            def _(act):
                for j, (t0, n) in enumerate(TILES):
                    act.wait_ge(turned, j + 1)
                    act.copy(vt[0:n, j, :], m.psum[0:n, 2 * j:2 * j + 2, :].rearrange("p a b -> p (a b)")).then_inc(copied, 1)
                for j in range(2):
                    bank = (6, 0)[j]
                    act.wait_ge(turned, 4 + j)
                    act.copy(kt[:, j, :], m.psum[:, bank:bank + 2, :].rearrange("p a b -> p (a b)")).then_inc(copied, 1)

            @block.vector
            def _(dve):
                dve.tensor_reduce(n_new[:, 0, h, :].unsqueeze(2), k_f[:, :, 0:T_P], AX_X, ALU.add)
                for b in range(B):
                    dve.tensor_reduce(n_new[:, 1 + b, h, :].unsqueeze(2), k_f[:, :, T_P + b * T_S:T_P + (b + 1) * T_S],
                                      AX_X, ALU.add)
                    dve.tensor_scalar(wn[:, :, b], n0[:, b, h, :], wcol[:, h, b:b + 1], None, ALU.mult)
                dve.drain()
                dve.tensor_tensor(n_new[:, 1:1 + B, h, :], n_new[:, 1:1 + B, h, :], wn.rearrange("p c b -> p b c"), ALU.add)

                def split(source, rep, outer):
                    for i in range(SPL):
                        dve.tensor_copy(p16, source if i == 0 else rest)
                        dve.drain()
                        if i < SPL - 1:
                            dve.tensor_tensor(rest, source if i == 0 else rest, p16, ALU.subtract)
                        for j in range(SPL):
                            r = (i * SPL + j if outer else j * SPL + i) * T_S
                            dve.tensor_copy(rep[:, :, :, r:r + T_S], p16.rearrange("p c (b t) -> p c b t", b=B))
                        dve.drain()
                split(k_f[:, :, T_P:T], krep, True)
                dve.wait_ge(turned, 5)
                split(xm_h[:, :, T_P:T], vrep, False)
        with signal(m, "num") as num, signal(m, "c_done") as c_done, signal(m, "c_kept") as c_kept, \
                signal(m, "stored") as stored, nc.Block() as block:
            @block.tensor
            def _(pe):
                for c in range(HC):
                    ps = m.psum[:, c // 2, (c % 2) * T_P:(c % 2 + 1) * T_P]
                    pe.matmul(ps, vt[:, 0, c * P:(c + 1) * P], s_t[0], start=True, stop=False, skip_group_check=True)
                    pe.matmul(ps[:, P:T_P], vt[:, 1, c * P:(c + 1) * P], s_t[1], start=False, stop=True,
                              skip_group_check=True).then_inc(num, 1)
                for c in range(HC):
                    for e in range(2):
                        i = 2 * c + e
                        if i >= 4:
                            pe.wait_ge(c_kept, i - 3)
                        for a in range(2):
                            mm = pe.matmul(m.psum[:, 4 + i % 4, :], kt[:, a, c * P:(c + 1) * P],
                                           vt[:, a, e * 512:(e + 1) * 512], start=(a == 0), stop=(a == 1))
                        mm.then_inc(c_done, 1)

            @block.vector
            def _(dve):
                for c in range(HC):
                    if c % 2 == 0:
                        dve.wait_ge(num, c + 2)
                    dve.tensor_tensor(xm_h[:, c, 0:T_P], m.psum[:, c // 2, (c % 2) * T_P:(c % 2 + 1) * T_P],
                                      rden[:, 0:T_P], ALU.mult)

            @block.scalar
            def _(act):
                for i in range(2 * HC):
                    act.wait_ge(c_done, i + 1)
                    act.copy(c_slot[:, i // 2, (i % 2) * 512:(i % 2 + 1) * 512], m.psum[:, 4 + i % 4, :]).then_inc(c_kept, 1)

            @block.sync
            def _(sp):
                for c in range(HC):
                    sp.wait_ge(c_kept, 2 * c + 2)
                    sp.dma_start(O["p_m_C"][0, 0, h, c * P:(c + 1) * P, :], c_slot[:, c, :]).then_inc(stored, 16)
                sp.wait_ge(stored, 16 * HC)
        c_in = I["state_mlstm_C"][0].rearrange("b h (c p) e -> b h c p e", p=P)
        c_out = O["s_m_C"][0].rearrange("b h (c p) e -> b h c p e", p=P)
        LAG = 3
        with ExitStack() as ctx:
            landed = [ctx.enter_context(signal(m, f"state_landed{c}")) for c in range(HC)]
            stored = [ctx.enter_context(signal(m, f"state_stored{c}")) for c in range(HC)]
            turned = ctx.enter_context(signal(m, "turned"))
            k_kept = ctx.enter_context(signal(m, "k_kept"))
            v_kept = ctx.enter_context(signal(m, "v_kept"))
            outer = ctx.enter_context(signal(m, "outer"))
            updated = ctx.enter_context(signal(m, "updated"))
            num = ctx.enter_context(signal(m, "num"))
            block = ctx.enter_context(nc.Block())

            def one(v, i):
                return v[i] if isinstance(i, int) else v[bass.ds(i, 1)].squeeze(0)

            @block.sync
            def _(sp):
                def load(b, c):
                    sp.dma_start(c_slot[:, c, :], one(c_in, b)[h, c]).then_inc(landed[c], 16)

                def sequence(b, more):
                    for c in range(HC):
                        sp.wait_ge(updated, b * (2 * HC) + (2 * c + 4))
                        sp.dma_start(one(c_out, b)[h, c], c_slot[:, c, :]).then_inc(stored[c], 16)
                        if c < LAG:
                            if not (isinstance(b, int) and b == 0):
                                sp.wait_ge(stored[c - LAG + HC], b * 16)
                            load(b, c - LAG + HC)
                        elif more:
                            sp.wait_ge(stored[c - LAG], b * 16 + 16)
                            load(b + 1, c - LAG)

                for c in range(HC - LAG):
                    load(0, c)
                sequence(0, True)
                with sp.Fori(1, B - 1) as b:
                    sequence(b, True)
                sequence(B - 1, False)
                for c in range(HC):
                    sp.wait_ge(stored[c], 16 * B)

            @block.tensor
            def _(pe):
                for c in range(HC):
                    pe.matmul(m.psum[:, 0, c * 64:(c + 1) * 64], vt[0:64, 2, c * P:(c + 1) * P], s_t[2][0:64, :],
                              start=(c == 0), stop=False, skip_group_check=True)
                with pe.Fori(0, B) as b:
                    pe.wait_ge(k_kept, b + 1)
                    pe.wait_ge(v_kept, b + 1)
                    for i, rep in enumerate((krep, vrep)):
                        for c in range(HC):
                            mm = pe.matmul(m.psum[0:ROWS72, 1 + 2 * i + c // 4, (c % 4) * P:(c % 4 + 1) * P],
                                           rep[:, c, bass.ds(b, 1), :].squeeze(1), m.identb[:, :], start=True, stop=True)
                        mm.then_inc(turned, 1)
                    for c in range(HC):
                        pe.wait_ge(landed[c], b * 16 + 16)
                        for e in range(HC):
                            pe.matmul(m.psum[:, 0, bass.ds(b * T_S + e * 64, T_S)], c_slot[:, c, e * P:(e + 1) * P],
                                      q_f[:, c, bass.ds(b * T_S + T_P, T_S)], start=False, stop=False,
                                      skip_group_check=True)
                        if c == 0:
                            pe.wait_ge(k_kept, b + 2)
                            pe.wait_ge(v_kept, b + 2)
                        for e in range(2):
                            pe.wait_ge(updated, b * (2 * HC) + (2 * c + e + 1))
                            pe.matmul(m.psum[:, 5 + e, :], k72[0:ROWS72, c * P:(c + 1) * P],
                                      v72[0:ROWS72, e * 512:(e + 1) * 512], start=True, stop=True).then_inc(outer, 1)
                pe.drain().then_inc(num, 1)

            @block.scalar
            def _(act):
                act.sem_inc(k_kept, 1)
                with act.Fori(0, B) as b:
                    act.wait_ge(turned, b * 2 + 1)
                    act.copy(k72[0:ROWS72, :], m.psum[0:ROWS72, 1:3, :].rearrange("p a b -> p (a b)")).then_inc(k_kept, 1)

            @block.vector
            def _(dve):
                dve.sem_inc(v_kept, 1)
                dve.sem_inc(updated, 2)
                with dve.Fori(0, B) as b:
                    dve.wait_ge(turned, b * 2 + 2)
                    dve.tensor_copy(v72[0:ROWS72, :],
                                    m.psum[0:ROWS72, 3:5, :].rearrange("p a b -> p (a b)")).then_inc(v_kept, 1)
                    for c in range(HC):
                        for e in range(2):
                            dve.wait_ge(outer, b * (2 * HC) + (2 * c + e + 1))
                            part_c = c_slot[:, c, e * 512:(e + 1) * 512]
                            dve.scalar_tensor_tensor(part_c, part_c, wcol[:, h, bass.ds(b, 1)], m.psum[:, 5 + e, :],
                                                     ALU.mult, ALU.add).then_inc(updated, 1)
                dve.wait_ge(num, 1)
                dve.tensor_tensor(xm_h[:, :, T_P:T], m.psum[:, 0, :].rearrange("p (c t) -> p c t", c=HC),
                                  rden[:, T_P:T].unsqueeze(1).to_broadcast([P, HC, 64]), ALU.mult)
        sq = view(m.ring, 0, HC, T)
        mean = view(m.ring, 2560, T)
        with signal(m, "summed") as summed, signal(m, "centred") as centred, signal(m, "sqd") as sqd, \
                signal(m, "root") as root, nc.Block() as block:
            @block.tensor
            def _(pe):
                for c in range(HC):
                    mm = pe.matmul(m.psum[:, 0, 0:T], m.ones[:, :], xm_h[:, c, :], start=(c == 0), stop=(c == HC - 1))
                mm.then_inc(summed, 1)
                for c in range(HC):
                    pe.wait_ge(sqd, c + 1)
                    mm = pe.matmul(m.psum[:, 1, 0:T], m.ones[:, :], sq[:, c, :], start=(c == 0), stop=(c == HC - 1))
                mm.then_inc(summed, 1)

            @block.scalar
            def _(act):
                for c in range(HC):
                    act.wait_ge(centred, c + 1)
                    act.activation(sq[:, c, :], xm_h[:, c, :], ACT.Square).then_inc(sqd, 1)
                act.wait_ge(root, 1)
                act.activation(mean, mean, ACT.Sqrt).then_inc(root, 1)

            @block.vector
            def _(dve):
                dve.wait_ge(summed, 1)
                dve.tensor_scalar(mean, m.psum[:, 0, 0:T], 1.0 / DH, None, ALU.mult)
                dve.drain()
                for c in range(HC):
                    dve.tensor_tensor(xm_h[:, c, :], xm_h[:, c, :], mean, ALU.subtract).then_inc(centred, 1)
                dve.wait_ge(summed, 2)
                dve.drain()
                dve.tensor_scalar(mean, m.psum[:, 1, 0:T], 1.0 / DH, EPS, ALU.mult, ALU.add)
                dve.drain().then_inc(root, 1)
                dve.wait_ge(root, 2)
                dve.reciprocal(mean, mean)
                dve.drain()
                for c in range(HC):
                    dve.scalar_tensor_tensor(xm_h[:, c, :], xm_h[:, c, :], param(m, "l1_norm_g", h * HC + c), mean,
                                             ALU.mult, ALU.mult)
                dve.drain()
                for c in range(HC):
                    dve.scalar_tensor_tensor(xm_h[:, c, :], xc_h[:, c, :], param(m, "l1_skip", h * HC + c),
                                             xm_h[:, c, :], ALU.mult, ALU.add)
    store_columns(nc, m, n_new.rearrange("p b h c -> p (b h c)"), 9 * H * HC, [
        (0, H * HC, O["p_m_n"].rearrange("a b h (c p) -> (a b h c) p", p=P)),
        (H * HC, 9 * H * HC, O["s_m_n"].rearrange("a b h (c p) -> (a b h c) p", p=P))])

    rmsnorm(nc, m, "norm_mix_g", DC, m.XN)

    def gate_with_z(dve, e, n):
        y = xm[:, bass.ds(n, 1), :].squeeze(1)
        return dve.tensor_tensor(y, y, e, ALU.mult)

    linear(nc, m, I["l1_w_up"][0][:, DI:2 * DI], DC, lambda k: m.XN[:, k, :], gate=gate_with_z)
    linear(nc, m, I["l1_w_down"][0], IC, lambda k: xm[:, k, :])


def build(nc, I, O):
    with ExitStack() as ctx:
        m = Mem(nc, ctx)
        proj = view(m.arena, 0, IN0C + 1, T)
        setup(nc, m, I)
        rmsnorm(nc, m, "norm_mix_g", 0, m.XN)
        first_projection(nc, m, I)
        rg_lru(nc, m, I, O)
        gla(nc, m, I, O)
        linear(nc, m, I["l0_w_out"][0], DC, lambda k: proj[:, GA + k if k < 8 else GG + k - 8, :])
        rmsnorm(nc, m, "norm_ffn_g", 0, m.XN)
        moe(nc, m, I, 0)
        rmsnorm(nc, m, "norm_mix_g", DC, m.XN)
        mlstm(nc, m, I, O)
        rmsnorm(nc, m, "norm_ffn_g", DC, m.XN)
        moe(nc, m, I, 1)
        final_norm(nc, m, O)


INS = """x_prompt x_sample state_lru_conv state_lru_h state_gla_S state_mlstm_conv state_mlstm_C state_mlstm_n
state_mlstm_m norm_mix_g norm_ffn_g norm_final_g l0_w_in l0_lru_conv_w l0_lru_conv_b l0_lru_wa l0_lru_ba l0_lru_wx
l0_lru_bx l0_lru_lam l0_gla_wa2 l0_gla_ba2 l0_gla_norm_g l0_w_out l1_w_up l1_conv_w l1_conv_b l1_wq l1_wk l1_wv l1_w_ig
l1_b_ig l1_w_fg l1_b_fg l1_skip l1_norm_g l1_w_down moe_w_rg moe_b_rg moe_w_re moe_b_re moe_w_gate moe_w_up
moe_w_down""".split()
OUTS = [("y_prompt", (1, T_P, D)), ("y_sample", (B, T_S, D))] + [
    (f"{g}_{name}", (1, n) + shape) for g, n in (("p", 1), ("s", B)) for name, shape in (
        ("lru_conv", (CW - 1, W_LRU)), ("lru_h", (W_LRU,)), ("gla_S", (H, DK, DV)), ("m_conv", (CW - 1, DI)),
        ("m_C", (H, DH, DH)), ("m_n", (H, DH)), ("m_m", (H,)))]


def kernel(**inputs):
    import numpy as np
    import concourse.bacc as bacc
    from concourse.bass_utils import run_bass_kernel_spmd

    nc = bacc.Bacc("TRN2", target_bir_lowering=False, num_devices=1)
    arrays, ins, outs = {}, {}, {}
    for name in INS:
        a = np.ascontiguousarray(inputs[name])
        arrays[f"in_{name}"] = a
        ins[name] = nc.dram_tensor(f"in_{name}", a.shape, mybir.dt.from_np(a.dtype), kind="ExternalInput").ap()
    for name, shape in OUTS:
        outs[name] = nc.dram_tensor(f"out_{name}", shape, F32, kind="ExternalOutput").ap()
    build(nc, ins, outs)
    r = run_bass_kernel_spmd(nc, [arrays], core_ids=[0])
    return tuple(r.results[0][f"out_{name}"] for name, _ in OUTS)
```

```python
from contextlib import ExitStack, contextmanager

import concourse.bass as bass
from concourse import mybir

ALU = mybir.AluOpType
ACT = mybir.ActivationFunctionType
AX_X = mybir.AxisListType.X
F32 = mybir.dt.float32
BF16 = mybir.dt.bfloat16

P = 128
D = 2048
T_P = 256
B = 8
T_S = 8
T = T_P + B * T_S
TILES = [(0, 128), (128, 128), (256, 64)]
EPS = 1e-6
CW = 4
DC = D // P
W_LRU = 1024
LC = W_LRU // P
H = 4
DK, DV = 128, 256
IN0 = 5136
IN0C = IN0 // P
RANK = 16
XA, GA, QA, KA, VA, GG, AL = 0, 8, 16, 20, 24, 32, 40
DI = 4096
QB = 4
IC = DI // P
DH = DI // H
HC = DH // P
NE, NG, EG = 16, 4, 4
FE = 256
CONV0 = (IN0C + 1) * T
GC = 32
NCH = T_P // GC
SLOT = 2048
NSLOT = 8
KPS = 4
TPB = 4
SPL = 3
ROWS72 = SPL * SPL * T_S
NEG = -1.0e30

PARAM_TILES = [
    [("norm_mix_g", 2 * DC), ("norm_ffn_g", 2 * DC), ("norm_final_g", DC)],
    [("l0_lru_conv_w", CW * LC), ("l0_lru_conv_b", LC), ("l0_lru_ba", LC), ("l0_lru_bx", LC), ("l0_lru_lam", LC),
     ("l0_gla_ba2", H), ("l0_gla_norm_g", 8)],
    [("state_lru_h", B * LC)],
    [("l1_conv_w", CW * IC)],
    [("l1_conv_b", IC), ("l1_skip", IC), ("l1_norm_g", IC)],
]
PCOL = {}
for _i, _tile in enumerate(PARAM_TILES):
    _at = 0
    for _n, _k in _tile:
        PCOL[_n] = _i * P + _at
        _at += _k


class Signals:

    MOST = 30

    def __init__(self, nc, count=120):
        self.nc = nc
        self.sems = [nc.alloc_semaphore(f"signal{i}") for i in range(count)]
        self.next = 0
        self.held = 0

    def take(self):
        if not self.held and self.next > len(self.sems) - self.MOST:
            numbers = [s.num for s in self.sems]
            with self.nc.Block() as block:
                @block.gpsimd
                def _(pool):
                    pool.sem_clear(range(min(numbers), max(numbers) + 1))
            self.next = 0
        self.next += 1
        self.held += 1
        return self.sems[self.next - 1]


@contextmanager
def signal(m, name):
    yield m.signals.take()
    m.signals.held -= 1


class Mem:

    def __init__(self, nc, ctx):
        self.signals = Signals(nc)

        def sb(name, shape, dt=F32):
            return ctx.enter_context(nc.sbuf_tensor(name, shape, dt))

        self.x = sb("x_resid", [P, DC, T])
        self.xn = sb("x_norm", [P, DC * T])
        self.ring = sb("ring", [P, NSLOT * SLOT])
        self.arena = sb("arena", [P, 21600])
        self.ident = sb("ident", [P, P])
        self.identb = sb("identb", [P, P], BF16)
        self.ones = sb("ones", [P, P])
        self.causal = sb("causal", [P, P])
        self.causal32 = sb("causal32", [P, P])
        self.causal8 = sb("causal8", [64, 64])
        self.prm = sb("params", [P, len(PARAM_TILES) * P])
        self.neg = sb("negated", [P, 2 * LC])
        self.keep32 = sb("keep32", [P, T])
        self.small = sb("small", [P, 1088])
        self.rows = sb("gate_rows", [4, 7 * T])
        self.psum = ctx.enter_context(nc.psum_tensor("psum", [P, 8, 512], F32))
        self.XN = self.xn[:, :].rearrange("p (c t) -> p c t", t=T)


def view(buf, at, *shape):
    n = 1
    for s in shape:
        n *= s
    v = buf[:, at:at + n]
    if len(shape) == 1:
        return v
    names = "abcd"[:len(shape)]
    return v.rearrange(f"p ({' '.join(names)}) -> p {' '.join(names)}", **dict(zip(names[1:], shape[1:])))


def param(m, name, i=0):
    return m.prm[:, PCOL[name] + i:PCOL[name] + i + 1]


def setup(nc, m, I):
    x_tok = view(m.arena, 0, 3, D)
    prow = view(m.arena, 3 * D, len(PARAM_TILES), P)
    with signal(m, "rows_in") as rows_in, signal(m, "consts") as consts, signal(m, "turned") as turned, \
            signal(m, "copied") as copied, nc.Block() as block:
        @block.sync
        def _(sp):
            sp.dma_start(x_tok[:, 0:2, :], I["x_prompt"].rearrange("a (j p) d -> p (a j) d", p=P)).then_inc(rows_in, 16)
            sp.dma_start(x_tok[0:64, 2, :], I["x_sample"].rearrange("b t d -> (b t) d")).then_inc(rows_in, 16)
            for i, tile in enumerate(PARAM_TILES):
                at = 0
                for name, k in tile:
                    src = I[name]
                    letters = " ".join("abcd"[:len(src.shape)])
                    src = src.rearrange(f"{letters} -> ({letters})") if len(src.shape) > 1 else src
                    sp.dma_start(prow[at:at + k, i, :], src.rearrange("(k p) -> k p", p=P)).then_inc(rows_in, 16)
                    at += k

        @block.gpsimd
        def _(pool):
            pool.memset(m.ones[:, :], 1.0)
            pool.memset(m.causal32[:, :], 1.0)
            pool.drain()
            pool.affine_select(m.ident[:, :], m.ones[:, :], [[1, P]], ALU.is_equal, 0.0, base=0, channel_multiplier=-1)
            pool.affine_select(m.causal[:, :], m.ones[:, :], [[1, P]], ALU.is_ge, 0.0, base=0, channel_multiplier=-1)
            pool.drain()
            pool.affine_select(m.causal32[:, :].rearrange("p (a b) -> p a b", b=GC),
                               m.causal[:, :].rearrange("p (a b) -> p a b", b=GC),
                               [[-GC, P // GC], [0, GC]], ALU.is_ge, 0.0, base=0, channel_multiplier=1)
            pool.affine_select(m.causal8[:, :].rearrange("p (a b) -> p a b", b=T_S),
                               m.causal[0:64, 0:64].rearrange("p (a b) -> p a b", b=T_S),
                               [[-T_S, B], [0, T_S]], ALU.is_ge, 0.0, base=0, channel_multiplier=1)
            pool.memset(m.keep32[:, :], 1.0)
            pool.drain()
            pool.memset(m.keep32[:, 0:T_P:GC], 0.0)
            pool.memset(m.keep32[:, T_P:T:T_S], 0.0)
            pool.tensor_copy(m.identb[:, :], m.ident[:, :])
            pool.drain().then_inc(consts, 1)

        @block.tensor
        def _(pe):
            pe.wait_ge(consts, 1)
            pe.wait_ge(rows_in, 16 * (2 + sum(len(t) for t in PARAM_TILES)))
            for c in range(DC):
                if c >= 8:
                    pe.wait_ge(copied, c - 7)
                for j, (t0, n) in enumerate(TILES):
                    last = pe.transpose(m.psum[:, c % 8, t0:t0 + n], x_tok[0:n, j, c * P:(c + 1) * P],
                                        m.ident[0:n, 0:n])
                last.then_inc(turned, 1)
            for i, tile in enumerate(PARAM_TILES):
                k = sum(n for _, n in tile)
                pe.wait_ge(copied, DC - 8 + i + 1)
                pe.transpose(m.psum[:, i, 0:k], prow[0:k, i, :], m.ident[0:k, 0:k]).then_inc(turned, 1)

        @block.scalar
        def _(act):
            for c in range(DC):
                act.wait_ge(turned, c + 1)
                act.copy(m.x[:, c, :], m.psum[:, c % 8, 0:T]).then_inc(copied, 1)
            for i, tile in enumerate(PARAM_TILES):
                k = sum(n for _, n in tile)
                act.wait_ge(turned, DC + i + 1)
                act.copy(m.prm[:, i * P:i * P + k], m.psum[:, i, 0:k]).then_inc(copied, 1)


def rmsnorm(nc, m, gain, at, out):
    sq = view(m.ring, 0, 2, T)
    rstd = view(m.ring, 2 * T, T)
    with signal(m, "squared") as squared, signal(m, "summed") as summed, signal(m, "root") as root, \
            nc.Block() as block:
        @block.scalar
        def _(act):
            for c in range(DC):
                if c >= 2:
                    act.wait_ge(summed, c - 1)
                act.activation(sq[:, c % 2, :], m.x[:, c, :], ACT.Square).then_inc(squared, 1)
            act.wait_ge(root, 1)
            act.activation(rstd, rstd, ACT.Sqrt).then_inc(root, 1)

        @block.tensor
        def _(pe):
            for c in range(DC):
                pe.wait_ge(squared, c + 1)
                pe.matmul(m.psum[:, 0, 0:T], m.ones[:, :], sq[:, c % 2, :], start=(c == 0),
                          stop=(c == DC - 1)).then_inc(summed, 1)

        @block.vector
        def _(dve):
            dve.wait_ge(summed, DC)
            dve.tensor_scalar(rstd, m.psum[:, 0, 0:T], 1.0 / D, EPS, ALU.mult, ALU.add).then_inc(root, 1)
            dve.wait_ge(root, 2)
            dve.reciprocal(rstd, rstd)
            dve.drain()
            for c in range(DC):
                dve.scalar_tensor_tensor(out[:, c, :], m.x[:, c, :], param(m, gain, at + c), rstd,
                                         ALU.mult, ALU.mult)


def linear(nc, m, weights, kc, rhs, copy_to=None, gate=None, conv=None):
    kg = kc // KPS
    cbs = NSLOT // kg
    width = TPB * P
    passes = weights.shape[1] // width // cbs
    w = weights.rearrange("(g k p) n -> p g k n", k=KPS, p=P)
    slots = view(m.ring, 0, NSLOT, KPS, 512)
    e = view(m.arena, 20480, 2, T)
    with ExitStack() as ctx:
        def signals(name, n):
            return [ctx.enter_context(signal(m, f"{name}{i}")) for i in range(n)]

        landed = signals("landed", NSLOT)
        used = signals("used", NSLOT)
        tile_done = signals("tile_done", cbs)
        by_act = signals("by_act", cbs)
        by_dve = signals("by_dve", cbs)
        block = ctx.enter_context(nc.Block())

        @block.sync
        def _(sp):
            def load(i, s):
                col = (i * cbs + s // kg) * width
                sp.dma_start(slots[:, s, :, :], w[:, s % kg, :, bass.ds(col, width)]).then_inc(landed[s], 16)

            for s in range(NSLOT):
                load(0, s)
            with sp.Fori(1, passes) as i:
                for s in range(NSLOT):
                    if s % kg < kg - 1:
                        sp.wait_ge(used[s], i)
                    else:
                        sp.wait_ge(tile_done[s // kg], i * TPB)
                    load(i, s)

        @block.tensor
        def _(pe):
            with pe.Fori(0, passes) as i:
                for s in range(NSLOT):
                    cb, g = s // kg, s % kg
                    pe.wait_ge(landed[s], i * 16 + 16)
                    if g == 0:
                        if copy_to is not None:
                            pe.wait_ge(by_act[cb], i * TPB + TPB)
                        else:
                            pe.wait_ge(by_dve[cb], i * TPB + TPB)
                    for k in range(KPS):
                        for t in range(TPB):
                            mm = pe.matmul(m.psum[:, cb * TPB + t, 0:T], slots[:, s, k, t * P:(t + 1) * P],
                                           rhs(g * KPS + k), start=(g == 0 and k == 0),
                                           stop=(g == kg - 1 and k == KPS - 1))
                            if g == kg - 1 and k == KPS - 1:
                                mm.then_inc(tile_done[cb], 1)
                    if g < kg - 1:
                        mm.then_inc(used[s], 1)

        @block.scalar
        def _(act):
            if copy_to is not None:
                for cb in range(cbs):
                    act.sem_inc(by_act[cb], TPB)
                with act.Fori(0, passes) as i:
                    for cb in range(cbs):
                        for t in range(TPB):
                            act.wait_ge(tile_done[cb], i * TPB + (t + 1))
                            act.copy(copy_to((i * cbs + cb) * TPB + t),
                                     m.psum[:, cb * TPB + t, 0:T]).then_inc(by_act[cb], 1)
                        if conv.silu:
                            act.wait_ge(by_dve[cb], i + 1)
                            x = conv.xout[:, bass.ds((i * cbs + cb) * TPB, TPB), :]
                            act.activation(x, x, ACT.Silu)
            elif gate is not None:
                with act.Fori(0, passes) as i:
                    for cb in range(cbs):
                        for t in range(TPB):
                            act.wait_ge(tile_done[cb], i * TPB + (t + 1))
                            if t >= 2:
                                act.wait_ge(by_dve[cb], i * TPB + (TPB + t - 1))
                            elif cb:
                                act.wait_ge(by_dve[cb - 1], i * TPB + (TPB + t + 3))
                            else:
                                act.wait_ge(by_dve[cbs - 1], i * TPB + TPB)
                            act.activation(e[:, t % 2, :], m.psum[:, cb * TPB + t, 0:T], ACT.Silu).then_inc(by_act[cb], 1)

        @block.vector
        def _(dve):
            if copy_to is not None:
                with dve.Fori(0, conv.passes) as i:
                    for cb in range(cbs):
                        dve.wait_ge(by_act[cb], i * TPB + 2 * TPB)
                        conv.convolve(dve, (i * cbs + cb) * TPB, TPB).then_inc(by_dve[cb], 1)
                return
            for cb in range(cbs):
                dve.sem_inc(by_dve[cb], TPB)
            with dve.Fori(0, passes) as i:
                for cb in range(cbs):
                    for t in range(TPB):
                        n = (i * cbs + cb) * TPB + t
                        ps = m.psum[:, cb * TPB + t, 0:T]
                        if gate is not None:
                            dve.wait_ge(by_act[cb], i * TPB + (t + 1))
                            gate(dve, e[:, t % 2, :], n).then_inc(by_dve[cb], 1)
                        else:
                            dve.wait_ge(tile_done[cb], i * TPB + (t + 1))
                            x = m.x[:, bass.ds(n, 1), :].squeeze(1)
                            dve.tensor_tensor(x, x, ps, ALU.add).then_inc(by_dve[cb], 1)


class Conv:

    def __init__(self, m, xin, xout, chunks, w_name, b_name, passes, silu):
        self.m, self.xin, self.xout, self.chunks, self.passes, self.silu = m, xin, xout, chunks, passes, silu
        self.w, self.b = PCOL[w_name], PCOL[b_name]

    def begin(self, nc, state, rows, tmp):
        m, n, half = self.m, self.chunks, min(self.chunks, 16)
        with signal(m, "state_in") as state_in, signal(m, "turned") as turned, nc.Block() as block:
            @block.sync
            def _(sp):
                sp.dma_start(rows[0:24, :], state.rearrange("a b r d -> (a b r) d")).then_inc(state_in, 16)

            @block.tensor
            def _(pe):
                pe.wait_ge(state_in, 16)
                for c in range(n):
                    mm = pe.transpose(m.psum[:, c // half, (c % half) * 24:(c % half) * 24 + 24],
                                      rows[0:24, c * P:(c + 1) * P], m.ident[0:24, 0:24])
                mm.then_inc(turned, 1)

            @block.vector
            def _(dve):
                new = self.xout[:, :, T_P:T].rearrange("p c (b t) -> p c b t", b=B)
                dve.tensor_copy(self.xout[:, :, T_P:T],
                                m.prm[:, self.b:self.b + n].unsqueeze(2).to_broadcast([P, n, B * T_S]))
                dve.drain()
                dve.wait_ge(turned, 1)
                for j in range(CW - 1):
                    k = CW - 1 - j
                    for g in range(n // half):
                        st = m.psum[:, g, 0:24 * half].rearrange("p (c b r) -> p c b r", b=B, r=3)
                        w = m.prm[:, self.w + j * n + g * half:self.w + j * n + (g + 1) * half]
                        part = tmp[:, g * half:(g + 1) * half, :, 0:k]
                        for r in range(k):
                            dve.tensor_tensor(part[:, :, :, r], st[:, :, :, j + r],
                                              w.unsqueeze(2).to_broadcast([P, half, B]), ALU.mult)
                    dve.drain()
                    dve.tensor_tensor(new[:, :, :, 0:k], new[:, :, :, 0:k], tmp[:, :, :, 0:k], ALU.add)
                    dve.drain()

    def convolve(self, dve, first, count):
        for j in reversed(range(CW)):
            d = CW - 1 - j
            for k in range(count):
                c = first + k
                x, y = (v[:, bass.ds(c, 1), :].squeeze(1) for v in (self.xin, self.xout))
                w = self.m.prm[:, bass.ds(c + (self.w + j * self.chunks), 1)]
                if d == 0:
                    dve.tensor_scalar(y[:, 0:T_P], x[:, 0:T_P], w, self.m.prm[:, bass.ds(c + self.b, 1)], ALU.mult,
                                      ALU.add)
                else:
                    dve.scalar_tensor_tensor(y[:, d:T_P], x[:, 0:T_P - d], w, y[:, d:T_P], ALU.mult, ALU.add)
                xs, ys = (v[:, T_P:T].rearrange("p (b t) -> p b t", b=B) for v in (x, y))
                last = dve.scalar_tensor_tensor(ys[:, :, d:T_S], xs[:, :, 0:T_S - d], w, ys[:, :, d:T_S], ALU.mult,
                                                ALU.add)
            if j:
                dve.drain()
        return dve.drain()


def store_last_rows(nc, m, xin, chunks, cols, prompt_rows, sample_rows):
    with nc.Block() as block:
        @block.vector
        def _(dve):
            for i in range(1 + B):
                end = T_P + i * T_S
                dve.tensor_copy(cols[:, i * 3 * chunks:(i + 1) * 3 * chunks].rearrange("p (r c) -> p c r", r=3),
                                xin[:, :, end - 3:end])
    store_columns(nc, m, cols, 27 * chunks, [
        (0, 3 * chunks, prompt_rows.rearrange("a b r (c p) -> (a b r c) p", p=P)),
        (3 * chunks, 27 * chunks, sample_rows.rearrange("a b r (c p) -> (a b r c) p", p=P))])


def moe(nc, m, I, layer):
    xn = m.XN
    logit = view(m.small, 0, 3, 20)
    rank = view(m.small, 64, 4)
    bias = view(m.small, 72, 20)
    wr = view(m.ring, 0, DC, 20)
    tmp = [view(m.small, 96 + 16 * i, 3, 4) for i in range(10)]
    mx, s1 = view(m.small, 280, 3, 1), view(m.small, 284, 3, 1)
    m1, pg = view(m.small, 288, 3, 1), view(m.small, 292, 3, 1)
    prod = view(m.small, 300, 3, NG, EG)
    gates = view(m.small, 352, 3, NG, EG)
    gt16 = view(m.ring, 4096, T)
    gb = view(m.arena, 0, NE, T)
    hid = view(m.arena, NE * T, NE, 2, T)
    ex = view(m.arena, 3 * NE * T, 2, T)
    up = view(m.arena, 3 * NE * T + 2 * T, 2, T)
    with signal(m, "w_in") as w_in, signal(m, "init") as init, signal(m, "logits") as logits, \
            signal(m, "to_exp") as to_exp, signal(m, "expd") as expd, signal(m, "gated") as gated, \
            signal(m, "turned") as turned, signal(m, "gt_done") as gt_done, signal(m, "spread") as spread, \
            signal(m, "kept") as kept, nc.Block() as block:
        @block.sync
        def _(sp):
            sp.dma_start(wr[:, :, 0:NG], I["moe_w_rg"][layer].rearrange("(c p) g -> p c g", p=P)).then_inc(w_in, 16)
            sp.dma_start(wr[:, :, NG:20], I["moe_w_re"][layer].rearrange("(c p) g -> p c g", p=P)).then_inc(w_in, 16)
            sp.dma_start(bias[:, 0:NG], I["moe_b_rg"][layer].partition_broadcast(P)).then_inc(w_in, 16)
            sp.dma_start(bias[:, NG:20], I["moe_b_re"][layer].partition_broadcast(P)).then_inc(w_in, 16)

        @block.gpsimd
        def _(pool):
            for g in range(4):
                pool.memset(rank[:, g:g + 1], float(4 - g))
            pool.memset(logit[:, :, :], 0.0)
            pool.drain().then_inc(init, 1)

        @block.tensor
        def _(pe):
            pe.wait_ge(w_in, 64)
            for j, (t0, n) in enumerate(TILES):
                for c in range(DC):
                    mm = pe.matmul(m.psum[0:n, j, 0:20], xn[:, c, t0:t0 + n], wr[:, c, :], start=(c == 0),
                                   stop=(c == DC - 1))
            mm.then_inc(logits, 1)
            pe.wait_ge(gated, 1)
            for j, (t0, n) in enumerate(TILES):
                mm = pe.transpose(m.psum[0:NE, 3, t0:t0 + n], gates[0:n, j, :, :].rearrange("p g e -> p (g e)"),
                                  m.ident[0:n, 0:n])
            mm.then_inc(turned, 1)
            pe.wait_ge(gt_done, 1)
            for e in range(NE):
                if e >= 4:
                    pe.wait_ge(kept, e - 3)
                pe.matmul(m.psum[:, 4 + e % 4, 0:T], m.ident[0:NE, e:e + 1].to_broadcast([NE, P]), gt16[0:NE, :],
                          start=True, stop=True).then_inc(spread, 1)

        @block.scalar
        def _(act):
            act.wait_ge(to_exp, 1)
            act.activation(tmp[3], tmp[3], ACT.Exp).then_inc(expd, 1)
            act.wait_ge(to_exp, 2)
            act.activation(tmp[9], tmp[9], ACT.Exp).then_inc(expd, 1)
            for e in range(NE):
                act.wait_ge(spread, e + 1)
                act.copy(gb[:, e, :], m.psum[:, 4 + e % 4, 0:T]).then_inc(kept, 1)

        @block.vector
        def _(dve):
            bc = [P, 3, 4]
            rk = rank.unsqueeze(1).to_broadcast(bc)

            def first_largest(values, largest, ranked, onehot):
                dve.tensor_reduce(largest, values, AX_X, ALU.max)
                dve.drain()
                dve.tensor_tensor(ranked, values, largest.to_broadcast(bc), ALU.is_ge)
                dve.drain()
                dve.tensor_tensor(ranked, ranked, rk, ALU.mult)
                dve.drain()
                dve.tensor_reduce(s1, ranked, AX_X, ALU.max)
                dve.drain()
                dve.tensor_tensor(onehot, ranked, s1.to_broadcast(bc), ALU.is_equal)
                dve.drain()

            dve.wait_ge(init, 1)
            dve.wait_ge(logits, 1)
            for j, (t0, n) in enumerate(TILES):
                dve.tensor_tensor(logit[0:n, j, :], m.psum[0:n, j, 0:20], bias[0:n, :], ALU.add)
            dve.drain()
            lg = logit[:, :, 0:NG]
            first_largest(lg, mx, tmp[0], tmp[1])
            dve.tensor_tensor(tmp[3], lg, mx.to_broadcast(bc), ALU.subtract)
            dve.drain().then_inc(to_exp, 1)
            el4 = logit[:, :, NG:20].rearrange("p j (g e) -> p j g e", g=NG)
            for g in range(NG):
                dve.tensor_tensor(prod[:, :, g, :], el4[:, :, g, :], tmp[1][:, :, g:g + 1].to_broadcast(bc), ALU.mult)
            dve.drain()
            dve.tensor_tensor(tmp[4], prod[:, :, 0, :], prod[:, :, 1, :], ALU.add)
            dve.tensor_tensor(tmp[5], prod[:, :, 2, :], prod[:, :, 3, :], ALU.add)
            dve.drain()
            dve.tensor_tensor(tmp[4], tmp[4], tmp[5], ALU.add)
            dve.drain()
            first_largest(tmp[4], m1, tmp[0], tmp[6])
            dve.scalar_tensor_tensor(tmp[5], tmp[6], NEG, tmp[4], ALU.mult, ALU.add)
            dve.drain()
            first_largest(tmp[5], mx, tmp[0], tmp[7])
            dve.tensor_tensor(tmp[9], tmp[4], m1.to_broadcast(bc), ALU.subtract)
            dve.drain().then_inc(to_exp, 1)
            dve.tensor_tensor(tmp[7], tmp[7], tmp[6], ALU.add)
            dve.wait_ge(expd, 2)
            dve.drain()
            dve.tensor_tensor(tmp[8], tmp[9], tmp[7], ALU.mult)
            dve.tensor_reduce(pg, tmp[3], AX_X, ALU.add)
            dve.drain()
            dve.tensor_reduce(s1, tmp[8], AX_X, ALU.add)
            dve.drain()
            dve.tensor_tensor(s1, s1, pg, ALU.mult)
            dve.drain()
            dve.reciprocal(s1, s1)
            dve.drain()
            dve.tensor_tensor(tmp[8], tmp[8], s1.to_broadcast(bc), ALU.mult)
            dve.drain()
            for g in range(NG):
                dve.tensor_tensor(gates[:, :, g, :], tmp[8], tmp[1][:, :, g:g + 1].to_broadcast(bc), ALU.mult)
            dve.drain().then_inc(gated, 1)
            dve.wait_ge(turned, 1)
            dve.tensor_copy(gt16[0:NE, :], m.psum[0:NE, 3, 0:T]).then_inc(gt_done, 1)

    wg = I["moe_w_gate"][layer].rearrange("e (g k p) f -> e p g k f", k=KPS, p=P)
    wu = I["moe_w_up"][layer].rearrange("e (g k p) f -> e p g k f", k=KPS, p=P)
    wd = I["moe_w_down"][layer].rearrange("e (k p) n -> e p k n", p=P)
    slots = view(m.ring, 0, NSLOT, KPS, 512)
    down = view(m.ring, 4 * SLOT, 2, D)
    with ExitStack() as ctx:
        landed = [ctx.enter_context(signal(m, f"gate_up_landed{s}")) for s in range(4)]
        used = [ctx.enter_context(signal(m, f"gate_up_used{s}")) for s in range(3)]
        down_landed = ctx.enter_context(signal(m, "down_landed"))
        hidden_raw = ctx.enter_context(signal(m, "hidden_raw"))
        expd = ctx.enter_context(signal(m, "expd"))
        up_kept = ctx.enter_context(signal(m, "up_kept"))
        hidden = ctx.enter_context(signal(m, "hidden"))
        down_done = ctx.enter_context(signal(m, "down_done"))
        added = ctx.enter_context(signal(m, "added"))
        block = ctx.enter_context(nc.Block())

        @block.sync
        def _(sp):
            def load_gate_up(e):
                fixed = isinstance(e, int)
                for s in range(4):
                    if not (fixed and e == 0):
                        sp.wait_ge(used[s] if s < 3 else hidden_raw, e)
                    for at, w in ((0, wg), (FE, wu)):
                        src = w[e, :, s, :, :] if fixed else w[bass.ds(e, 1), :, s, :, :].squeeze(0)
                        sp.dma_start(slots[:, s, :, at:at + FE], src).then_inc(landed[s], 16)

            def load_down(e):
                fixed = isinstance(e, int)
                if not (fixed and e == 0):
                    sp.wait_ge(down_done, e * DC)
                sp.dma_start(down, wd[e] if fixed else wd[bass.ds(e, 1), :, :, :].squeeze(0)).then_inc(down_landed, 16)

            load_gate_up(0)
            load_down(0)
            load_gate_up(1)
            with sp.Fori(2, NE) as e:
                load_gate_up(e)
                load_down(e - 1)
            load_down(NE - 1)

        @block.tensor
        def _(pe):
            def gate_up(e):
                for s in range(4):
                    pe.wait_ge(landed[s], e * 32 + 32)
                    if s == 0 and not (isinstance(e, int) and e == 0):
                        pe.wait_ge(hidden, e * 2)
                    for k in range(KPS):
                        for t in range(TPB):
                            mm = pe.matmul(m.psum[:, t, 0:T], slots[:, s, k, t * P:(t + 1) * P], xn[:, s * KPS + k, :],
                                           start=(s == 0 and k == 0), stop=(s == 3 and k == KPS - 1))
                    if s < 3:
                        mm.then_inc(used[s], 1)
                mm.then_inc(hidden_raw, 1)

            def project_down(e):
                pe.wait_ge(hidden, e * 2 + 2)
                pe.wait_ge(down_landed, e * 16 + 16)
                for n in range(DC):
                    if isinstance(e, int) and e == 0 and n < 4:
                        pass
                    else:
                        pe.wait_ge(added, e * DC + (n - 3))
                    for k in range(2):
                        rhs = hid[:, e, k, :] if isinstance(e, int) else hid[:, bass.ds(e, 1), k, :].squeeze(1)
                        mm = pe.matmul(m.psum[:, 4 + n % 4, 0:T], down[:, k, n * P:(n + 1) * P], rhs, start=(k == 0),
                                       stop=(k == 1))
                    mm.then_inc(down_done, 1)

            gate_up(0)
            gate_up(1)
            project_down(0)
            with pe.Fori(2, NE) as e:
                gate_up(e)
                project_down(e - 1)
            project_down(NE - 1)

        @block.scalar
        def _(act):
            act.wait_ge(hidden_raw, 1)
            for f in range(2):
                act.activation(ex[:, f, :], m.psum[:, f, 0:T], ACT.Silu).then_inc(expd, 1)
            with act.Fori(1, NE) as e:
                act.wait_ge(hidden_raw, e + 1)
                act.wait_ge(hidden, e * 2)
                for f in range(2):
                    act.activation(ex[:, f, :], m.psum[:, f, 0:T], ACT.Silu).then_inc(expd, 1)

        @block.vector
        def _(dve):
            def hidden_values(e):
                dve.wait_ge(hidden_raw, e + 1)
                g = gb[:, e, :] if isinstance(e, int) else gb[:, bass.ds(e, 1), :].squeeze(1)
                for f in range(2):
                    dve.tensor_tensor(up[:, f, :], m.psum[:, 2 + f, 0:T], g, ALU.mult)
                dve.drain()
                for f in range(2):
                    dve.wait_ge(expd, e * 2 + (f + 1))
                    h = hid[:, e, f, :] if isinstance(e, int) else hid[:, bass.ds(e, 1), f, :].squeeze(1)
                    dve.tensor_tensor(h, up[:, f, :], ex[:, f, :], ALU.mult).then_inc(hidden, 1)

            def add_down(e):
                for n in range(DC):
                    dve.wait_ge(down_done, e * DC + (n + 1))
                    dve.tensor_tensor(m.x[:, n, :], m.x[:, n, :], m.psum[:, 4 + n % 4, 0:T], ALU.add).then_inc(added, 1)

            hidden_values(0)
            hidden_values(1)
            add_down(0)
            with dve.Fori(2, NE) as e:
                hidden_values(e)
                add_down(e - 1)
            add_down(NE - 1)


def store_columns(nc, m, columns, n, dram_rows):
    stage = view(m.xn, 0, 8, P)
    tiles = [(i, min(P, n - i)) for i in range(0, n, P)]
    with signal(m, "turned") as turned, signal(m, "copied") as copied, signal(m, "stored") as stored, \
            nc.Block() as block:
        @block.tensor
        def _(pe):
            for i, (a, k) in enumerate(tiles):
                pe.transpose(m.psum[0:k, i, 0:P], columns[:, a:a + k], m.ident[:, :]).then_inc(turned, 1)

        @block.scalar
        def _(act):
            for i, (a, k) in enumerate(tiles):
                act.wait_ge(turned, i + 1)
                act.copy(stage[0:k, i, :], m.psum[0:k, i, 0:P]).then_inc(copied, 1)

        @block.sync
        def _(sp):
            stores = 0
            for i, (a, k) in enumerate(tiles):
                sp.wait_ge(copied, i + 1)
                for lo, hi, rows in dram_rows:
                    f, t = max(lo, a), min(hi, a + k)
                    if f < t:
                        sp.dma_start(rows[f - lo:t - lo, :], stage[f - a:t - a, i, :]).then_inc(stored, 16)
                        stores += 1
            sp.wait_ge(stored, 16 * stores)


def rg_lru(nc, m, I, O):
    proj = view(m.arena, 0, IN0C + 1, T)
    xc = view(m.arena, CONV0, LC, T)
    wa = view(m.arena, 15700, LC, P)
    wx = view(m.arena, 16800, LC, P)
    cols = view(m.arena, 17900, 27 * LC)
    r, g, a, b, h = (view(m.ring, 2560 * i, LC, T) for i in range(5))
    store_last_rows(nc, m, proj[:, XA:XA + LC], LC, cols, O["p_lru_conv"], O["s_lru_conv"])
    c8 = m.neg[:, 0:LC]
    tl = m.neg[:, LC:2 * LC]
    lam = m.prm[:, PCOL["l0_lru_lam"]:PCOL["l0_lru_lam"] + LC]
    h0 = m.prm[:, PCOL["state_lru_h"]:PCOL["state_lru_h"] + B * LC].rearrange("p (b c) -> p c b", b=B)
    hl = view(m.small, 0, 9 * LC)
    add0 = view(m.small, 96, LC, B)
    with signal(m, "blank") as blank, signal(m, "w_in") as w_in, signal(m, "negs") as negs, \
            signal(m, "prod") as prod, signal(m, "expd") as expd, signal(m, "sig") as sig, \
            signal(m, "pwr") as pwr, signal(m, "om") as om, signal(m, "ge") as ge, nc.Block() as block:
        @block.gpsimd
        def _(pool):
            pool.memset(wa, 0.0)
            pool.memset(wx, 0.0)
            pool.drain().then_inc(blank, 1)

        @block.sync
        def _(sp):
            sp.wait_ge(blank, 1)
            for w, name in ((wa, "l0_lru_wa"), (wx, "l0_lru_wx")):
                src = I[name].rearrange("a (c two) i o -> two i (a c) o", two=2)
                sp.dma_start(w[0:64, :, 0:64], src[0]).then_inc(w_in, 16)
                sp.dma_start(w[64:128, :, 64:128], src[1]).then_inc(w_in, 16)

        @block.tensor
        def _(pe):
            pe.wait_ge(w_in, 64)
            for q, w in enumerate((wa, wx)):
                for c in range(LC):
                    if q:
                        pe.wait_ge(expd, 2 + c + 1)
                    pe.matmul(m.psum[:, c, 0:T], w[:, c, :], xc[:, c, :], start=True, stop=True).then_inc(prod, 1)

        @block.scalar
        def _(act):
            act.wait_ge(negs, 1)
            act.activation(tl, tl, ACT.Exp, scale=-1.0).then_inc(expd, 1)
            act.drain()
            act.activation(tl, tl, ACT.Ln, bias=1.0).then_inc(expd, 1)
            for q, dst in enumerate((r, g)):
                for c in range(LC):
                    act.wait_ge(prod, q * LC + c + 1)
                    act.activation(dst[:, c, :], m.psum[:, c, 0:T], ACT.Sigmoid,
                                   bias=param(m, ("l0_lru_ba", "l0_lru_bx")[q], c)).then_inc(expd, 1)
            act.wait_ge(sig, 1)
            for c in range(LC):
                act.activation(a[:, c, :], r[:, c, :], ACT.Exp, scale=c8[:, c:c + 1]).then_inc(pwr, 1)
            for c in range(LC):
                act.activation(b[:, c, :], r[:, c, :], ACT.Tanh, scale=c8[:, c:c + 1]).then_inc(pwr, 1)
            act.drain()
            act.activation(r, proj[:, GA:GA + LC], ACT.Gelu_apprx_tanh).then_inc(ge, 1)
            act.wait_ge(om, 1)
            act.activation(b, b, ACT.Sqrt, scale=-1.0).then_inc(om, 1)

        @block.vector
        def _(dve):
            dve.scalar_tensor_tensor(tl, lam, -1.0, lam, ALU.mult, ALU.max)
            dve.drain().then_inc(negs, 1)
            dve.wait_ge(expd, 2)
            dve.tensor_scalar(c8, lam, -1.0, 0.0, ALU.mult, ALU.max)
            dve.drain()
            dve.tensor_tensor(c8, c8, tl, ALU.add)
            dve.drain()
            dve.tensor_scalar(c8, c8, -8.0, None, ALU.mult)
            dve.wait_ge(expd, 2 + 2 * LC)
            dve.drain().then_inc(sig, 1)
            dve.tensor_tensor(g, g, xc, ALU.mult)
            dve.wait_ge(pwr, LC)
            dve.tensor_tensor(h, a, a, ALU.mult)
            dve.drain()
            dve.wait_ge(pwr, 2 * LC)
            dve.scalar_tensor_tensor(b, h, 1.0, b, ALU.add, ALU.mult)
            dve.drain().then_inc(om, 1)
            dve.wait_ge(om, 2)
            dve.tensor_tensor(b, b, g, ALU.mult)
            dve.tensor_tensor(add0, a[:, :, T_P:T:T_S], h0, ALU.mult)
            dve.drain()
            dve.tensor_tensor(b[:, :, T_P:T:T_S], b[:, :, T_P:T:T_S], add0, ALU.add)
            dve.memset(a[:, :, T_P:T:T_S], 0.0)
            dve.memset(a[:, :, 0:1], 0.0)
            dve.drain()
            flat = "p c t -> p (c t)"
            dve.tensor_tensor_scan(h.rearrange(flat), a.rearrange(flat), b.rearrange(flat), 0.0, ALU.mult, ALU.add)
            dve.wait_ge(ge, 1)
            dve.drain()
            dve.tensor_copy(hl[:, 0:LC], h[:, :, T_P - 1:T_P].squeeze(2))
            dve.tensor_copy(hl[:, LC:9 * LC].rearrange("p (b c) -> p c b", b=B), h[:, :, T_P + T_S - 1:T:T_S])
            dve.drain()
            dve.tensor_tensor(proj[:, GA:GA + LC], h, r, ALU.mult)
    store_columns(nc, m, hl, 9 * LC, [(0, LC, O["p_lru_h"].rearrange("a b (c p) -> (a b c) p", p=P)),
                                      (LC, 9 * LC, O["s_lru_h"].rearrange("a b (c p) -> (a b c) p", p=P))])


def gla(nc, m, I, O):
    proj = view(m.arena, 0, IN0C + 1, T)
    bc, t1, qe, ke, qi, kh, ab = (view(m.ring, 1280 * i, H, T) for i in range(7))
    vt = view(m.ring, 8960, 3, H, DV)
    kt = view(m.ring, 12032, 3, H, DK)
    att = view(m.ring, 13568, H, 3, P)
    sp_ = view(m.ring, 15104, H, DV)
    ebl = view(m.small, 0, H, 16)
    wa2 = view(m.small, 64, 512)
    ss = view(m.arena, 13200, B, H, DV)
    km = view(m.arena, 0, 2, B, DK)
    osb = proj[:, QA:QA + 8]

    def cut(v, w):
        return (v[:, :, 0:T_P].rearrange("p h (c l) -> p h c l", l=GC) if w == 0 else
                v[:, :, T_P:T].rearrange("p h (c l) -> p h c l", l=T_S))

    with signal(m, "w_in") as w_in, signal(m, "prod") as prod, signal(m, "zd") as zd, \
            signal(m, "lnd") as lnd, signal(m, "dd") as dd, signal(m, "ee") as ee, nc.Block() as block:
        @block.sync
        def _(sp):
            sp.dma_start(wa2[0:RANK, :], I["l0_gla_wa2"].rearrange("a r n -> (a r) n")).then_inc(w_in, 16)
            sp.wait_ge(w_in, 16)

        @block.tensor
        def _(pe):
            pe.wait_ge(w_in, 16)
            for h in range(H):
                pe.matmul(m.psum[:, h, 0:T], wa2[0:RANK, h * DK:(h + 1) * DK], proj[0:RANK, AL, :], start=True,
                          stop=True).then_inc(prod, 1)

        @block.scalar
        def _(act):
            act.wait_ge(zd, 1)
            act.activation(ab, ab, ACT.Exp, scale=-1.0)
            act.drain()
            act.activation(ab, ab, ACT.Ln, bias=1.0).then_inc(lnd, 1)
            act.wait_ge(dd, 1)
            act.activation(qe, t1, ACT.Exp)
            act.activation(ke, t1, ACT.Exp, scale=-1.0)
            act.activation(qi, bc, ACT.Exp).then_inc(ee, 1)
            act.wait_ge(dd, 2)
            act.activation(kh, t1, ACT.Exp)
            act.activation(ebl, ebl, ACT.Exp).then_inc(ee, 1)

        @block.vector
        def _(dve):
            for h in range(H):
                dve.wait_ge(prod, h + 1)
                dve.tensor_scalar(t1[:, h, :], m.psum[:, h, 0:T], param(m, "l0_gla_ba2", h), None, ALU.add)
            dve.drain()
            dve.scalar_tensor_tensor(ab, t1, -1.0, t1, ALU.mult, ALU.max).then_inc(zd, 1)
            dve.wait_ge(lnd, 1)
            dve.scalar_tensor_tensor(t1, t1, 0.0, ab, ALU.min, ALU.subtract)
            dve.drain()
            dve.tensor_scalar(t1, t1, 1.0 / 16.0, None, ALU.mult)
            dve.drain()
            for h in range(H):
                dve.tensor_tensor_scan(bc[:, h, :], m.keep32[:, :], t1[:, h, :], 0.0, ALU.mult, ALU.add)
            dve.drain()
            for w, (l, ref) in enumerate(((GC, GC // 2 - 1), (T_S, T_S // 2 - 1))):
                b4 = cut(bc, w)
                dve.tensor_tensor(cut(t1, w), b4, b4[:, :, :, ref:ref + 1].to_broadcast([P, H, 8, l]), ALU.subtract)
                dve.tensor_copy(ebl[:, :, 8 * w:8 * w + 8], b4[:, :, :, l - 1:l].squeeze(3))
            dve.drain().then_inc(dd, 1)
            dve.wait_ge(ee, 1)
            for w, l in ((0, GC), (1, T_S)):
                b4 = cut(bc, w)
                dve.tensor_tensor(cut(t1, w), b4[:, :, :, l - 1:l].to_broadcast([P, H, 8, l]), b4, ALU.subtract)
            dve.drain().then_inc(dd, 1)
            q, k = proj[:, QA:QA + H], proj[:, KA:KA + H]
            dve.scalar_tensor_tensor(qe, q, DK ** -0.5, qe, ALU.mult, ALU.mult)
            dve.scalar_tensor_tensor(qi, q, DK ** -0.5, qi, ALU.mult, ALU.mult)
            dve.tensor_tensor(ke, ke, k, ALU.mult)
            dve.wait_ge(ee, 2)
            dve.tensor_tensor(kh, kh, k, ALU.mult)
    with signal(m, "turned") as turned, signal(m, "st_in") as st_in, nc.Block() as block:
        @block.sync
        def _(sp):
            for b in range(B):
                sp.dma_start(ss[:, b, :, :], I["state_gla_S"][0, b].rearrange("h d e -> d h e")).then_inc(st_in, 16)
            sp.wait_ge(st_in, 16 * B)

        @block.tensor
        def _(pe):
            for j, (t0, n) in enumerate(TILES):
                for c in range(8):
                    mm = pe.transpose(m.psum[0:n, 2 * j + c // 4, (c % 4) * P:(c % 4 + 1) * P], proj[:, VA + c, t0:t0 + n],
                                      m.ident[:, :])
                mm.then_inc(turned, 1)
            for j, (t0, n) in enumerate(TILES[0:2]):
                for h in range(H):
                    mm = pe.transpose(m.psum[0:n, 6 + j, h * P:(h + 1) * P], kh[:, h, t0:t0 + n], m.ident[:, :])
                mm.then_inc(turned, 1)

        @block.vector
        def _(dve):
            for j, (t0, n) in enumerate(TILES):
                dve.wait_ge(turned, j + 1)
                dve.tensor_copy(vt[0:n, j].rearrange("p h e -> p (h e)"),
                                m.psum[0:n, 2 * j:2 * j + 2, :].rearrange("p a b -> p (a b)"))
            for j, (t0, n) in enumerate(TILES[0:2]):
                dve.wait_ge(turned, 4 + j)
                dve.tensor_copy(kt[0:n, j].rearrange("p h e -> p (h e)"), m.psum[0:n, 6 + j, :])
    with signal(m, "turned") as turned, signal(m, "scored") as scored, nc.Block() as block:
        @block.tensor
        def _(pe):
            t0, n = TILES[2]
            for h in range(H):
                mm = pe.transpose(m.psum[0:n, 4, h * P:(h + 1) * P], kh[:, h, t0:t0 + n], m.ident[:, :])
            mm.then_inc(turned, 1)
            for h in range(H):
                for j, (t0, n) in enumerate(TILES):
                    mm = pe.matmul(m.psum[0:n, h, j * P:j * P + n], ke[:, h, t0:t0 + n], qe[:, h, t0:t0 + n], start=True,
                                   stop=True)
                mm.then_inc(scored, 1)

        @block.vector
        def _(dve):
            dve.wait_ge(turned, 1)
            dve.tensor_copy(kt[0:64, 2].rearrange("p h e -> p (h e)"), m.psum[0:64, 4, :])
            for h in range(H):
                dve.wait_ge(scored, h + 1)
                for j, (t0, n) in enumerate(TILES):
                    mask = m.causal8 if j == 2 else m.causal32
                    dve.tensor_tensor(att[0:n, h, j, 0:n], m.psum[0:n, h, j * P:j * P + n], mask[0:n, 0:n], ALU.mult)
    for pair in range(2):
        heads = (2 * pair, 2 * pair + 1)
        with signal(m, "masked") as masked, signal(m, "upd") as upd, signal(m, "new_s") as new_s, \
                signal(m, "supd") as supd, signal(m, "snew") as snew, signal(m, "o_done") as o_done, \
                nc.Block() as block:
            @block.gpsimd
            def _(pool):
                for i, h in enumerate(heads):
                    for b in range(B):
                        pool.affine_select(km[0:64, i, b, :], kt[0:64, 2, h, :], [[0, DK]], ALU.is_ge, 0.0,
                                           base=-T_S * b, channel_multiplier=1)
                pool.drain()
                for i, h in enumerate(heads):
                    for b in range(B):
                        pool.affine_select(km[0:64, i, b, :], km[0:64, i, b, :], [[0, DK]], ALU.is_ge, 0.0,
                                           base=T_S * b + T_S - 1, channel_multiplier=-1)
                pool.drain().then_inc(masked, 1)

            @block.tensor
            def _(pe):
                def o(i, e):
                    return m.psum[:, 2 * i + e]
                for i, h in enumerate(heads):
                    for e in range(2):
                        for j, (t0, n) in enumerate(TILES):
                            pe.matmul(o(i, e)[:, t0:t0 + n], vt[0:n, j, h, e * P:(e + 1) * P], att[0:n, h, j, 0:n],
                                      start=(j == 0), stop=False, skip_group_check=True)
                pe.wait_ge(masked, 1)
                for c in range(NCH):
                    j, r0 = c // 4, (c % 4) * GC
                    for i, h in enumerate(heads):
                        if c:
                            pe.wait_ge(new_s, 2 * (c - 1) + i + 1)
                            for e in range(2):
                                pe.matmul(o(i, e)[:, c * GC:(c + 1) * GC], sp_[:, h, e * P:(e + 1) * P],
                                          qi[:, h, c * GC:(c + 1) * GC], start=False, stop=False, skip_group_check=True)
                        pe.matmul(m.psum[:, 4 + i, 0:DV], kt[r0:r0 + GC, j, h, :], vt[r0:r0 + GC, j, h, :], start=True,
                                  stop=True, tile_position=(r0, 0)).then_inc(upd, 1)
                    b = c
                    for i, h in enumerate(heads):
                        for e in range(2):
                            pe.matmul(o(i, e)[:, T_P + b * T_S:T_P + (b + 1) * T_S], ss[:, b, h, e * P:(e + 1) * P],
                                      qi[:, h, T_P + b * T_S:T_P + (b + 1) * T_S], start=False, stop=False,
                                      skip_group_check=True)
                        if b:
                            pe.wait_ge(snew, 2 * (b - 1) + i + 1)
                        pe.matmul(m.psum[:, 6 + i, 0:DV], km[0:64, i, b, :], vt[0:64, 2, h, :], start=True,
                                  stop=True).then_inc(supd, 1)
                pe.drain().then_inc(o_done, 1)

            @block.vector
            def _(dve):
                for c in range(NCH):
                    for i, h in enumerate(heads):
                        dve.wait_ge(upd, 2 * c + i + 1)
                        if c == 0:
                            dve.tensor_copy(sp_[:, h, :], m.psum[:, 4 + i, 0:DV]).then_inc(new_s, 1)
                        else:
                            dve.scalar_tensor_tensor(sp_[:, h, :], sp_[:, h, :], ebl[:, h, c:c + 1], m.psum[:, 4 + i, 0:DV],
                                                     ALU.mult, ALU.add).then_inc(new_s, 1)
                    b = c
                    for i, h in enumerate(heads):
                        dve.wait_ge(supd, 2 * b + i + 1)
                        dve.scalar_tensor_tensor(ss[:, b, h, :], ss[:, b, h, :], ebl[:, h, 8 + b:9 + b],
                                                 m.psum[:, 6 + i, 0:DV], ALU.mult, ALU.add).then_inc(snew, 1)
                    dve.drain()
                dve.wait_ge(o_done, 1)
                for i, h in enumerate(heads):
                    for e in range(2):
                        dve.tensor_copy(osb[:, 2 * h + e, :], m.psum[:, 2 * i + e, 0:T])
    sq = view(m.ring, 0, 8, T)
    rs = view(m.ring, 2560, H, T)
    sg = view(m.ring, 5120, 8, T)
    with signal(m, "sqd") as sqd, signal(m, "summed") as summed, signal(m, "root") as root, \
            signal(m, "expd") as expd, signal(m, "stored") as stored, nc.Block() as block:
        @block.sync
        def _(sp):
            for b in range(B):
                sp.dma_start(O["s_gla_S"][0, b].rearrange("h d e -> d h e"), ss[:, b, :, :]).then_inc(stored, 16)
            sp.dma_start(O["p_gla_S"][0, 0].rearrange("h d e -> d h e"), sp_).then_inc(stored, 16)
            sp.wait_ge(stored, 16 * (B + 1))

        @block.scalar
        def _(act):
            act.activation(sq, osb, ACT.Square).then_inc(sqd, 1)
            act.activation(sg, proj[:, GG:GG + 8], ACT.Silu).then_inc(expd, 1)
            act.wait_ge(root, 1)
            act.activation(rs, rs, ACT.Sqrt).then_inc(root, 1)

        @block.tensor
        def _(pe):
            pe.wait_ge(sqd, 1)
            for h in range(H):
                for e in range(2):
                    mm = pe.matmul(m.psum[:, h, 0:T], m.ones[:, :], sq[:, 2 * h + e, :], start=(e == 0), stop=(e == 1))
                mm.then_inc(summed, 1)

        @block.vector
        def _(dve):
            for h in range(H):
                dve.wait_ge(summed, h + 1)
                dve.tensor_scalar(rs[:, h, :], m.psum[:, h, 0:T], 1.0 / DV, EPS, ALU.mult, ALU.add)
            dve.drain().then_inc(root, 1)
            dve.wait_ge(root, 2)
            dve.reciprocal(rs, rs)
            dve.drain()
            for c in range(8):
                dve.scalar_tensor_tensor(osb[:, c, :], osb[:, c, :], param(m, "l0_gla_norm_g", c), rs[:, c // 2, :],
                                         ALU.mult, ALU.mult)
            dve.wait_ge(expd, 1)
            dve.drain()
            dve.tensor_tensor(proj[:, GG:GG + 8], osb, sg, ALU.mult)


def first_projection(nc, m, I):
    proj = view(m.arena, 0, IN0C + 1, T)
    w_in = I["l0_w_in"][0]
    conv = Conv(m, proj[:, XA:XA + LC], view(m.arena, CONV0, LC, T), LC, "l0_lru_conv_w", "l0_lru_conv_b", 1, False)
    conv.begin(nc, I["state_lru_conv"], view(m.arena, 18200, W_LRU), view(m.ring, 0, LC, B, 3))
    linear(nc, m, w_in[:, 0:IN0C * P], DC, lambda k: m.XN[:, k, :],
           copy_to=lambda n: proj[:, bass.ds(n, 1), :].squeeze(1), conv=conv)
    wt = view(m.ring, 0, DC, RANK)
    with signal(m, "tail_in") as tail_in, signal(m, "tail") as tail, nc.Block() as block:
        @block.sync
        def _(sp):
            sp.dma_start(wt, w_in[:, IN0C * P:IN0].rearrange("(k p) n -> p k n", p=P)).then_inc(tail_in, 16)

        @block.tensor
        def _(pe):
            pe.wait_ge(tail_in, 16)
            for k in range(DC):
                mm = pe.matmul(m.psum[0:RANK, 0, 0:T], wt[:, k, :], m.XN[:, k, :], start=(k == 0), stop=(k == DC - 1))
            mm.then_inc(tail, 1)

        @block.scalar
        def _(act):
            act.wait_ge(tail, 1)
            act.copy(proj[0:RANK, AL, :], m.psum[0:RANK, 0, 0:T])


def final_norm(nc, m, O):
    y = view(m.arena, 0, DC, T)
    rmsnorm(nc, m, "norm_final_g", 0, y)
    y_tok = view(m.arena, DC * T, 3, D)
    with signal(m, "turned") as turned, signal(m, "copied") as copied, signal(m, "stored") as stored, \
            nc.Block() as block:
        @block.tensor
        def _(pe):
            q = 0
            for j, (t0, n) in enumerate(TILES):
                for g in range(4):
                    if q >= 8:
                        pe.wait_ge(copied, q - 7)
                    for c in range(4):
                        mm = pe.transpose(m.psum[0:n, q % 8, c * P:(c + 1) * P], y[:, 4 * g + c, t0:t0 + n], m.ident[:, :])
                    mm.then_inc(turned, 1)
                    q += 1

        @block.scalar
        def _(act):
            q = 0
            for j, (t0, n) in enumerate(TILES):
                for g in range(4):
                    act.wait_ge(turned, q + 1)
                    act.copy(y_tok[0:n, j, g * 512:(g + 1) * 512], m.psum[0:n, q % 8, :]).then_inc(copied, 1)
                    q += 1

        @block.sync
        def _(sp):
            outs = [O["y_prompt"][0, 0:P, :], O["y_prompt"][0, P:T_P, :], O["y_sample"].rearrange("b t d -> (b t) d")]
            for j, (t0, n) in enumerate(TILES):
                sp.wait_ge(copied, 4 * (j + 1))
                sp.dma_start(outs[j], y_tok[0:n, j, :]).then_inc(stored, 16)
            sp.wait_ge(stored, 48)


def mlstm(nc, m, I, O):
    xm = view(m.arena, 0, IC, T)
    xc = view(m.arena, IC * T, IC, T)
    conv = Conv(m, xm, xc, IC, "l1_conv_w", "l1_conv_b", IC // (2 * TPB), True)
    conv.begin(nc, I["state_mlstm_conv"], view(m.arena, 0, DI), view(m.ring, 0, IC, B, 3))
    linear(nc, m, I["l1_w_up"][0][:, 0:DI], DC, lambda k: m.XN[:, k, :],
           copy_to=lambda n: xm[:, bass.ds(n, 1), :].squeeze(1), conv=conv)
    store_last_rows(nc, m, xm, IC, view(m.arena, 20480, 27 * IC), O["p_m_conv"], O["s_m_conv"])

    wq, wk, wv = (view(m.small, IC * QB * i, IC, QB) for i in range(3))
    q_f = view(m.ring, 0, HC, T)
    k_f = view(m.ring, 2560, HC, T)
    bd = view(m.ring, 5120, 3, HC, P)
    blk = view(m.small, 384, 32)
    bg, bgf = view(m.small, 416, 1), view(m.small, 417, 1)
    u_col = view(m.small, 448, 3, H)
    NW = 3 * IC
    wg_rows = view(m.ring, 0, 2, P, 4)
    wg = view(m.ring, 1024, 8, NW)
    spread_o = view(m.ring, 2048, QB, P)
    row_of = view(m.ring, 2560, QB)
    term = view(m.ring, 3072, 3, 8, IC)
    total = view(m.ring, 4096, 3, 8, IC)
    g_xc, g_xm = view(m.ring, 5120, IC, 8), view(m.ring, 5376, IC, 8)
    gates8 = view(m.ring, 6144, T)

    def expand(dve, h):
        for i, w in enumerate((wq, wk, wv)):
            for c in range(HC):
                dve.tensor_tensor(bd[:, i, c, :].rearrange("p (b o) -> p b o", o=QB),
                                  w[:, h * HC + c, :].unsqueeze(1).to_broadcast([P, 32, QB]),
                                  blk.unsqueeze(2).to_broadcast([P, 32, QB]), ALU.mult)
        return dve.drain()

    with signal(m, "w_in") as w_in, signal(m, "blk_done") as blk_done, signal(m, "turned") as turned, \
            signal(m, "wg_kept") as wg_kept, signal(m, "spread_made") as spread_made, \
            signal(m, "spread") as spread, signal(m, "folded") as folded, signal(m, "gates_done") as gates_done, \
            signal(m, "gates_kept") as gates_kept, nc.Block() as block:
        @block.sync
        def _(sp):
            for j, name in enumerate(("l1_w_ig", "l1_w_fg")):
                sp.dma_start(wg_rows[0:NW, j, :, :], I[name][0].rearrange("(n p) g -> n p g", p=P)).then_inc(w_in, 16)
            for w, name in ((wq, "l1_wq"), (wk, "l1_wk"), (wv, "l1_wv")):
                sp.dma_start(w, I[name][0].rearrange("(c b) i o -> (b i) c o", c=IC)).then_inc(w_in, 16)
            sp.dma_start(bg[0:4, :], I["l1_b_ig"].rearrange("a g -> g a")).then_inc(w_in, 16)
            sp.dma_start(bgf[0:4, :], I["l1_b_fg"].rearrange("a g -> g a")).then_inc(w_in, 16)
            sp.wait_ge(w_in, 7 * 16)

        @block.gpsimd
        def _(pool):
            pool.memset(blk, 1.0)
            pool.drain()
            pool.affine_select(blk, blk, [[-QB, 32]], ALU.is_ge, 0.0, base=0, channel_multiplier=1)
            pool.drain()
            pool.affine_select(blk, blk, [[QB, 32]], ALU.is_ge, 0.0, base=QB - 1, channel_multiplier=-1)
            pool.drain().then_inc(blk_done, 1)

        @block.tensor
        def _(pe):
            pe.wait_ge(w_in, 7 * 16)
            for g in range(8):
                mm = pe.transpose(m.psum[:, g // 4, (g % 4) * NW:(g % 4 + 1) * NW], wg_rows[0:NW, g // 4, :, g % 4],
                                  m.ident[0:NW, 0:NW])
            mm.then_inc(turned, 1)
            pe.wait_ge(wg_kept, 1)
            pe.wait_ge(spread_made, 1)
            for o in range(QB):
                for e in range(2):
                    mm = pe.matmul(m.psum[:, 2 * o + e, 0:4 * NW], spread_o[:, o, :], wg[:, 4 * e:4 * e + 4, :],
                                   start=True, stop=True)
                mm.then_inc(spread, 1)
            pe.wait_ge(folded, 1)
            for c in range(IC):
                for q, (w, src) in enumerate(((g_xc, xc), (g_xm, xm))):
                    mm = pe.matmul(m.psum[0:8, 0, 0:T], w[:, c, :], src[:, c, :], start=(c == 0 and q == 0),
                                   stop=(c == IC - 1 and q == 1))
            mm.then_inc(gates_done, 1)
            pe.wait_ge(gates_kept, 1)
            pe.matmul(m.psum[0:4, 1, 0:T], m.ident[0:8, 4:8], gates8[0:8, :], start=True, stop=True)

        @block.scalar
        def _(act):
            act.wait_ge(turned, 1)
            for e in range(2):
                act.copy(wg[:, 4 * e:4 * e + 4, :], m.psum[:, e, 0:4 * NW].rearrange("p (g n) -> p g n", g=4))
            act.drain().then_inc(wg_kept, 1)
            act.wait_ge(gates_done, 1)
            act.copy(gates8[0:8, :], m.psum[0:8, 0, 0:T]).then_inc(gates_kept, 1)

        @block.vector
        def _(dve):
            dve.tensor_reduce(row_of.unsqueeze(2), m.ident[:, :].rearrange("p (b o) -> p o b", o=QB), AX_X, ALU.add)
            dve.drain()
            dve.wait_ge(blk_done, 1)
            for o in range(QB):
                dve.tensor_scalar(spread_o[:, o, :].rearrange("p (b i) -> p b i", i=QB),
                                  blk.unsqueeze(2).to_broadcast([P, 32, QB]), row_of[:, o:o + 1], None, ALU.mult)
            dve.drain().then_inc(spread_made, 1)
            for o in range(QB):
                dve.wait_ge(spread, o + 1)
                dst = total if o == 0 else term
                for i, w in enumerate((wq, wk, wv)):
                    for e in range(2):
                        rows = m.psum[:, 2 * o + e, 0:4 * NW].rearrange("p (g n) -> p g n", g=4)
                        dve.tensor_tensor(dst[:, i, 4 * e:4 * e + 4, :], rows[:, :, i * IC:(i + 1) * IC],
                                          w[:, :, o].unsqueeze(1).to_broadcast([P, 4, IC]), ALU.mult)
                dve.drain()
                if o:
                    dve.tensor_tensor(total, total, term, ALU.add)
                    dve.drain()
            dve.tensor_tensor(g_xc.rearrange("p c g -> p g c"), total[:, 0], total[:, 1], ALU.add)
            dve.tensor_copy(g_xm.rearrange("p c g -> p g c"), total[:, 2])
            dve.drain().then_inc(folded, 1)

    ig, lf, big, keep, cut, ws, wp = (m.rows[:, T * i:T * (i + 1)] for i in range(7))
    m0 = view(m.small, 464, B)
    wc_row = view(m.small, 472, B)
    ml = view(m.small, 480, 9)
    wcol = view(m.small, 496, H, B)

    def seqs(v):
        return v[:, T_P:T].rearrange("p (b t) -> p b t", b=B)

    with signal(m, "turned") as turned, signal(m, "e1") as e1, signal(m, "e2") as e2, \
            signal(m, "m_in") as m_in, signal(m, "m_out") as m_out, signal(m, "u_done") as u_done, \
            signal(m, "ends") as ends, signal(m, "m_done") as m_done, nc.Block() as block:
        @block.sync
        def _(sp):
            with nc.allow_non_contiguous_dma(reason="32 values"):
                sp.dma_start(m0[0:H, :], I["state_mlstm_m"][0].rearrange("b h -> h b")).then_inc(m_in, 16)
                sp.wait_ge(m_done, 1)
                sp.dma_start(O["p_m_m"].rearrange("a b h -> h (a b)"), ml[0:H, 0:1]).then_inc(m_out, 16)
                sp.dma_start(O["s_m_m"][0].rearrange("b h -> h b"), ml[0:H, 1:9]).then_inc(m_out, 16)
            sp.wait_ge(m_out, 32)

        @block.gpsimd
        def _(pool):
            pool.memset(keep, 1.0)
            pool.memset(cut, 0.0)
            pool.drain()
            for v, x in ((keep, 0.0), (cut, NEG)):
                pool.memset(v[:, 0:1], x)
                pool.memset(v[:, T_P:T:T_S], x)
            pool.drain().then_inc(ends, 1)

        @block.tensor
        def _(pe):
            pe.wait_ge(u_done, 1)
            for j, (t0, n) in enumerate(TILES):
                mm = pe.transpose(m.psum[0:n, 2, 4 * j:4 * j + 4], ig[:, t0:t0 + n], m.ident[0:4, 0:4])
            mm.then_inc(turned, 1)
            pe.wait_ge(u_done, 2)
            for h in range(H):
                mm = pe.matmul(m.psum[:, 3, B * h:B * h + B], m.ident[0:H, h:h + 1].to_broadcast([H, P]), wc_row[0:H, :],
                               start=(h == 0), stop=(h == H - 1), skip_group_check=True)
            mm.then_inc(turned, 1)

        @block.scalar
        def _(act):
            act.wait_ge(e1, 1)
            act.activation(ws, ws, ACT.Exp, scale=-1.0)
            act.drain()
            act.activation(ws, ws, ACT.Ln, bias=1.0).then_inc(e1, 1)
            act.wait_ge(e2, 1)
            act.activation(ws, ws, ACT.Exp)
            act.activation(wp, wp, ACT.Exp)
            act.activation(wc_row[0:H, :], wc_row[0:H, :], ACT.Exp)
            act.activation(lf, lf, ACT.Exp, scale=-1.0).then_inc(e2, 1)

        @block.vector
        def _(dve):
            dve.wait_ge(m_in, 16)
            dve.wait_ge(ends, 1)
            dve.tensor_scalar(ig, m.psum[0:4, 0, 0:T], bg[0:4, :], None, ALU.add)
            dve.tensor_scalar(lf, m.psum[0:4, 1, 0:T], bgf[0:4, :], None, ALU.add)
            dve.drain()
            dve.scalar_tensor_tensor(ws, lf, -1.0, lf, ALU.mult, ALU.max)
            dve.drain().then_inc(e1, 1)
            dve.wait_ge(e1, 2)
            dve.scalar_tensor_tensor(lf, lf, 0.0, ws, ALU.min, ALU.subtract)
            dve.drain()
            dve.tensor_tensor_scan(big, keep, lf, 0.0, ALU.mult, ALU.add)
            dve.drain()
            dve.tensor_tensor(ig, ig, big, ALU.subtract)
            dve.drain().then_inc(u_done, 1)
            dve.tensor_copy(wp, ig)
            dve.drain()
            dve.tensor_scalar(wp[:, 0:1], wp[:, 0:1], 0.0, None, ALU.max)
            dve.tensor_tensor(seqs(wp)[:, :, 0:1], seqs(wp)[:, :, 0:1], m0[0:H, :].unsqueeze(2), ALU.max)
            dve.drain()
            dve.tensor_tensor_scan(lf, cut, wp, 0.0, ALU.add, ALU.max)
            dve.drain()
            dve.tensor_copy(keep, lf)
            ends_m = lf[:, T_P + T_S - 1:T:T_S]
            dve.tensor_tensor(ws[:, 0:T_P], ig[:, 0:T_P], lf[:, T_P - 1:T_P].to_broadcast([4, T_P]), ALU.subtract)
            dve.tensor_tensor(seqs(ws), seqs(ig), ends_m.unsqueeze(2).to_broadcast([4, B, T_S]), ALU.subtract)
            dve.tensor_scalar(wp[:, 0:T_P], lf[:, 0:T_P], -1.0, None, ALU.mult)
            dve.tensor_tensor(seqs(wp), m0[0:H, :].unsqueeze(2).to_broadcast([4, B, T_S]), seqs(lf), ALU.subtract)
            dve.tensor_tensor(wc_row[0:H, :], m0[0:H, :], ends_m, ALU.subtract)
            dve.drain()
            dve.tensor_tensor(lf, lf, big, ALU.add)
            dve.drain()
            dve.tensor_copy(ml[0:H, 0:1], lf[:, T_P - 1:T_P])
            dve.tensor_copy(ml[0:H, 1:9], lf[:, T_P + T_S - 1:T:T_S])
            dve.drain().then_inc(m_done, 1)
            dve.drain().then_inc(e2, 1)
            dve.wait_ge(e2, 2)
            dve.drain().then_inc(u_done, 1)
            dve.wait_ge(turned, 2)
            for j, (t0, n) in enumerate(TILES):
                dve.tensor_copy(u_col[0:n, j, :], m.psum[0:n, 2, 4 * j:4 * j + 4])
            dve.tensor_copy(wcol.rearrange("p h b -> p (h b)"), m.psum[:, 3, 0:H * B])
    big_m = keep
    em = lf


    n0 = view(m.small, 528, B, H, HC)
    n_new = view(m.small, 784, 1 + B, H, HC)
    n_rows = view(m.arena, 20480, 2, P)
    rden = view(m.arena, 20480 + 2 * P, T)
    with signal(m, "n_in") as n_in, signal(m, "turned") as turned, nc.Block() as block:
        @block.sync
        def _(sp):
            src = I["state_mlstm_n"].rearrange("a b h (c p) -> (a b h c) p", p=P)
            for i in range(2):
                sp.dma_start(n_rows[:, i, :], src[i * P:(i + 1) * P, :]).then_inc(n_in, 16)

        @block.tensor
        def _(pe):
            pe.wait_ge(n_in, 32)
            for i in range(2):
                mm = pe.transpose(m.psum[:, 0, i * P:(i + 1) * P], n_rows[:, i, :], m.ident[:, :])
            mm.then_inc(turned, 1)

        @block.vector
        def _(dve):
            dve.wait_ge(turned, 1)
            dve.tensor_copy(n0.rearrange("p b h c -> p (b h c)"), m.psum[:, 0, 0:2 * P])

    c_slot = view(m.ring, 8192, HC, DH)
    s_t = [view(m.ring, 7424, T_P), view(m.ring, 7424 + T_P, P), view(m.ring, 7424 + T_P + P, 64)]
    vt = view(m.xn, 0, 3, DH)
    kt = view(m.xn, 3 * DH, 2, DH)
    k72, v72 = ([m.xn[:, at + i * DH // 2:at + (i + 1) * DH // 2].bitcast(BF16) for i in range(2)]
                for at in (3 * DH, 4 * DH))
    q_one = [view(m.xn, 512 * i, HC, 64) for i in range(2)]
    columns = view(m.xn, 1024, B, 64)
    num_tok = view(m.xn, 0, DH)
    rep_words = HC * B * ROWS72 // 2
    krep = m.ring[:, 5120:5120 + rep_words].bitcast(BF16).rearrange("p (c b r) -> p c b r", c=HC, b=B)
    vrep = m.ring[:, 2560:2560 + rep_words].bitcast(BF16).rearrange("p (c b r) -> p c b r", c=HC, b=B)
    qn = view(m.ring, 8192, HC, 64)
    rest = view(m.ring, 8704, HC, 64)
    p16 = m.ring[:, 9216:9216 + HC * 32].bitcast(BF16).rearrange("p (c t) -> p c t", c=HC)
    wn = view(m.ring, 9728, HC, B)
    for h in range(H):
        xm_h, xc_h = xm[:, h * HC:(h + 1) * HC], xc[:, h * HC:(h + 1) * HC]
        with signal(m, "expanded") as expanded, signal(m, "prod") as prod, signal(m, "kept") as kept, \
                signal(m, "v_kept") as v_kept, nc.Block() as block:
            @block.vector
            def _(dve):
                expand(dve, h).then_inc(expanded, 1)
                for c in range(HC):
                    dve.wait_ge(prod, 3 * c + 3)
                    dve.tensor_copy(xm_h[:, c, :], m.psum[:, 3 * (c % 2) + 2, 0:T]).then_inc(v_kept, 1)

            @block.scalar
            def _(act):
                for c in range(HC):
                    for i, dst in enumerate((q_f, k_f)):
                        act.wait_ge(prod, 3 * c + i + 1)
                        act.activation(dst[:, c, :], m.psum[:, 3 * (c % 2) + i, 0:T], ACT.Copy,
                                       scale=1.0 if i == 0 else DH ** -0.5).then_inc(kept, 1)

            @block.tensor
            def _(pe):
                pe.wait_ge(expanded, 1)
                for c in range(HC):
                    if c >= 2:
                        pe.wait_ge(kept, 2 * (c - 1))
                        pe.wait_ge(v_kept, c - 1)
                    for i, src in enumerate((xc_h, xc_h, xm_h)):
                        pe.matmul(m.psum[:, 3 * (c % 2) + i, 0:T], bd[:, i, c, :], src[:, c, :], start=True,
                                  stop=True).then_inc(prod, 1)
        with signal(m, "scored") as scored, signal(m, "spread") as spread, signal(m, "arg") as arg, \
                signal(m, "weight") as weight, signal(m, "st_done") as st_done, signal(m, "den") as den, \
                nc.Block() as block:
            @block.tensor
            def _(pe):
                for i, row in enumerate((big_m, em, ws, wp)):
                    mm = pe.matmul(m.psum[:, 3 + i, 0:T], m.ident[0:H, h:h + 1].to_broadcast([H, P]), row, start=True,
                                   stop=True)
                mm.then_inc(spread, 1)
                for a in range(2):
                    for c in range(HC):
                        pe.matmul(m.psum[:, a, 0:T_P - a * P], k_f[:, c, a * P:(a + 1) * P], q_f[:, c, a * P:T_P],
                                  start=(c == 0), stop=(c == HC - 1))
                for c in range(HC):
                    mm = pe.matmul(m.psum[0:64, 2, 0:64], k_f[:, c, T_P:T], q_f[:, c, T_P:T], start=(c == 0),
                                   stop=(c == HC - 1))
                mm.then_inc(scored, 1)
                pe.wait_ge(st_done, 1)
                pe.matmul(m.psum[:, 7, 0:T_P], m.ones[:, :], s_t[0], start=True, stop=False, skip_group_check=True)
                pe.matmul(m.psum[:, 7, P:T_P], m.ones[:, :], s_t[1], start=False, stop=False, skip_group_check=True)
                pe.matmul(m.psum[:, 7, T_P:T], m.ones[0:64, :], s_t[2][0:64, :], start=False, stop=False,
                          skip_group_check=True)
                for c in range(HC):
                    mm = pe.matmul(m.psum[:, 7, T_P:T], m.ones[:, :], qn[:, c, :], start=False, stop=(c == HC - 1),
                                   skip_group_check=True)
                mm.then_inc(den, 1)

            @block.scalar
            def _(act):
                for a in range(3):
                    n = TILES[a][1]
                    act.wait_ge(arg, a + 1)
                    act.activation(s_t[a][0:n, :], s_t[a][0:n, :], ACT.Exp, scale=-1.0).then_inc(weight, 1)

            @block.vector
            def _(dve):
                dve.wait_ge(spread, 1)
                for a, (t0, n) in enumerate(TILES):
                    end = T_P if a < 2 else T
                    dve.tensor_scalar(s_t[a][0:n, :], m.psum[0:n, 3, t0:end], u_col[0:n, a, h:h + 1], 0.0, ALU.subtract,
                                      ALU.max).then_inc(arg, 1)
                dve.wait_ge(scored, 1)
                for a, (t0, n) in enumerate(TILES):
                    dve.wait_ge(weight, a + 1)
                    dve.tensor_tensor(s_t[a][0:n, :], s_t[a][0:n, :], m.psum[0:n, a, 0:s_t[a].shape[1]], ALU.mult)
                dve.drain()
                for a, mask in enumerate((m.causal, m.causal, m.causal8)):
                    n = TILES[a][1]
                    dve.tensor_tensor(s_t[a][0:n, 0:n], s_t[a][0:n, 0:n], mask[0:n, 0:n], ALU.mult)
                q_s = q_f[:, :, T_P:T]
                dve.tensor_tensor(q_s, q_s, m.psum[:, 6, T_P:T].unsqueeze(1).to_broadcast([P, HC, 64]), ALU.mult)
                dve.tensor_tensor(k_f, k_f, m.psum[:, 5, 0:T].unsqueeze(1).to_broadcast([P, HC, T]), ALU.mult)
                dve.drain()
                for b in range(B):
                    dve.tensor_tensor(qn[:, :, b * T_S:(b + 1) * T_S], q_s[:, :, b * T_S:(b + 1) * T_S],
                                      n0[:, b, h, :].unsqueeze(2).to_broadcast([P, HC, T_S]), ALU.mult)
                dve.drain().then_inc(st_done, 1)
                dve.wait_ge(den, 1)
                dve.tensor_copy(rden, m.psum[:, 7, 0:T])
                dve.drain()
                dve.scalar_tensor_tensor(rden, rden, -1.0, rden, ALU.mult, ALU.max)
                dve.drain()
                dve.tensor_tensor(rden, rden, m.psum[:, 4, 0:T], ALU.max)
                dve.drain()
                dve.reciprocal(rden, rden)
        with signal(m, "turned") as turned, signal(m, "copied") as copied, nc.Block() as block:
            @block.tensor
            def _(pe):
                for j, (t0, n) in enumerate(TILES):
                    for c in range(HC):
                        mm = pe.transpose(m.psum[0:n, 2 * j + c // 4, (c % 4) * P:(c % 4 + 1) * P], xm_h[:, c, t0:t0 + n],
                                          m.ident[:, :])
                    mm.then_inc(turned, 1)
                for j, (t0, n) in enumerate(TILES[0:2]):
                    if j:
                        pe.wait_ge(copied, 1)
                    for c in range(HC):
                        bank = (6, 0)[j] + c // 4
                        mm = pe.transpose(m.psum[0:n, bank, (c % 4) * P:(c % 4 + 1) * P], k_f[:, c, t0:t0 + n],
                                          m.ident[:, :])
                    mm.then_inc(turned, 1)

            @block.scalar
            def _(act):
                for j, (t0, n) in enumerate(TILES):
                    act.wait_ge(turned, j + 1)
                    act.copy(vt[0:n, j, :], m.psum[0:n, 2 * j:2 * j + 2, :].rearrange("p a b -> p (a b)")).then_inc(copied, 1)
                for j in range(2):
                    bank = (6, 0)[j]
                    act.wait_ge(turned, 4 + j)
                    act.copy(kt[:, j, :], m.psum[:, bank:bank + 2, :].rearrange("p a b -> p (a b)")).then_inc(copied, 1)

            @block.vector
            def _(dve):
                dve.tensor_reduce(n_new[:, 0, h, :].unsqueeze(2), k_f[:, :, 0:T_P], AX_X, ALU.add)
                for b in range(B):
                    dve.tensor_reduce(n_new[:, 1 + b, h, :].unsqueeze(2), k_f[:, :, T_P + b * T_S:T_P + (b + 1) * T_S],
                                      AX_X, ALU.add)
                    dve.tensor_scalar(wn[:, :, b], n0[:, b, h, :], wcol[:, h, b:b + 1], None, ALU.mult)
                dve.drain()
                dve.tensor_tensor(n_new[:, 1:1 + B, h, :], n_new[:, 1:1 + B, h, :], wn.rearrange("p c b -> p b c"), ALU.add)

                def split(source, rep, outer):
                    for i in range(SPL):
                        dve.tensor_copy(p16, source if i == 0 else rest)
                        dve.drain()
                        if i < SPL - 1:
                            dve.tensor_tensor(rest, source if i == 0 else rest, p16, ALU.subtract)
                        for j in range(SPL):
                            r = (i * SPL + j if outer else j * SPL + i) * T_S
                            dve.tensor_copy(rep[:, :, :, r:r + T_S], p16.rearrange("p c (b t) -> p c b t", b=B))
                        dve.drain()
                split(k_f[:, :, T_P:T], krep, True)
                dve.wait_ge(turned, 5)
                split(xm_h[:, :, T_P:T], vrep, False)
        with signal(m, "num") as num, signal(m, "c_done") as c_done, signal(m, "c_kept") as c_kept, \
                signal(m, "stored") as stored, nc.Block() as block:
            @block.tensor
            def _(pe):
                for c in range(HC):
                    ps = m.psum[:, c // 2, (c % 2) * T_P:(c % 2 + 1) * T_P]
                    pe.matmul(ps, vt[:, 0, c * P:(c + 1) * P], s_t[0], start=True, stop=False, skip_group_check=True)
                    pe.matmul(ps[:, P:T_P], vt[:, 1, c * P:(c + 1) * P], s_t[1], start=False, stop=True,
                              skip_group_check=True).then_inc(num, 1)
                for c in range(HC):
                    for e in range(2):
                        i = 2 * c + e
                        if i >= 4:
                            pe.wait_ge(c_kept, i - 3)
                        for a in range(2):
                            mm = pe.matmul(m.psum[:, 4 + i % 4, :], kt[:, a, c * P:(c + 1) * P],
                                           vt[:, a, e * 512:(e + 1) * 512], start=(a == 0), stop=(a == 1))
                        mm.then_inc(c_done, 1)

            @block.vector
            def _(dve):
                for c in range(HC):
                    if c % 2 == 0:
                        dve.wait_ge(num, c + 2)
                    dve.tensor_tensor(xm_h[:, c, 0:T_P], m.psum[:, c // 2, (c % 2) * T_P:(c % 2 + 1) * T_P],
                                      rden[:, 0:T_P], ALU.mult)

            @block.scalar
            def _(act):
                for i in range(2 * HC):
                    act.wait_ge(c_done, i + 1)
                    act.copy(c_slot[:, i // 2, (i % 2) * 512:(i % 2 + 1) * 512], m.psum[:, 4 + i % 4, :]).then_inc(c_kept, 1)

            @block.sync
            def _(sp):
                for c in range(HC):
                    sp.wait_ge(c_kept, 2 * c + 2)
                    sp.dma_start(O["p_m_C"][0, 0, h, c * P:(c + 1) * P, :], c_slot[:, c, :]).then_inc(stored, 16)
                sp.wait_ge(stored, 16 * HC)
        c_in = I["state_mlstm_C"][0].rearrange("b h (c p) e -> b h c p e", p=P)
        c_out = O["s_m_C"][0].rearrange("b h (c p) e -> b h c p e", p=P)
        LAG = 3
        with ExitStack() as ctx:
            landed = [ctx.enter_context(signal(m, f"state_landed{c}")) for c in range(HC)]
            stored = [ctx.enter_context(signal(m, f"state_stored{c}")) for c in range(HC)]
            turned = ctx.enter_context(signal(m, "turned"))
            k_kept = ctx.enter_context(signal(m, "k_kept"))
            v_kept = ctx.enter_context(signal(m, "v_kept"))
            queries = ctx.enter_context(signal(m, "queries"))
            read = ctx.enter_context(signal(m, "read"))
            outer = ctx.enter_context(signal(m, "outer"))
            updated = ctx.enter_context(signal(m, "updated"))
            num = ctx.enter_context(signal(m, "num"))
            num_kept = ctx.enter_context(signal(m, "num_kept"))
            block = ctx.enter_context(nc.Block())

            def one(v, i):
                return v[i] if isinstance(i, int) else v[bass.ds(i, 1)].squeeze(0)

            def at(i, odd, each, more=0):
                return i * (2 * each) + (odd * each + more)

            @block.sync
            def _(sp):
                def load(b, c):
                    sp.dma_start(c_slot[:, c, :], one(c_in, b)[h, c]).then_inc(landed[c], 16)

                def sequence(b, more):
                    for c in range(HC):
                        sp.wait_ge(updated, b * (2 * HC) + (2 * c + 4))
                        sp.dma_start(one(c_out, b)[h, c], c_slot[:, c, :]).then_inc(stored[c], 16)
                        if c < LAG:
                            if not (isinstance(b, int) and b == 0):
                                sp.wait_ge(stored[c - LAG + HC], b * 16)
                            load(b, c - LAG + HC)
                        elif more:
                            sp.wait_ge(stored[c - LAG], b * 16 + 16)
                            load(b + 1, c - LAG)

                for c in range(HC - LAG):
                    load(0, c)
                sequence(0, True)
                with sp.Fori(1, B - 1) as b:
                    sequence(b, True)
                sequence(B - 1, False)
                for c in range(HC):
                    sp.wait_ge(stored[c], 16 * B)

            @block.gpsimd
            def _(pool):
                def one_sequence(i, odd):
                    mask = columns[:, bass.ds(at(i, odd, 1), 1), :].to_broadcast([P, HC, 64])
                    pool.tensor_tensor(q_one[odd], q_f[:, :, T_P:T], mask, ALU.mult).then_inc(queries, 1)

                pool.memset(columns, 1.0)
                pool.drain()
                pool.affine_select(columns, columns, [[-T_S, B], [1, 64]], ALU.is_ge, 0.0, base=0, channel_multiplier=0)
                pool.drain()
                pool.affine_select(columns, columns, [[T_S, B], [-1, 64]], ALU.is_ge, 0.0, base=T_S - 1,
                                   channel_multiplier=0)
                pool.drain()
                for odd in range(2):
                    one_sequence(0, odd)
                with pool.Fori(1, B // 2) as i:
                    for odd in range(2):
                        pool.wait_ge(read, at(i, odd, 1, -1))
                        one_sequence(i, odd)

            @block.tensor
            def _(pe):
                def turn(i, odd):
                    for j, rep in enumerate((krep, vrep)):
                        for c in range(HC):
                            mm = pe.matmul(m.psum[0:ROWS72, 1 + 2 * j + c // 4, (c % 4) * P:(c % 4 + 1) * P],
                                           rep[:, c, bass.ds(at(i, odd, 1), 1), :].squeeze(1), m.identb[:, :],
                                           start=True, stop=True)
                        mm.then_inc(turned, 1)

                def sequence(i, odd, last=False):
                    pe.wait_ge(queries, at(i, odd, 1, 1))
                    for c in range(HC):
                        pe.wait_ge(landed[c], at(i, odd, 16, 16))
                        for e in range(2):
                            mm = pe.matmul(m.psum[0:64, 7 * e, :], q_one[odd][:, c, :],
                                           c_slot[:, c, e * 512:(e + 1) * 512], start=False, stop=last and c == HC - 1,
                                           skip_group_check=True)
                        if c == HC - 1:
                            mm.then_inc(read, 1)
                        if c == 0:
                            pe.wait_ge(k_kept, at(i, odd, 1, 1))
                            pe.wait_ge(v_kept, at(i, odd, 1, 1))
                        for e in range(2):
                            pe.wait_ge(updated, at(i, odd, 2 * HC, 2 * c + e + 1))
                            pe.matmul(m.psum[:, 5 + e, :], k72[odd][0:ROWS72, c * P:(c + 1) * P],
                                      v72[odd][0:ROWS72, e * 512:(e + 1) * 512], start=True, stop=True).then_inc(outer, 1)
                        if c == HC // 2 and not last:
                            turn(i if odd == 0 else i + 1, 1 - odd)

                for e in range(2):
                    pe.matmul(m.psum[0:64, 7 * e, :], s_t[2][0:64, :], vt[0:64, 2, e * 512:(e + 1) * 512], start=True,
                              stop=False, skip_group_check=True)
                turn(0, 0)
                with pe.Fori(0, B // 2 - 1) as i:
                    sequence(i, 0)
                    sequence(i, 1)
                sequence(B // 2 - 1, 0)
                sequence(B // 2 - 1, 1, last=True)
                pe.drain().then_inc(num, 1)
                pe.wait_ge(num_kept, 2)
                for c in range(HC):
                    mm = pe.transpose(m.psum[:, 0, c * 64:(c + 1) * 64], num_tok[0:64, c * P:(c + 1) * P],
                                      m.ident[0:64, 0:64])
                mm.then_inc(num, 1)

            @block.scalar
            def _(act):
                with act.Fori(0, B // 2) as i:
                    for odd in range(2):
                        act.wait_ge(turned, at(i, odd, 2, 1))
                        act.copy(k72[odd][0:ROWS72, :],
                                 m.psum[0:ROWS72, 1:3, :].rearrange("p a b -> p (a b)")).then_inc(k_kept, 1)
                        act.wait_ge(turned, at(i, odd, 2, 2))
                        act.copy(v72[odd][0:ROWS72, :],
                                 m.psum[0:ROWS72, 3:5, :].rearrange("p a b -> p (a b)")).then_inc(v_kept, 1)
                act.wait_ge(num, 1)
                act.copy(num_tok[0:64, 0:512], m.psum[0:64, 0, :]).then_inc(num_kept, 1)

            @block.vector
            def _(dve):
                dve.sem_inc(updated, 2)
                with dve.Fori(0, B) as b:
                    for c in range(HC):
                        for e in range(2):
                            dve.wait_ge(outer, b * (2 * HC) + (2 * c + e + 1))
                            part_c = c_slot[:, c, e * 512:(e + 1) * 512]
                            dve.scalar_tensor_tensor(part_c, part_c, wcol[:, h, bass.ds(b, 1)], m.psum[:, 5 + e, :],
                                                     ALU.mult, ALU.add).then_inc(updated, 1)
                dve.wait_ge(num, 1)
                dve.tensor_copy(num_tok[0:64, 512:1024], m.psum[0:64, 7, :]).then_inc(num_kept, 1)
                dve.wait_ge(num, 2)
                dve.tensor_tensor(xm_h[:, :, T_P:T], m.psum[:, 0, :].rearrange("p (c t) -> p c t", c=HC),
                                  rden[:, T_P:T].unsqueeze(1).to_broadcast([P, HC, 64]), ALU.mult)
        sq = view(m.ring, 0, HC, T)
        mean = view(m.ring, 2560, T)
        with signal(m, "summed") as summed, signal(m, "centred") as centred, signal(m, "sqd") as sqd, \
                signal(m, "root") as root, nc.Block() as block:
            @block.tensor
            def _(pe):
                for c in range(HC):
                    mm = pe.matmul(m.psum[:, 0, 0:T], m.ones[:, :], xm_h[:, c, :], start=(c == 0), stop=(c == HC - 1))
                mm.then_inc(summed, 1)
                for c in range(HC):
                    pe.wait_ge(sqd, c + 1)
                    mm = pe.matmul(m.psum[:, 1, 0:T], m.ones[:, :], sq[:, c, :], start=(c == 0), stop=(c == HC - 1))
                mm.then_inc(summed, 1)

            @block.scalar
            def _(act):
                for c in range(HC):
                    act.wait_ge(centred, c + 1)
                    act.activation(sq[:, c, :], xm_h[:, c, :], ACT.Square).then_inc(sqd, 1)
                act.wait_ge(root, 1)
                act.activation(mean, mean, ACT.Sqrt).then_inc(root, 1)

            @block.vector
            def _(dve):
                dve.wait_ge(summed, 1)
                dve.tensor_scalar(mean, m.psum[:, 0, 0:T], 1.0 / DH, None, ALU.mult)
                dve.drain()
                for c in range(HC):
                    dve.tensor_tensor(xm_h[:, c, :], xm_h[:, c, :], mean, ALU.subtract).then_inc(centred, 1)
                dve.wait_ge(summed, 2)
                dve.drain()
                dve.tensor_scalar(mean, m.psum[:, 1, 0:T], 1.0 / DH, EPS, ALU.mult, ALU.add)
                dve.drain().then_inc(root, 1)
                dve.wait_ge(root, 2)
                dve.reciprocal(mean, mean)
                dve.drain()
                for c in range(HC):
                    dve.scalar_tensor_tensor(xm_h[:, c, :], xm_h[:, c, :], param(m, "l1_norm_g", h * HC + c), mean,
                                             ALU.mult, ALU.mult)
                dve.drain()
                for c in range(HC):
                    dve.scalar_tensor_tensor(xm_h[:, c, :], xc_h[:, c, :], param(m, "l1_skip", h * HC + c),
                                             xm_h[:, c, :], ALU.mult, ALU.add)
    store_columns(nc, m, n_new.rearrange("p b h c -> p (b h c)"), 9 * H * HC, [
        (0, H * HC, O["p_m_n"].rearrange("a b h (c p) -> (a b h c) p", p=P)),
        (H * HC, 9 * H * HC, O["s_m_n"].rearrange("a b h (c p) -> (a b h c) p", p=P))])

    rmsnorm(nc, m, "norm_mix_g", DC, m.XN)

    def gate_with_z(dve, e, n):
        y = xm[:, bass.ds(n, 1), :].squeeze(1)
        return dve.tensor_tensor(y, y, e, ALU.mult)

    linear(nc, m, I["l1_w_up"][0][:, DI:2 * DI], DC, lambda k: m.XN[:, k, :], gate=gate_with_z)
    linear(nc, m, I["l1_w_down"][0], IC, lambda k: xm[:, k, :])


def build(nc, I, O):
    with ExitStack() as ctx:
        m = Mem(nc, ctx)
        proj = view(m.arena, 0, IN0C + 1, T)
        setup(nc, m, I)
        rmsnorm(nc, m, "norm_mix_g", 0, m.XN)
        first_projection(nc, m, I)
        rg_lru(nc, m, I, O)
        gla(nc, m, I, O)
        linear(nc, m, I["l0_w_out"][0], DC, lambda k: proj[:, GA + k if k < 8 else GG + k - 8, :])
        rmsnorm(nc, m, "norm_ffn_g", 0, m.XN)
        moe(nc, m, I, 0)
        rmsnorm(nc, m, "norm_mix_g", DC, m.XN)
        mlstm(nc, m, I, O)
        rmsnorm(nc, m, "norm_ffn_g", DC, m.XN)
        moe(nc, m, I, 1)
        final_norm(nc, m, O)


INS = """x_prompt x_sample state_lru_conv state_lru_h state_gla_S state_mlstm_conv state_mlstm_C state_mlstm_n
state_mlstm_m norm_mix_g norm_ffn_g norm_final_g l0_w_in l0_lru_conv_w l0_lru_conv_b l0_lru_wa l0_lru_ba l0_lru_wx
l0_lru_bx l0_lru_lam l0_gla_wa2 l0_gla_ba2 l0_gla_norm_g l0_w_out l1_w_up l1_conv_w l1_conv_b l1_wq l1_wk l1_wv l1_w_ig
l1_b_ig l1_w_fg l1_b_fg l1_skip l1_norm_g l1_w_down moe_w_rg moe_b_rg moe_w_re moe_b_re moe_w_gate moe_w_up
moe_w_down""".split()
OUTS = [("y_prompt", (1, T_P, D)), ("y_sample", (B, T_S, D))] + [
    (f"{g}_{name}", (1, n) + shape) for g, n in (("p", 1), ("s", B)) for name, shape in (
        ("lru_conv", (CW - 1, W_LRU)), ("lru_h", (W_LRU,)), ("gla_S", (H, DK, DV)), ("m_conv", (CW - 1, DI)),
        ("m_C", (H, DH, DH)), ("m_n", (H, DH)), ("m_m", (H,)))]


def kernel(**inputs):
    import numpy as np
    import concourse.bacc as bacc
    from concourse.bass_utils import run_bass_kernel_spmd

    nc = bacc.Bacc("TRN2", target_bir_lowering=False, num_devices=1)
    arrays, ins, outs = {}, {}, {}
    for name in INS:
        a = np.ascontiguousarray(inputs[name])
        arrays[f"in_{name}"] = a
        ins[name] = nc.dram_tensor(f"in_{name}", a.shape, mybir.dt.from_np(a.dtype), kind="ExternalInput").ap()
    for name, shape in OUTS:
        outs[name] = nc.dram_tensor(f"out_{name}", shape, F32, kind="ExternalOutput").ap()
    build(nc, ins, outs)
    r = run_bass_kernel_spmd(nc, [arrays], core_ids=[0])
    return tuple(r.results[0][f"out_{name}"] for name, _ in OUTS)
```

```python
from contextlib import ExitStack, contextmanager

import concourse.bass as bass
from concourse import mybir

ALU = mybir.AluOpType
ACT = mybir.ActivationFunctionType
AX_X = mybir.AxisListType.X
F32 = mybir.dt.float32
BF16 = mybir.dt.bfloat16

P = 128
D = 2048
T_P = 256
B = 8
T_S = 8
T = T_P + B * T_S
TILES = [(0, 128), (128, 128), (256, 64)]
EPS = 1e-6
CW = 4
DC = D // P
W_LRU = 1024
LC = W_LRU // P
H = 4
DK, DV = 128, 256
IN0 = 5136
IN0C = IN0 // P
RANK = 16
XA, GA, QA, KA, VA, GG, AL = 0, 8, 16, 20, 24, 32, 40
DI = 4096
QB = 4
IC = DI // P
DH = DI // H
HC = DH // P
NE, NG, EG = 16, 4, 4
FE = 256
CONV0 = (IN0C + 1) * T
GC = 32
NCH = T_P // GC
SLOT = 2048
NSLOT = 8
KPS = 4
TPB = 4
SPL = 3
ROWS72 = SPL * SPL * T_S
NEG = -1.0e30

PARAM_TILES = [
    [("norm_mix_g", 2 * DC), ("norm_ffn_g", 2 * DC), ("norm_final_g", DC)],
    [("l0_lru_conv_w", CW * LC), ("l0_lru_conv_b", LC), ("l0_lru_ba", LC), ("l0_lru_bx", LC), ("l0_lru_lam", LC),
     ("l0_gla_ba2", H), ("l0_gla_norm_g", 8)],
    [("state_lru_h", B * LC)],
    [("l1_conv_w", CW * IC)],
    [("l1_conv_b", IC), ("l1_skip", IC), ("l1_norm_g", IC)],
]
PCOL = {}
for _i, _tile in enumerate(PARAM_TILES):
    _at = 0
    for _n, _k in _tile:
        PCOL[_n] = _i * P + _at
        _at += _k


class Signals:

    MOST = 40

    def __init__(self, nc, count=120):
        self.nc = nc
        self.sems = [nc.alloc_semaphore(f"signal{i}") for i in range(count)]
        self.next = 0
        self.held = 0

    def take(self):
        if not self.held and self.next > len(self.sems) - self.MOST:
            numbers = [s.num for s in self.sems]
            with self.nc.Block() as block:
                @block.gpsimd
                def _(pool):
                    pool.sem_clear(range(min(numbers), max(numbers) + 1))
            self.next = 0
        self.next += 1
        self.held += 1
        return self.sems[self.next - 1]


@contextmanager
def signal(m, name):
    yield m.signals.take()
    m.signals.held -= 1


class Mem:

    def __init__(self, nc, ctx):
        self.signals = Signals(nc)

        def sb(name, shape, dt=F32):
            return ctx.enter_context(nc.sbuf_tensor(name, shape, dt))

        self.x = sb("x_resid", [P, DC, T])
        self.xn = sb("x_norm", [P, DC * T])
        self.ring = sb("ring", [P, NSLOT * SLOT])
        self.arena = sb("arena", [P, 21600])
        self.ident = sb("ident", [P, P])
        self.identb = sb("identb", [P, P], BF16)
        self.ones = sb("ones", [P, P])
        self.causal = sb("causal", [P, P])
        self.causal32 = sb("causal32", [P, P])
        self.causal8 = sb("causal8", [64, 64])
        self.prm = sb("params", [P, len(PARAM_TILES) * P])
        self.decay = sb("decay", [P, 2 * LC])
        self.keep32 = sb("keep32", [P, T])
        self.small = sb("small", [P, 1088])
        self.rows = sb("gate_rows", [4, 7 * T])
        self.psum = ctx.enter_context(nc.psum_tensor("psum", [P, 8, 512], F32))
        self.XN = self.xn[:, :].rearrange("p (c t) -> p c t", t=T)


def view(buf, at, *shape):
    n = 1
    for s in shape:
        n *= s
    v = buf[:, at:at + n]
    if len(shape) == 1:
        return v
    names = "abcd"[:len(shape)]
    return v.rearrange(f"p ({' '.join(names)}) -> p {' '.join(names)}", **dict(zip(names[1:], shape[1:])))


def param(m, name, i=0):
    return m.prm[:, PCOL[name] + i:PCOL[name] + i + 1]


def setup(nc, m, I):
    x_tok = view(m.arena, 0, 3, D)
    prow = view(m.arena, 3 * D, len(PARAM_TILES), P)
    with signal(m, "rows_in") as rows_in, signal(m, "consts") as consts, signal(m, "turned") as turned, \
            signal(m, "copied") as copied, nc.Block() as block:
        @block.sync
        def _(sp):
            sp.dma_start(x_tok[:, 0:2, :], I["x_prompt"].rearrange("a (j p) d -> p (a j) d", p=P)).then_inc(rows_in, 16)
            sp.dma_start(x_tok[0:64, 2, :], I["x_sample"].rearrange("b t d -> (b t) d")).then_inc(rows_in, 16)
            for i, tile in enumerate(PARAM_TILES):
                at = 0
                for name, k in tile:
                    src = I[name]
                    letters = " ".join("abcd"[:len(src.shape)])
                    src = src.rearrange(f"{letters} -> ({letters})") if len(src.shape) > 1 else src
                    sp.dma_start(prow[at:at + k, i, :], src.rearrange("(k p) -> k p", p=P)).then_inc(rows_in, 16)
                    at += k

        @block.gpsimd
        def _(pool):
            pool.memset(m.ones[:, :], 1.0)
            pool.memset(m.causal32[:, :], 1.0)
            pool.drain()
            pool.affine_select(m.ident[:, :], m.ones[:, :], [[1, P]], ALU.is_equal, 0.0, base=0, channel_multiplier=-1)
            pool.affine_select(m.causal[:, :], m.ones[:, :], [[1, P]], ALU.is_ge, 0.0, base=0, channel_multiplier=-1)
            pool.drain()
            pool.affine_select(m.causal32[:, :].rearrange("p (a b) -> p a b", b=GC),
                               m.causal[:, :].rearrange("p (a b) -> p a b", b=GC),
                               [[-GC, P // GC], [0, GC]], ALU.is_ge, 0.0, base=0, channel_multiplier=1)
            pool.affine_select(m.causal8[:, :].rearrange("p (a b) -> p a b", b=T_S),
                               m.causal[0:64, 0:64].rearrange("p (a b) -> p a b", b=T_S),
                               [[-T_S, B], [0, T_S]], ALU.is_ge, 0.0, base=0, channel_multiplier=1)
            pool.memset(m.keep32[:, :], 1.0)
            pool.drain()
            pool.memset(m.keep32[:, 0:T_P:GC], 0.0)
            pool.memset(m.keep32[:, T_P:T:T_S], 0.0)
            pool.tensor_copy(m.identb[:, :], m.ident[:, :])
            pool.drain().then_inc(consts, 1)

        @block.tensor
        def _(pe):
            pe.wait_ge(consts, 1)
            pe.wait_ge(rows_in, 16 * (2 + sum(len(t) for t in PARAM_TILES)))
            for c in range(DC):
                if c >= 8:
                    pe.wait_ge(copied, c - 7)
                for j, (t0, n) in enumerate(TILES):
                    last = pe.transpose(m.psum[:, c % 8, t0:t0 + n], x_tok[0:n, j, c * P:(c + 1) * P],
                                        m.ident[0:n, 0:n])
                last.then_inc(turned, 1)
            for i, tile in enumerate(PARAM_TILES):
                k = sum(n for _, n in tile)
                pe.wait_ge(copied, DC - 8 + i + 1)
                pe.transpose(m.psum[:, i, 0:k], prow[0:k, i, :], m.ident[0:k, 0:k]).then_inc(turned, 1)

        @block.scalar
        def _(act):
            for c in range(DC):
                act.wait_ge(turned, c + 1)
                act.copy(m.x[:, c, :], m.psum[:, c % 8, 0:T]).then_inc(copied, 1)
            for i, tile in enumerate(PARAM_TILES):
                k = sum(n for _, n in tile)
                act.wait_ge(turned, DC + i + 1)
                act.copy(m.prm[:, i * P:i * P + k], m.psum[:, i, 0:k]).then_inc(copied, 1)


class Norm:

    def __init__(self, m, ctx, gain, at, out):
        self.m, self.gain, self.at, self.out = m, gain, at, out
        self.sq = view(m.arena, 20480, 2, T)
        self.rstd = view(m.arena, 20480 + 2 * T, T)
        self.squared, self.summed, self.root, self.normed = (
            ctx.enter_context(signal(m, name)) for name in ("squared", "summed", "root", "normed"))

    def scalar(self, act):
        for c in range(DC):
            if c >= 2:
                act.wait_ge(self.summed, c - 1)
            act.activation(self.sq[:, c % 2, :], self.m.x[:, c, :], ACT.Square).then_inc(self.squared, 1)
        act.wait_ge(self.root, 1)
        act.activation(self.rstd, self.rstd, ACT.Sqrt).then_inc(self.root, 1)

    def tensor(self, pe):
        for c in range(DC):
            pe.wait_ge(self.squared, c + 1)
            pe.matmul(self.m.psum[:, 7, 0:T], self.m.ones[:, :], self.sq[:, c % 2, :], start=(c == 0),
                      stop=(c == DC - 1)).then_inc(self.summed, 1)

    def vector(self, dve):
        dve.wait_ge(self.summed, DC)
        dve.tensor_scalar(self.rstd, self.m.psum[:, 7, 0:T], 1.0 / D, EPS, ALU.mult, ALU.add).then_inc(self.root, 1)
        dve.wait_ge(self.root, 2)
        dve.reciprocal(self.rstd, self.rstd)
        dve.drain()
        for c in range(DC):
            dve.scalar_tensor_tensor(self.out[:, c, :], self.m.x[:, c, :], param(self.m, self.gain, self.at + c),
                                     self.rstd, ALU.mult, ALU.mult).then_inc(self.normed, 1)


def linear(nc, m, weights, kc, rhs, copy_to=None, gate=None, conv=None, norm=None):
    kg = kc // KPS
    cbs = NSLOT // kg
    width = TPB * P
    passes = weights.shape[1] // width // cbs
    w = weights.rearrange("(g k p) n -> p g k n", k=KPS, p=P)
    slots = view(m.ring, 0, NSLOT, KPS, 512)
    e = view(m.arena, 20480, 2, T)
    with ExitStack() as ctx:
        def signals(name, n):
            return [ctx.enter_context(signal(m, f"{name}{i}")) for i in range(n)]

        landed = signals("landed", NSLOT)
        used = signals("used", NSLOT)
        tile_done = signals("tile_done", cbs)
        by_act = signals("by_act", cbs)
        by_dve = signals("by_dve", cbs)
        norm = Norm(m, ctx, *norm, m.XN) if norm else None
        block = ctx.enter_context(nc.Block())

        @block.sync
        def _(sp):
            def load(i, s):
                col = (i * cbs + s // kg) * width
                sp.dma_start(slots[:, s, :, :], w[:, s % kg, :, bass.ds(col, width)]).then_inc(landed[s], 16)

            for s in range(NSLOT):
                load(0, s)
            with sp.Fori(1, passes) as i:
                for s in range(NSLOT):
                    if s % kg < kg - 1:
                        sp.wait_ge(used[s], i)
                    else:
                        sp.wait_ge(tile_done[s // kg], i * TPB)
                    load(i, s)

        @block.tensor
        def _(pe):
            if norm:
                norm.tensor(pe)
            with pe.Fori(0, passes) as i:
                for s in range(NSLOT):
                    cb, g = s // kg, s % kg
                    pe.wait_ge(landed[s], i * 16 + 16)
                    if g == 0:
                        if copy_to is not None:
                            pe.wait_ge(by_act[cb], i * TPB + TPB)
                        else:
                            pe.wait_ge(by_dve[cb], i * TPB + TPB)
                    for k in range(KPS):
                        if norm:
                            pe.wait_ge(norm.normed, g * KPS + k + 1)
                        for t in range(TPB):
                            mm = pe.matmul(m.psum[:, cb * TPB + t, 0:T], slots[:, s, k, t * P:(t + 1) * P],
                                           rhs(g * KPS + k), start=(g == 0 and k == 0),
                                           stop=(g == kg - 1 and k == KPS - 1))
                            if g == kg - 1 and k == KPS - 1:
                                mm.then_inc(tile_done[cb], 1)
                    if g < kg - 1:
                        mm.then_inc(used[s], 1)

        @block.scalar
        def _(act):
            if norm:
                norm.scalar(act)
            if copy_to is not None:
                for cb in range(cbs):
                    act.sem_inc(by_act[cb], TPB)
                with act.Fori(0, passes) as i:
                    for cb in range(cbs):
                        for t in range(TPB):
                            act.wait_ge(tile_done[cb], i * TPB + (t + 1))
                            act.copy(copy_to((i * cbs + cb) * TPB + t),
                                     m.psum[:, cb * TPB + t, 0:T]).then_inc(by_act[cb], 1)
                        if conv.silu:
                            act.wait_ge(by_dve[cb], i + 1)
                            x = conv.xout[:, bass.ds((i * cbs + cb) * TPB, TPB), :]
                            act.activation(x, x, ACT.Silu)
            elif gate is not None:
                with act.Fori(0, passes) as i:
                    for cb in range(cbs):
                        for t in range(TPB):
                            act.wait_ge(tile_done[cb], i * TPB + (t + 1))
                            if t >= 2:
                                act.wait_ge(by_dve[cb], i * TPB + (TPB + t - 1))
                            elif cb:
                                act.wait_ge(by_dve[cb - 1], i * TPB + (TPB + t + 3))
                            else:
                                act.wait_ge(by_dve[cbs - 1], i * TPB + TPB)
                            act.activation(e[:, t % 2, :], m.psum[:, cb * TPB + t, 0:T],
                                           ACT.Silu).then_inc(by_act[cb], 1)

        @block.vector
        def _(dve):
            if norm:
                norm.vector(dve)
            if copy_to is not None:
                with dve.Fori(0, conv.passes) as i:
                    for cb in range(cbs):
                        dve.wait_ge(by_act[cb], i * TPB + 2 * TPB)
                        conv.convolve(dve, (i * cbs + cb) * TPB, TPB).then_inc(by_dve[cb], 1)
                return
            for cb in range(cbs):
                dve.sem_inc(by_dve[cb], TPB)
            with dve.Fori(0, passes) as i:
                for cb in range(cbs):
                    for t in range(TPB):
                        n = (i * cbs + cb) * TPB + t
                        ps = m.psum[:, cb * TPB + t, 0:T]
                        if gate is not None:
                            dve.wait_ge(by_act[cb], i * TPB + (t + 1))
                            gate(dve, e[:, t % 2, :], n).then_inc(by_dve[cb], 1)
                        else:
                            dve.wait_ge(tile_done[cb], i * TPB + (t + 1))
                            x = m.x[:, bass.ds(n, 1), :].squeeze(1)
                            dve.tensor_tensor(x, x, ps, ALU.add).then_inc(by_dve[cb], 1)


class Conv:

    def __init__(self, m, xin, xout, chunks, w_name, b_name, passes, silu):
        self.m, self.xin, self.xout, self.chunks, self.passes, self.silu = m, xin, xout, chunks, passes, silu
        self.w, self.b = PCOL[w_name], PCOL[b_name]

    def begin(self, nc, state, rows, tmp):
        m, n, half = self.m, self.chunks, min(self.chunks, 16)
        with signal(m, "state_in") as state_in, signal(m, "turned") as turned, nc.Block() as block:
            @block.sync
            def _(sp):
                sp.dma_start(rows[0:24, :], state.rearrange("a b r d -> (a b r) d")).then_inc(state_in, 16)

            @block.tensor
            def _(pe):
                pe.wait_ge(state_in, 16)
                for c in range(n):
                    mm = pe.transpose(m.psum[:, c // half, (c % half) * 24:(c % half) * 24 + 24],
                                      rows[0:24, c * P:(c + 1) * P], m.ident[0:24, 0:24])
                mm.then_inc(turned, 1)

            @block.vector
            def _(dve):
                new = self.xout[:, :, T_P:T].rearrange("p c (b t) -> p c b t", b=B)
                dve.tensor_copy(self.xout[:, :, T_P:T],
                                m.prm[:, self.b:self.b + n].unsqueeze(2).to_broadcast([P, n, B * T_S]))
                dve.drain()
                dve.wait_ge(turned, 1)
                for j in range(CW - 1):
                    k = CW - 1 - j
                    for g in range(n // half):
                        st = m.psum[:, g, 0:24 * half].rearrange("p (c b r) -> p c b r", b=B, r=3)
                        w = m.prm[:, self.w + j * n + g * half:self.w + j * n + (g + 1) * half]
                        part = tmp[:, g * half:(g + 1) * half, :, 0:k]
                        for r in range(k):
                            dve.tensor_tensor(part[:, :, :, r], st[:, :, :, j + r],
                                              w.unsqueeze(2).to_broadcast([P, half, B]), ALU.mult)
                    dve.drain()
                    dve.tensor_tensor(new[:, :, :, 0:k], new[:, :, :, 0:k], tmp[:, :, :, 0:k], ALU.add)
                    dve.drain()

    def convolve(self, dve, first, count):
        for j in reversed(range(CW)):
            d = CW - 1 - j
            for k in range(count):
                c = first + k
                x, y = (v[:, bass.ds(c, 1), :].squeeze(1) for v in (self.xin, self.xout))
                w = self.m.prm[:, bass.ds(c + (self.w + j * self.chunks), 1)]
                if d == 0:
                    dve.tensor_scalar(y[:, 0:T_P], x[:, 0:T_P], w, self.m.prm[:, bass.ds(c + self.b, 1)], ALU.mult,
                                      ALU.add)
                else:
                    dve.scalar_tensor_tensor(y[:, d:T_P], x[:, 0:T_P - d], w, y[:, d:T_P], ALU.mult, ALU.add)
                xs, ys = (v[:, T_P:T].rearrange("p (b t) -> p b t", b=B) for v in (x, y))
                last = dve.scalar_tensor_tensor(ys[:, :, d:T_S], xs[:, :, 0:T_S - d], w, ys[:, :, d:T_S], ALU.mult,
                                                ALU.add)
            if j:
                dve.drain()
        return dve.drain()


def store_last_rows(nc, m, xin, chunks, cols, prompt_rows, sample_rows):
    with nc.Block() as block:
        @block.vector
        def _(dve):
            for i in range(1 + B):
                end = T_P + i * T_S
                dve.tensor_copy(cols[:, i * 3 * chunks:(i + 1) * 3 * chunks].rearrange("p (r c) -> p c r", r=3),
                                xin[:, :, end - 3:end])
    store_columns(nc, m, cols, 27 * chunks, [
        (0, 3 * chunks, prompt_rows.rearrange("a b r (c p) -> (a b r c) p", p=P)),
        (3 * chunks, 27 * chunks, sample_rows.rearrange("a b r (c p) -> (a b r c) p", p=P))])


def moe(nc, m, I, layer):
    xn = m.XN
    logit = view(m.small, 0, 3, 20)
    rank = view(m.small, 64, 4)
    bias = view(m.small, 72, 20)
    wr = view(m.ring, 12288, DC, 20)
    logit_rows = view(m.ring, 12608, T)
    tmp = [view(m.small, 96 + 16 * i, 3, 4) for i in range(10)]
    mx, s1 = view(m.small, 280, 3, 1), view(m.small, 284, 3, 1)
    m1, pg = view(m.small, 288, 3, 1), view(m.small, 292, 3, 1)
    prod = view(m.small, 300, 3, NG, EG)
    gates = view(m.small, 352, 3, NG, EG)
    gt16 = view(m.ring, 12928, T)
    gb = view(m.arena, 0, NE, T)
    hid = view(m.arena, NE * T, NE, 2, T)
    ex = view(m.arena, 3 * NE * T, 2, T)
    up = view(m.arena, 3 * NE * T + 2 * T, 2, T)
    wg = I["moe_w_gate"][layer].rearrange("e (g k p) f -> e p g k f", k=KPS, p=P)
    wu = I["moe_w_up"][layer].rearrange("e (g k p) f -> e p g k f", k=KPS, p=P)
    wd = I["moe_w_down"][layer].rearrange("e (k p) n -> e p k n", p=P)
    slots = view(m.ring, 0, NSLOT, KPS, 512)
    down = view(m.ring, 4 * SLOT, 2, D)
    with ExitStack() as ctx:
        landed = [ctx.enter_context(signal(m, f"gate_up_landed{s}")) for s in range(4)]
        used = [ctx.enter_context(signal(m, f"gate_up_used{s}")) for s in range(3)]
        down_landed = ctx.enter_context(signal(m, "down_landed"))
        hidden_raw = ctx.enter_context(signal(m, "hidden_raw"))
        expd = ctx.enter_context(signal(m, "expd"))
        hidden = ctx.enter_context(signal(m, "hidden"))
        down_done = ctx.enter_context(signal(m, "down_done"))
        added = ctx.enter_context(signal(m, "added"))
        w_in = ctx.enter_context(signal(m, "w_in"))
        init = ctx.enter_context(signal(m, "init"))
        logits = ctx.enter_context(signal(m, "logits"))
        logits_kept = ctx.enter_context(signal(m, "logits_kept"))
        by_token = ctx.enter_context(signal(m, "by_token"))
        to_exp = ctx.enter_context(signal(m, "to_exp"))
        routed_exp = ctx.enter_context(signal(m, "routed_exp"))
        gated = ctx.enter_context(signal(m, "gated"))
        turned = ctx.enter_context(signal(m, "turned"))
        gt_done = ctx.enter_context(signal(m, "gt_done"))
        spread = ctx.enter_context(signal(m, "spread"))
        kept = ctx.enter_context(signal(m, "kept"))
        norm = Norm(m, ctx, "norm_ffn_g", layer * DC, xn)
        block = ctx.enter_context(nc.Block())

        @block.sync
        def _(sp):
            sp.dma_start(wr[:, :, 0:NG], I["moe_w_rg"][layer].rearrange("(c p) g -> p c g", p=P)).then_inc(w_in, 16)
            sp.dma_start(wr[:, :, NG:20], I["moe_w_re"][layer].rearrange("(c p) g -> p c g", p=P)).then_inc(w_in, 16)
            sp.dma_start(bias[:, 0:NG], I["moe_b_rg"][layer].partition_broadcast(P)).then_inc(w_in, 16)
            sp.dma_start(bias[:, NG:20], I["moe_b_re"][layer].partition_broadcast(P)).then_inc(w_in, 16)
            def load_gate_up(e):
                fixed = isinstance(e, int)
                for s in range(4):
                    if not (fixed and e == 0):
                        sp.wait_ge(used[s] if s < 3 else hidden_raw, e)
                    for at, w in ((0, wg), (FE, wu)):
                        src = w[e, :, s, :, :] if fixed else w[bass.ds(e, 1), :, s, :, :].squeeze(0)
                        sp.dma_start(slots[:, s, :, at:at + FE], src).then_inc(landed[s], 16)

            def load_down(e):
                fixed = isinstance(e, int)
                if not (fixed and e == 0):
                    sp.wait_ge(down_done, e * DC)
                sp.dma_start(down, wd[e] if fixed else wd[bass.ds(e, 1), :, :, :].squeeze(0)).then_inc(down_landed, 16)

            load_gate_up(0)
            load_down(0)
            load_gate_up(1)
            with sp.Fori(2, NE) as e:
                load_gate_up(e)
                load_down(e - 1)
            load_down(NE - 1)

        @block.gpsimd
        def _(pool):
            for g in range(4):
                pool.memset(rank[:, g:g + 1], float(4 - g))
            pool.memset(logit[:, :, :], 0.0)
            pool.drain().then_inc(init, 1)

        @block.tensor
        def _(pe):
            def gate_up(e):
                for s in range(4):
                    pe.wait_ge(landed[s], e * 32 + 32)
                    if s == 0 and not (isinstance(e, int) and e == 0):
                        pe.wait_ge(hidden, e * 2)
                    for k in range(KPS):
                        for t in range(TPB):
                            mm = pe.matmul(m.psum[:, t, 0:T], slots[:, s, k, t * P:(t + 1) * P], xn[:, s * KPS + k, :],
                                           start=(s == 0 and k == 0), stop=(s == 3 and k == KPS - 1))
                    if s < 3:
                        mm.then_inc(used[s], 1)
                mm.then_inc(hidden_raw, 1)

            def project_down(e):
                pe.wait_ge(hidden, e * 2 + 2)
                pe.wait_ge(down_landed, e * 16 + 16)
                for n in range(DC):
                    if isinstance(e, int) and e == 0 and n < 4:
                        pass
                    else:
                        pe.wait_ge(added, e * DC + (n - 3))
                    for k in range(2):
                        rhs = hid[:, e, k, :] if isinstance(e, int) else hid[:, bass.ds(e, 1), k, :].squeeze(1)
                        mm = pe.matmul(m.psum[:, 4 + n % 4, 0:T], down[:, k, n * P:(n + 1) * P], rhs, start=(k == 0),
                                       stop=(k == 1))
                    mm.then_inc(down_done, 1)

            norm.tensor(pe)
            pe.wait_ge(w_in, 64)
            for c in range(DC):
                pe.wait_ge(norm.normed, c + 1)
                mm = pe.matmul(m.psum[0:20, 4, 0:T], wr[:, c, :], xn[:, c, :], start=(c == 0), stop=(c == DC - 1))
            mm.then_inc(logits, 1)
            pe.wait_ge(logits_kept, 1)
            for j, (t0, n) in enumerate(TILES):
                mm = pe.transpose(m.psum[0:n, 5, 20 * j:20 * j + 20], logit_rows[0:20, t0:t0 + n], m.ident[0:20, 0:20])
            mm.then_inc(by_token, 1)
            gate_up(0)
            pe.wait_ge(gated, 1)
            for j, (t0, n) in enumerate(TILES):
                mm = pe.transpose(m.psum[0:NE, 6, t0:t0 + n], gates[0:n, j, :, :].rearrange("p g e -> p (g e)"),
                                  m.ident[0:n, 0:n])
            mm.then_inc(turned, 1)
            pe.wait_ge(gt_done, 1)
            for e in range(NE):
                if e >= 4:
                    pe.wait_ge(kept, e - 3)
                pe.matmul(m.psum[:, 4 + e % 4, 0:T], m.ident[0:NE, e:e + 1].to_broadcast([NE, P]), gt16[0:NE, :],
                          start=True, stop=True).then_inc(spread, 1)
            gate_up(1)
            project_down(0)
            with pe.Fori(2, NE) as e:
                gate_up(e)
                project_down(e - 1)
            project_down(NE - 1)

        @block.scalar
        def _(act):
            norm.scalar(act)
            act.wait_ge(logits, 1)
            act.copy(logit_rows[0:20, :], m.psum[0:20, 4, 0:T]).then_inc(logits_kept, 1)
            act.wait_ge(to_exp, 1)
            act.activation(tmp[3], tmp[3], ACT.Exp).then_inc(routed_exp, 1)
            act.wait_ge(to_exp, 2)
            act.activation(tmp[9], tmp[9], ACT.Exp).then_inc(routed_exp, 1)
            for e in range(NE):
                act.wait_ge(spread, e + 1)
                act.copy(gb[:, e, :], m.psum[:, 4 + e % 4, 0:T]).then_inc(kept, 1)
            act.wait_ge(hidden_raw, 1)
            for f in range(2):
                act.activation(ex[:, f, :], m.psum[:, f, 0:T], ACT.Silu).then_inc(expd, 1)
            with act.Fori(1, NE) as e:
                act.wait_ge(hidden_raw, e + 1)
                act.wait_ge(hidden, e * 2)
                for f in range(2):
                    act.activation(ex[:, f, :], m.psum[:, f, 0:T], ACT.Silu).then_inc(expd, 1)

        @block.vector
        def _(dve):
            norm.vector(dve)
            bc = [P, 3, 4]
            rk = rank.unsqueeze(1).to_broadcast(bc)

            def first_largest(values, largest, ranked, onehot):
                dve.tensor_reduce(largest, values, AX_X, ALU.max)
                dve.drain()
                dve.tensor_tensor(ranked, values, largest.to_broadcast(bc), ALU.is_ge)
                dve.drain()
                dve.tensor_tensor(ranked, ranked, rk, ALU.mult)
                dve.drain()
                dve.tensor_reduce(s1, ranked, AX_X, ALU.max)
                dve.drain()
                dve.tensor_tensor(onehot, ranked, s1.to_broadcast(bc), ALU.is_equal)
                dve.drain()

            dve.wait_ge(init, 1)
            dve.wait_ge(by_token, 1)
            for j, (t0, n) in enumerate(TILES):
                dve.tensor_tensor(logit[0:n, j, :], m.psum[0:n, 5, 20 * j:20 * j + 20], bias[0:n, :], ALU.add)
            dve.drain()
            lg = logit[:, :, 0:NG]
            first_largest(lg, mx, tmp[0], tmp[1])
            dve.tensor_tensor(tmp[3], lg, mx.to_broadcast(bc), ALU.subtract)
            dve.drain().then_inc(to_exp, 1)
            el4 = logit[:, :, NG:20].rearrange("p j (g e) -> p j g e", g=NG)
            for g in range(NG):
                dve.tensor_tensor(prod[:, :, g, :], el4[:, :, g, :], tmp[1][:, :, g:g + 1].to_broadcast(bc), ALU.mult)
            dve.drain()
            dve.tensor_tensor(tmp[4], prod[:, :, 0, :], prod[:, :, 1, :], ALU.add)
            dve.tensor_tensor(tmp[5], prod[:, :, 2, :], prod[:, :, 3, :], ALU.add)
            dve.drain()
            dve.tensor_tensor(tmp[4], tmp[4], tmp[5], ALU.add)
            dve.drain()
            first_largest(tmp[4], m1, tmp[0], tmp[6])
            dve.scalar_tensor_tensor(tmp[5], tmp[6], NEG, tmp[4], ALU.mult, ALU.add)
            dve.drain()
            first_largest(tmp[5], mx, tmp[0], tmp[7])
            dve.tensor_tensor(tmp[9], tmp[4], m1.to_broadcast(bc), ALU.subtract)
            dve.drain().then_inc(to_exp, 1)
            dve.tensor_tensor(tmp[7], tmp[7], tmp[6], ALU.add)
            dve.wait_ge(routed_exp, 2)
            dve.drain()
            dve.tensor_tensor(tmp[8], tmp[9], tmp[7], ALU.mult)
            dve.tensor_reduce(pg, tmp[3], AX_X, ALU.add)
            dve.drain()
            dve.tensor_reduce(s1, tmp[8], AX_X, ALU.add)
            dve.drain()
            dve.tensor_tensor(s1, s1, pg, ALU.mult)
            dve.drain()
            dve.reciprocal(s1, s1)
            dve.drain()
            dve.tensor_tensor(tmp[8], tmp[8], s1.to_broadcast(bc), ALU.mult)
            dve.drain()
            for g in range(NG):
                dve.tensor_tensor(gates[:, :, g, :], tmp[8], tmp[1][:, :, g:g + 1].to_broadcast(bc), ALU.mult)
            dve.drain().then_inc(gated, 1)
            dve.wait_ge(turned, 1)
            dve.tensor_copy(gt16[0:NE, :], m.psum[0:NE, 6, 0:T]).then_inc(gt_done, 1)
            def hidden_values(e):
                dve.wait_ge(hidden_raw, e + 1)
                g = gb[:, e, :] if isinstance(e, int) else gb[:, bass.ds(e, 1), :].squeeze(1)
                for f in range(2):
                    dve.tensor_tensor(up[:, f, :], m.psum[:, 2 + f, 0:T], g, ALU.mult)
                dve.drain()
                for f in range(2):
                    dve.wait_ge(expd, e * 2 + (f + 1))
                    h = hid[:, e, f, :] if isinstance(e, int) else hid[:, bass.ds(e, 1), f, :].squeeze(1)
                    dve.tensor_tensor(h, up[:, f, :], ex[:, f, :], ALU.mult).then_inc(hidden, 1)

            def add_down(e):
                for n in range(DC):
                    dve.wait_ge(down_done, e * DC + (n + 1))
                    dve.tensor_tensor(m.x[:, n, :], m.x[:, n, :], m.psum[:, 4 + n % 4, 0:T], ALU.add).then_inc(added, 1)

            dve.wait_ge(kept, NE)
            hidden_values(0)
            hidden_values(1)
            add_down(0)
            with dve.Fori(2, NE) as e:
                hidden_values(e)
                add_down(e - 1)
            add_down(NE - 1)


def store_columns(nc, m, columns, n, dram_rows):
    stage = view(m.xn, 0, 8, P)
    tiles = [(i, min(P, n - i)) for i in range(0, n, P)]
    with signal(m, "turned") as turned, signal(m, "copied") as copied, signal(m, "stored") as stored, \
            nc.Block() as block:
        @block.tensor
        def _(pe):
            for i, (a, k) in enumerate(tiles):
                pe.transpose(m.psum[0:k, i, 0:P], columns[:, a:a + k], m.ident[:, :]).then_inc(turned, 1)

        @block.scalar
        def _(act):
            for i, (a, k) in enumerate(tiles):
                act.wait_ge(turned, i + 1)
                act.copy(stage[0:k, i, :], m.psum[0:k, i, 0:P]).then_inc(copied, 1)

        @block.sync
        def _(sp):
            stores = 0
            for i, (a, k) in enumerate(tiles):
                sp.wait_ge(copied, i + 1)
                for lo, hi, rows in dram_rows:
                    f, t = max(lo, a), min(hi, a + k)
                    if f < t:
                        sp.dma_start(rows[f - lo:t - lo, :], stage[f - a:t - a, i, :]).then_inc(stored, 16)
                        stores += 1
            sp.wait_ge(stored, 16 * stores)


def rg_lru(nc, m, I, O):
    proj = view(m.arena, 0, IN0C + 1, T)
    xc = view(m.arena, CONV0, LC, T)
    wa = view(m.arena, 15700, LC, P)
    wx = view(m.arena, 16800, LC, P)
    cols = view(m.arena, 17900, 27 * LC)
    wt = view(m.arena, 18200, DC, RANK)
    r, g, a, b, h = (view(m.ring, 2560 * i, LC, T) for i in range(5))
    c8 = m.decay[:, 0:LC]
    tl = m.decay[:, LC:2 * LC]
    lam = m.prm[:, PCOL["l0_lru_lam"]:PCOL["l0_lru_lam"] + LC]
    h0 = m.prm[:, PCOL["state_lru_h"]:PCOL["state_lru_h"] + B * LC].rearrange("p (b c) -> p c b", b=B)
    hl = view(m.small, 0, 9 * LC)
    add0 = view(m.small, 96, LC, B)
    with signal(m, "blank") as blank, signal(m, "w_in") as w_in, signal(m, "negs") as negs, \
            signal(m, "prod") as prod, signal(m, "expd") as expd, signal(m, "sig") as sig, \
            signal(m, "pwr") as pwr, signal(m, "om") as om, signal(m, "ge") as ge, \
            signal(m, "tail_in") as tail_in, signal(m, "tail") as tail, nc.Block() as block:
        @block.gpsimd
        def _(pool):
            pool.memset(wa, 0.0)
            pool.memset(wx, 0.0)
            pool.drain().then_inc(blank, 1)

        @block.sync
        def _(sp):
            sp.dma_start(wt, I["l0_w_in"][0][:, IN0C * P:IN0].rearrange("(k p) n -> p k n", p=P)).then_inc(tail_in, 16)
            sp.wait_ge(blank, 1)
            for w, name in ((wa, "l0_lru_wa"), (wx, "l0_lru_wx")):
                src = I[name].rearrange("a (c two) i o -> two i (a c) o", two=2)
                sp.dma_start(w[0:64, :, 0:64], src[0]).then_inc(w_in, 16)
                sp.dma_start(w[64:128, :, 64:128], src[1]).then_inc(w_in, 16)

        @block.tensor
        def _(pe):
            pe.wait_ge(w_in, 64)
            for q, w in enumerate((wa, wx)):
                for c in range(LC):
                    if q:
                        pe.wait_ge(expd, 2 + c + 1)
                    pe.matmul(m.psum[:, c, 0:T], w[:, c, :], xc[:, c, :], start=True, stop=True).then_inc(prod, 1)
            pe.wait_ge(tail_in, 16)
            pe.wait_ge(expd, 2 + LC + 1)
            for k in range(DC):
                mm = pe.matmul(m.psum[0:RANK, 0, 0:T], wt[:, k, :], m.XN[:, k, :], start=(k == 0), stop=(k == DC - 1))
            mm.then_inc(tail, 1)

        @block.scalar
        def _(act):
            act.wait_ge(negs, 1)
            act.activation(tl, tl, ACT.Exp, scale=-1.0).then_inc(expd, 1)
            act.drain()
            act.activation(tl, tl, ACT.Ln, bias=1.0).then_inc(expd, 1)
            for q, dst in enumerate((r, g)):
                for c in range(LC):
                    act.wait_ge(prod, q * LC + c + 1)
                    act.activation(dst[:, c, :], m.psum[:, c, 0:T], ACT.Sigmoid,
                                   bias=param(m, ("l0_lru_ba", "l0_lru_bx")[q], c)).then_inc(expd, 1)
            act.wait_ge(sig, 1)
            for c in range(LC):
                act.activation(a[:, c, :], r[:, c, :], ACT.Exp, scale=c8[:, c:c + 1]).then_inc(pwr, 1)
            for c in range(LC):
                act.activation(b[:, c, :], r[:, c, :], ACT.Tanh, scale=c8[:, c:c + 1]).then_inc(pwr, 1)
            act.drain()
            act.activation(r, proj[:, GA:GA + LC], ACT.Gelu_apprx_tanh).then_inc(ge, 1)
            act.wait_ge(tail, 1)
            act.copy(proj[0:RANK, AL, :], m.psum[0:RANK, 0, 0:T])
            act.wait_ge(om, 1)
            act.activation(b, b, ACT.Sqrt, scale=-1.0).then_inc(om, 1)

        @block.vector
        def _(dve):
            dve.scalar_tensor_tensor(tl, lam, -1.0, lam, ALU.mult, ALU.max)
            dve.drain().then_inc(negs, 1)
            dve.wait_ge(expd, 2)
            dve.tensor_scalar(c8, lam, -1.0, 0.0, ALU.mult, ALU.max)
            dve.drain()
            dve.tensor_tensor(c8, c8, tl, ALU.add)
            dve.drain()
            dve.tensor_scalar(c8, c8, -8.0, None, ALU.mult)
            dve.wait_ge(expd, 2 + 2 * LC)
            dve.drain().then_inc(sig, 1)
            dve.tensor_tensor(g, g, xc, ALU.mult)
            dve.wait_ge(pwr, LC)
            dve.tensor_tensor(h, a, a, ALU.mult)
            dve.drain()
            dve.wait_ge(pwr, 2 * LC)
            dve.scalar_tensor_tensor(b, h, 1.0, b, ALU.add, ALU.mult)
            dve.drain().then_inc(om, 1)
            dve.wait_ge(om, 2)
            dve.tensor_tensor(b, b, g, ALU.mult)
            dve.tensor_tensor(add0, a[:, :, T_P:T:T_S], h0, ALU.mult)
            dve.drain()
            dve.tensor_tensor(b[:, :, T_P:T:T_S], b[:, :, T_P:T:T_S], add0, ALU.add)
            dve.memset(a[:, :, T_P:T:T_S], 0.0)
            dve.memset(a[:, :, 0:1], 0.0)
            dve.drain()
            flat = "p c t -> p (c t)"
            dve.tensor_tensor_scan(h.rearrange(flat), a.rearrange(flat), b.rearrange(flat), 0.0, ALU.mult, ALU.add)
            dve.wait_ge(ge, 1)
            dve.drain()
            dve.tensor_copy(hl[:, 0:LC], h[:, :, T_P - 1:T_P].squeeze(2))
            dve.tensor_copy(hl[:, LC:9 * LC].rearrange("p (b c) -> p c b", b=B), h[:, :, T_P + T_S - 1:T:T_S])
            dve.drain()
            dve.tensor_tensor(proj[:, GA:GA + LC], h, r, ALU.mult)
    store_last_rows(nc, m, proj[:, XA:XA + LC], LC, cols, O["p_lru_conv"], O["s_lru_conv"])
    store_columns(nc, m, hl, 9 * LC, [(0, LC, O["p_lru_h"].rearrange("a b (c p) -> (a b c) p", p=P)),
                                      (LC, 9 * LC, O["s_lru_h"].rearrange("a b (c p) -> (a b c) p", p=P))])


def gla(nc, m, I, O):
    proj = view(m.arena, 0, IN0C + 1, T)
    bc, t1, qe, ke, qi, kh, ab = (view(m.ring, 1280 * i, H, T) for i in range(7))
    vt = view(m.ring, 8960, 3, H, DV)
    kt = view(m.ring, 12032, 3, H, DK)
    att = view(m.ring, 13568, H, 3, P)
    sp_ = view(m.ring, 15104, H, DV)
    ebl = view(m.small, 0, H, 16)
    wa2 = view(m.small, 64, 512)
    ss = view(m.arena, 13200, B, H, DV)
    km = view(m.arena, 0, 2, B, DK)
    osb = proj[:, QA:QA + 8]

    def cut(v, w):
        return (v[:, :, 0:T_P].rearrange("p h (c l) -> p h c l", l=GC) if w == 0 else
                v[:, :, T_P:T].rearrange("p h (c l) -> p h c l", l=T_S))

    with signal(m, "w_in") as w_in, signal(m, "prod") as prod, signal(m, "zd") as zd, \
            signal(m, "lnd") as lnd, signal(m, "dd") as dd, signal(m, "ee") as ee, \
            signal(m, "states_in") as states_in, nc.Block() as block:
        @block.sync
        def _(sp):
            sp.dma_start(wa2[0:RANK, :], I["l0_gla_wa2"].rearrange("a r n -> (a r) n")).then_inc(w_in, 16)
            for b in range(B):
                sp.dma_start(ss[:, b, :, :], I["state_gla_S"][0, b].rearrange("h d e -> d h e")).then_inc(states_in, 16)
            sp.wait_ge(states_in, 16 * B)
            sp.wait_ge(w_in, 16)

        @block.tensor
        def _(pe):
            pe.wait_ge(w_in, 16)
            for h in range(H):
                pe.matmul(m.psum[:, h, 0:T], wa2[0:RANK, h * DK:(h + 1) * DK], proj[0:RANK, AL, :], start=True,
                          stop=True).then_inc(prod, 1)

        @block.scalar
        def _(act):
            act.wait_ge(zd, 1)
            act.activation(ab, ab, ACT.Exp, scale=-1.0)
            act.drain()
            act.activation(ab, ab, ACT.Ln, bias=1.0).then_inc(lnd, 1)
            act.wait_ge(dd, 1)
            act.activation(qe, t1, ACT.Exp)
            act.activation(ke, t1, ACT.Exp, scale=-1.0)
            act.activation(qi, bc, ACT.Exp).then_inc(ee, 1)
            act.wait_ge(dd, 2)
            act.activation(kh, t1, ACT.Exp)
            act.activation(ebl, ebl, ACT.Exp).then_inc(ee, 1)

        @block.vector
        def _(dve):
            for h in range(H):
                dve.wait_ge(prod, h + 1)
                dve.tensor_scalar(t1[:, h, :], m.psum[:, h, 0:T], param(m, "l0_gla_ba2", h), None, ALU.add)
            dve.drain()
            dve.scalar_tensor_tensor(ab, t1, -1.0, t1, ALU.mult, ALU.max).then_inc(zd, 1)
            dve.wait_ge(lnd, 1)
            dve.scalar_tensor_tensor(t1, t1, 0.0, ab, ALU.min, ALU.subtract)
            dve.drain()
            dve.tensor_scalar(t1, t1, 1.0 / 16.0, None, ALU.mult)
            dve.drain()
            for h in range(H):
                dve.tensor_tensor_scan(bc[:, h, :], m.keep32[:, :], t1[:, h, :], 0.0, ALU.mult, ALU.add)
            dve.drain()
            for w, (l, ref) in enumerate(((GC, GC // 2 - 1), (T_S, T_S // 2 - 1))):
                b4 = cut(bc, w)
                dve.tensor_tensor(cut(t1, w), b4, b4[:, :, :, ref:ref + 1].to_broadcast([P, H, 8, l]), ALU.subtract)
                dve.tensor_copy(ebl[:, :, 8 * w:8 * w + 8], b4[:, :, :, l - 1:l].squeeze(3))
            dve.drain().then_inc(dd, 1)
            dve.wait_ge(ee, 1)
            for w, l in ((0, GC), (1, T_S)):
                b4 = cut(bc, w)
                dve.tensor_tensor(cut(t1, w), b4[:, :, :, l - 1:l].to_broadcast([P, H, 8, l]), b4, ALU.subtract)
            dve.drain().then_inc(dd, 1)
            q, k = proj[:, QA:QA + H], proj[:, KA:KA + H]
            dve.scalar_tensor_tensor(qe, q, DK ** -0.5, qe, ALU.mult, ALU.mult)
            dve.scalar_tensor_tensor(qi, q, DK ** -0.5, qi, ALU.mult, ALU.mult)
            dve.tensor_tensor(ke, ke, k, ALU.mult)
            dve.wait_ge(ee, 2)
            dve.tensor_tensor(kh, kh, k, ALU.mult)
    with signal(m, "turned") as turned, nc.Block() as block:
        @block.tensor
        def _(pe):
            for j, (t0, n) in enumerate(TILES):
                for c in range(8):
                    mm = pe.transpose(m.psum[0:n, 2 * j + c // 4, (c % 4) * P:(c % 4 + 1) * P], proj[:, VA + c, t0:t0 + n],
                                      m.ident[:, :])
                mm.then_inc(turned, 1)
            for j, (t0, n) in enumerate(TILES[0:2]):
                for h in range(H):
                    mm = pe.transpose(m.psum[0:n, 6 + j, h * P:(h + 1) * P], kh[:, h, t0:t0 + n], m.ident[:, :])
                mm.then_inc(turned, 1)

        @block.vector
        def _(dve):
            for j, (t0, n) in enumerate(TILES):
                dve.wait_ge(turned, j + 1)
                dve.tensor_copy(vt[0:n, j].rearrange("p h e -> p (h e)"),
                                m.psum[0:n, 2 * j:2 * j + 2, :].rearrange("p a b -> p (a b)"))
            for j, (t0, n) in enumerate(TILES[0:2]):
                dve.wait_ge(turned, 4 + j)
                dve.tensor_copy(kt[0:n, j].rearrange("p h e -> p (h e)"), m.psum[0:n, 6 + j, :])
    with signal(m, "turned") as turned, signal(m, "scored") as scored, nc.Block() as block:
        @block.tensor
        def _(pe):
            t0, n = TILES[2]
            for h in range(H):
                mm = pe.transpose(m.psum[0:n, 4, h * P:(h + 1) * P], kh[:, h, t0:t0 + n], m.ident[:, :])
            mm.then_inc(turned, 1)
            for h in range(H):
                for j, (t0, n) in enumerate(TILES):
                    mm = pe.matmul(m.psum[0:n, h, j * P:j * P + n], ke[:, h, t0:t0 + n], qe[:, h, t0:t0 + n], start=True,
                                   stop=True)
                mm.then_inc(scored, 1)

        @block.vector
        def _(dve):
            dve.wait_ge(turned, 1)
            dve.tensor_copy(kt[0:64, 2].rearrange("p h e -> p (h e)"), m.psum[0:64, 4, :])
            for h in range(H):
                dve.wait_ge(scored, h + 1)
                for j, (t0, n) in enumerate(TILES):
                    mask = m.causal8 if j == 2 else m.causal32
                    dve.tensor_tensor(att[0:n, h, j, 0:n], m.psum[0:n, h, j * P:j * P + n], mask[0:n, 0:n], ALU.mult)
    for pair in range(2):
        heads = (2 * pair, 2 * pair + 1)
        with signal(m, "masked") as masked, signal(m, "upd") as upd, signal(m, "new_s") as new_s, \
                signal(m, "supd") as supd, signal(m, "snew") as snew, signal(m, "o_done") as o_done, \
                nc.Block() as block:
            @block.gpsimd
            def _(pool):
                for i, h in enumerate(heads):
                    for b in range(B):
                        pool.affine_select(km[0:64, i, b, :], kt[0:64, 2, h, :], [[0, DK]], ALU.is_ge, 0.0,
                                           base=-T_S * b, channel_multiplier=1)
                pool.drain()
                for i, h in enumerate(heads):
                    for b in range(B):
                        pool.affine_select(km[0:64, i, b, :], km[0:64, i, b, :], [[0, DK]], ALU.is_ge, 0.0,
                                           base=T_S * b + T_S - 1, channel_multiplier=-1)
                pool.drain().then_inc(masked, 1)

            @block.tensor
            def _(pe):
                def o(i, e):
                    return m.psum[:, 2 * i + e]
                for i, h in enumerate(heads):
                    for e in range(2):
                        for j, (t0, n) in enumerate(TILES):
                            pe.matmul(o(i, e)[:, t0:t0 + n], vt[0:n, j, h, e * P:(e + 1) * P], att[0:n, h, j, 0:n],
                                      start=(j == 0), stop=False, skip_group_check=True)
                pe.wait_ge(masked, 1)
                for c in range(NCH):
                    j, r0 = c // 4, (c % 4) * GC
                    for i, h in enumerate(heads):
                        if c:
                            pe.wait_ge(new_s, 2 * (c - 1) + i + 1)
                            for e in range(2):
                                pe.matmul(o(i, e)[:, c * GC:(c + 1) * GC], sp_[:, h, e * P:(e + 1) * P],
                                          qi[:, h, c * GC:(c + 1) * GC], start=False, stop=False, skip_group_check=True)
                        pe.matmul(m.psum[:, 4 + i, 0:DV], kt[r0:r0 + GC, j, h, :], vt[r0:r0 + GC, j, h, :], start=True,
                                  stop=True, tile_position=(r0, 0)).then_inc(upd, 1)
                    b = c
                    for i, h in enumerate(heads):
                        for e in range(2):
                            pe.matmul(o(i, e)[:, T_P + b * T_S:T_P + (b + 1) * T_S], ss[:, b, h, e * P:(e + 1) * P],
                                      qi[:, h, T_P + b * T_S:T_P + (b + 1) * T_S], start=False, stop=False,
                                      skip_group_check=True)
                        if b:
                            pe.wait_ge(snew, 2 * (b - 1) + i + 1)
                        pe.matmul(m.psum[:, 6 + i, 0:DV], km[0:64, i, b, :], vt[0:64, 2, h, :], start=True,
                                  stop=True).then_inc(supd, 1)
                pe.drain().then_inc(o_done, 1)

            @block.vector
            def _(dve):
                for c in range(NCH):
                    for i, h in enumerate(heads):
                        dve.wait_ge(upd, 2 * c + i + 1)
                        if c == 0:
                            dve.tensor_copy(sp_[:, h, :], m.psum[:, 4 + i, 0:DV]).then_inc(new_s, 1)
                        else:
                            dve.scalar_tensor_tensor(sp_[:, h, :], sp_[:, h, :], ebl[:, h, c:c + 1], m.psum[:, 4 + i, 0:DV],
                                                     ALU.mult, ALU.add).then_inc(new_s, 1)
                    b = c
                    for i, h in enumerate(heads):
                        dve.wait_ge(supd, 2 * b + i + 1)
                        dve.scalar_tensor_tensor(ss[:, b, h, :], ss[:, b, h, :], ebl[:, h, 8 + b:9 + b],
                                                 m.psum[:, 6 + i, 0:DV], ALU.mult, ALU.add).then_inc(snew, 1)
                    dve.drain()
                dve.wait_ge(o_done, 1)
                for i, h in enumerate(heads):
                    for e in range(2):
                        dve.tensor_copy(osb[:, 2 * h + e, :], m.psum[:, 2 * i + e, 0:T])
    sq = view(m.ring, 0, 8, T)
    rs = view(m.ring, 2560, H, T)
    sg = view(m.ring, 5120, 8, T)
    with signal(m, "sqd") as sqd, signal(m, "summed") as summed, signal(m, "root") as root, \
            signal(m, "expd") as expd, signal(m, "stored") as stored, nc.Block() as block:
        @block.sync
        def _(sp):
            for b in range(B):
                sp.dma_start(O["s_gla_S"][0, b].rearrange("h d e -> d h e"), ss[:, b, :, :]).then_inc(stored, 16)
            sp.dma_start(O["p_gla_S"][0, 0].rearrange("h d e -> d h e"), sp_).then_inc(stored, 16)
            sp.wait_ge(stored, 16 * (B + 1))

        @block.scalar
        def _(act):
            act.activation(sq, osb, ACT.Square).then_inc(sqd, 1)
            act.activation(sg, proj[:, GG:GG + 8], ACT.Silu).then_inc(expd, 1)
            act.wait_ge(root, 1)
            act.activation(rs, rs, ACT.Sqrt).then_inc(root, 1)

        @block.tensor
        def _(pe):
            pe.wait_ge(sqd, 1)
            for h in range(H):
                for e in range(2):
                    mm = pe.matmul(m.psum[:, h, 0:T], m.ones[:, :], sq[:, 2 * h + e, :], start=(e == 0), stop=(e == 1))
                mm.then_inc(summed, 1)

        @block.vector
        def _(dve):
            for h in range(H):
                dve.wait_ge(summed, h + 1)
                dve.tensor_scalar(rs[:, h, :], m.psum[:, h, 0:T], 1.0 / DV, EPS, ALU.mult, ALU.add)
            dve.drain().then_inc(root, 1)
            dve.wait_ge(root, 2)
            dve.reciprocal(rs, rs)
            dve.drain()
            for c in range(8):
                dve.scalar_tensor_tensor(osb[:, c, :], osb[:, c, :], param(m, "l0_gla_norm_g", c), rs[:, c // 2, :],
                                         ALU.mult, ALU.mult)
            dve.wait_ge(expd, 1)
            dve.drain()
            dve.tensor_tensor(proj[:, GG:GG + 8], osb, sg, ALU.mult)


def first_projection(nc, m, I):
    proj = view(m.arena, 0, IN0C + 1, T)
    w_in = I["l0_w_in"][0]
    conv = Conv(m, proj[:, XA:XA + LC], view(m.arena, CONV0, LC, T), LC, "l0_lru_conv_w", "l0_lru_conv_b", 1, False)
    conv.begin(nc, I["state_lru_conv"], view(m.arena, 18200, W_LRU), view(m.ring, 0, LC, B, 3))
    linear(nc, m, w_in[:, 0:IN0C * P], DC, lambda k: m.XN[:, k, :],
           copy_to=lambda n: proj[:, bass.ds(n, 1), :].squeeze(1), conv=conv, norm=("norm_mix_g", 0))


def final_norm(nc, m, O):
    y = view(m.arena, 0, DC, T)
    y_tok = view(m.arena, DC * T, 3, D)
    with ExitStack() as ctx:
        norm = Norm(m, ctx, "norm_final_g", 0, y)
        turned, copied, stored = (ctx.enter_context(signal(m, n)) for n in ("turned", "copied", "stored"))
        block = ctx.enter_context(nc.Block())

        @block.tensor
        def _(pe):
            norm.tensor(pe)
            q = 0
            for j, (t0, n) in enumerate(TILES):
                for g in range(4):
                    pe.wait_ge(norm.normed, 4 * g + 4)
                    if q >= 8:
                        pe.wait_ge(copied, q - 7)
                    for c in range(4):
                        mm = pe.transpose(m.psum[0:n, q % 8, c * P:(c + 1) * P], y[:, 4 * g + c, t0:t0 + n], m.ident[:, :])
                    mm.then_inc(turned, 1)
                    q += 1

        @block.scalar
        def _(act):
            norm.scalar(act)
            q = 0
            for j, (t0, n) in enumerate(TILES):
                for g in range(4):
                    act.wait_ge(turned, q + 1)
                    act.copy(y_tok[0:n, j, g * 512:(g + 1) * 512], m.psum[0:n, q % 8, :]).then_inc(copied, 1)
                    q += 1

        @block.vector
        def _(dve):
            norm.vector(dve)

        @block.sync
        def _(sp):
            outs = [O["y_prompt"][0, 0:P, :], O["y_prompt"][0, P:T_P, :], O["y_sample"].rearrange("b t d -> (b t) d")]
            for j, (t0, n) in enumerate(TILES):
                sp.wait_ge(copied, 4 * (j + 1))
                sp.dma_start(outs[j], y_tok[0:n, j, :]).then_inc(stored, 16)
            sp.wait_ge(stored, 48)


class HeadNorm:

    def __init__(self, m, xm, xc, h, summed, centred, sqd, root):
        self.m, self.h = m, h
        self.x, self.xc = xm[:, h * HC:(h + 1) * HC], xc[:, h * HC:(h + 1) * HC]
        self.sq = view(m.ring, 8192, HC, T)
        self.mean = view(m.ring, 8192 + HC * T, T)
        self.summed, self.centred, self.sqd, self.root = summed, centred, sqd, root

    def sum(self, pe):
        for c in range(HC):
            mm = pe.matmul(self.m.psum[:, 6, 0:T], self.m.ones[:, :], self.x[:, c, :], start=(c == 0),
                           stop=(c == HC - 1))
        mm.then_inc(self.summed, 1)

    def centre(self, dve):
        dve.wait_ge(self.summed, 1)
        dve.tensor_scalar(self.mean, self.m.psum[:, 6, 0:T], 1.0 / DH, None, ALU.mult)
        dve.drain()
        for c in range(HC):
            dve.tensor_tensor(self.x[:, c, :], self.x[:, c, :], self.mean, ALU.subtract).then_inc(self.centred, 1)

    def square(self, act):
        for c in range(HC):
            act.wait_ge(self.centred, c + 1)
            act.activation(self.sq[:, c, :], self.x[:, c, :], ACT.Square).then_inc(self.sqd, 1)

    def sum_squares(self, pe):
        for c in range(HC):
            pe.wait_ge(self.sqd, c + 1)
            mm = pe.matmul(self.m.psum[:, 7, 0:T], self.m.ones[:, :], self.sq[:, c, :], start=(c == 0),
                           stop=(c == HC - 1))
        mm.then_inc(self.summed, 1)

    def variance(self, dve):
        dve.wait_ge(self.summed, 2)
        dve.drain()
        dve.tensor_scalar(self.mean, self.m.psum[:, 7, 0:T], 1.0 / DH, EPS, ALU.mult, ALU.add)
        dve.drain().then_inc(self.root, 1)

    def take_root(self, act):
        act.wait_ge(self.root, 1)
        act.activation(self.mean, self.mean, ACT.Sqrt).then_inc(self.root, 1)

    def invert(self, dve):
        dve.wait_ge(self.root, 2)
        dve.reciprocal(self.mean, self.mean)
        dve.drain()

    def apply(self, dve):
        for c in range(HC):
            dve.scalar_tensor_tensor(self.x[:, c, :], self.x[:, c, :], param(self.m, "l1_norm_g", self.h * HC + c),
                                     self.mean, ALU.mult, ALU.mult)
        dve.drain()
        for c in range(HC):
            dve.scalar_tensor_tensor(self.x[:, c, :], self.xc[:, c, :], param(self.m, "l1_skip", self.h * HC + c),
                                     self.x[:, c, :], ALU.mult, ALU.add)


def mlstm(nc, m, I, O):
    xm = view(m.arena, 0, IC, T)
    xc = view(m.arena, IC * T, IC, T)
    conv = Conv(m, xm, xc, IC, "l1_conv_w", "l1_conv_b", IC // (2 * TPB), True)
    conv.begin(nc, I["state_mlstm_conv"], view(m.arena, 0, DI), view(m.ring, 0, IC, B, 3))
    linear(nc, m, I["l1_w_up"][0][:, 0:DI], DC, lambda k: m.XN[:, k, :],
           copy_to=lambda n: xm[:, bass.ds(n, 1), :].squeeze(1), conv=conv, norm=("norm_mix_g", DC))
    store_last_rows(nc, m, xm, IC, view(m.arena, 20480, 27 * IC), O["p_m_conv"], O["s_m_conv"])

    wq, wk, wv = (view(m.small, IC * QB * i, IC, QB) for i in range(3))
    q_f = view(m.ring, 0, HC, T)
    k_f = view(m.ring, 2560, HC, T)
    bd = view(m.ring, 5120, 3, HC, P)
    blk = view(m.small, 384, 32)
    bg, bgf = view(m.small, 416, 1), view(m.small, 417, 1)
    u_col = view(m.small, 448, 3, H)
    NW = 3 * IC
    wg_rows = view(m.ring, 0, 2, P, 4)
    wg = view(m.ring, 1024, 8, NW)
    spread_o = view(m.ring, 2048, QB, P)
    row_of = view(m.ring, 2560, QB)
    term = view(m.ring, 3072, 3, 8, IC)
    total = view(m.ring, 4096, 3, 8, IC)
    g_xc, g_xm = view(m.ring, 5120, IC, 8), view(m.ring, 5376, IC, 8)
    gates8 = view(m.ring, 6144, T)

    def expand(dve, h, chunks, expanded):
        for c in chunks:
            for i, w in enumerate((wq, wk, wv)):
                dve.tensor_tensor(bd[:, i, c, :].rearrange("p (b o) -> p b o", o=QB),
                                  w[:, h * HC + c, :].unsqueeze(1).to_broadcast([P, 32, QB]),
                                  blk.unsqueeze(2).to_broadcast([P, 32, QB]), ALU.mult).then_inc(expanded, 1)

    with signal(m, "w_in") as w_in, signal(m, "blk_done") as blk_done, signal(m, "turned") as turned, \
            signal(m, "wg_kept") as wg_kept, signal(m, "spread_made") as spread_made, \
            signal(m, "spread") as spread, signal(m, "folded") as folded, signal(m, "gates_done") as gates_done, \
            signal(m, "gates_kept") as gates_kept, nc.Block() as block:
        @block.sync
        def _(sp):
            for j, name in enumerate(("l1_w_ig", "l1_w_fg")):
                sp.dma_start(wg_rows[0:NW, j, :, :], I[name][0].rearrange("(n p) g -> n p g", p=P)).then_inc(w_in, 16)
            for w, name in ((wq, "l1_wq"), (wk, "l1_wk"), (wv, "l1_wv")):
                sp.dma_start(w, I[name][0].rearrange("(c b) i o -> (b i) c o", c=IC)).then_inc(w_in, 16)
            sp.dma_start(bg[0:4, :], I["l1_b_ig"].rearrange("a g -> g a")).then_inc(w_in, 16)
            sp.dma_start(bgf[0:4, :], I["l1_b_fg"].rearrange("a g -> g a")).then_inc(w_in, 16)
            sp.wait_ge(w_in, 7 * 16)

        @block.gpsimd
        def _(pool):
            pool.memset(blk, 1.0)
            pool.drain()
            pool.affine_select(blk, blk, [[-QB, 32]], ALU.is_ge, 0.0, base=0, channel_multiplier=1)
            pool.drain()
            pool.affine_select(blk, blk, [[QB, 32]], ALU.is_ge, 0.0, base=QB - 1, channel_multiplier=-1)
            pool.drain().then_inc(blk_done, 1)

        @block.tensor
        def _(pe):
            pe.wait_ge(w_in, 7 * 16)
            for g in range(8):
                mm = pe.transpose(m.psum[:, g // 4, (g % 4) * NW:(g % 4 + 1) * NW], wg_rows[0:NW, g // 4, :, g % 4],
                                  m.ident[0:NW, 0:NW])
            mm.then_inc(turned, 1)
            pe.wait_ge(wg_kept, 1)
            pe.wait_ge(spread_made, 1)
            for o in range(QB):
                for e in range(2):
                    mm = pe.matmul(m.psum[:, 2 * o + e, 0:4 * NW], spread_o[:, o, :], wg[:, 4 * e:4 * e + 4, :],
                                   start=True, stop=True)
                mm.then_inc(spread, 1)
            pe.wait_ge(folded, 1)
            for c in range(IC):
                for q, (w, src) in enumerate(((g_xc, xc), (g_xm, xm))):
                    mm = pe.matmul(m.psum[0:8, 0, 0:T], w[:, c, :], src[:, c, :], start=(c == 0 and q == 0),
                                   stop=(c == IC - 1 and q == 1))
            mm.then_inc(gates_done, 1)
            pe.wait_ge(gates_kept, 1)
            pe.matmul(m.psum[0:4, 1, 0:T], m.ident[0:8, 4:8], gates8[0:8, :], start=True, stop=True)

        @block.scalar
        def _(act):
            act.wait_ge(turned, 1)
            for e in range(2):
                act.copy(wg[:, 4 * e:4 * e + 4, :], m.psum[:, e, 0:4 * NW].rearrange("p (g n) -> p g n", g=4))
            act.drain().then_inc(wg_kept, 1)
            act.wait_ge(gates_done, 1)
            act.copy(gates8[0:8, :], m.psum[0:8, 0, 0:T]).then_inc(gates_kept, 1)

        @block.vector
        def _(dve):
            dve.tensor_reduce(row_of.unsqueeze(2), m.ident[:, :].rearrange("p (b o) -> p o b", o=QB), AX_X, ALU.add)
            dve.drain()
            dve.wait_ge(blk_done, 1)
            for o in range(QB):
                dve.tensor_scalar(spread_o[:, o, :].rearrange("p (b i) -> p b i", i=QB),
                                  blk.unsqueeze(2).to_broadcast([P, 32, QB]), row_of[:, o:o + 1], None, ALU.mult)
            dve.drain().then_inc(spread_made, 1)
            for o in range(QB):
                dve.wait_ge(spread, o + 1)
                dst = total if o == 0 else term
                for i, w in enumerate((wq, wk, wv)):
                    for e in range(2):
                        rows = m.psum[:, 2 * o + e, 0:4 * NW].rearrange("p (g n) -> p g n", g=4)
                        dve.tensor_tensor(dst[:, i, 4 * e:4 * e + 4, :], rows[:, :, i * IC:(i + 1) * IC],
                                          w[:, :, o].unsqueeze(1).to_broadcast([P, 4, IC]), ALU.mult)
                dve.drain()
                if o:
                    dve.tensor_tensor(total, total, term, ALU.add)
                    dve.drain()
            dve.tensor_tensor(g_xc.rearrange("p c g -> p g c"), total[:, 0], total[:, 1], ALU.add)
            dve.tensor_copy(g_xm.rearrange("p c g -> p g c"), total[:, 2])
            dve.drain().then_inc(folded, 1)

    ig, lf, big, keep, cut, ws, wp = (m.rows[:, T * i:T * (i + 1)] for i in range(7))
    m0 = view(m.small, 464, B)
    wc_row = view(m.small, 472, B)
    ml = view(m.small, 480, 9)
    wcol = view(m.small, 496, H, B)

    def seqs(v):
        return v[:, T_P:T].rearrange("p (b t) -> p b t", b=B)

    with signal(m, "turned") as turned, signal(m, "e1") as e1, signal(m, "e2") as e2, \
            signal(m, "m_in") as m_in, signal(m, "m_out") as m_out, signal(m, "u_done") as u_done, \
            signal(m, "ends") as ends, signal(m, "m_done") as m_done, nc.Block() as block:
        @block.sync
        def _(sp):
            with nc.allow_non_contiguous_dma(reason="32 values"):
                sp.dma_start(m0[0:H, :], I["state_mlstm_m"][0].rearrange("b h -> h b")).then_inc(m_in, 16)
                sp.wait_ge(m_done, 1)
                sp.dma_start(O["p_m_m"].rearrange("a b h -> h (a b)"), ml[0:H, 0:1]).then_inc(m_out, 16)
                sp.dma_start(O["s_m_m"][0].rearrange("b h -> h b"), ml[0:H, 1:9]).then_inc(m_out, 16)
            sp.wait_ge(m_out, 32)

        @block.gpsimd
        def _(pool):
            pool.memset(keep, 1.0)
            pool.memset(cut, 0.0)
            pool.drain()
            for v, x in ((keep, 0.0), (cut, NEG)):
                pool.memset(v[:, 0:1], x)
                pool.memset(v[:, T_P:T:T_S], x)
            pool.drain().then_inc(ends, 1)

        @block.tensor
        def _(pe):
            pe.wait_ge(u_done, 1)
            for j, (t0, n) in enumerate(TILES):
                mm = pe.transpose(m.psum[0:n, 2, 4 * j:4 * j + 4], ig[:, t0:t0 + n], m.ident[0:4, 0:4])
            mm.then_inc(turned, 1)
            pe.wait_ge(u_done, 2)
            for h in range(H):
                mm = pe.matmul(m.psum[:, 3, B * h:B * h + B], m.ident[0:H, h:h + 1].to_broadcast([H, P]), wc_row[0:H, :],
                               start=(h == 0), stop=(h == H - 1), skip_group_check=True)
            mm.then_inc(turned, 1)

        @block.scalar
        def _(act):
            act.wait_ge(e1, 1)
            act.activation(ws, ws, ACT.Exp, scale=-1.0)
            act.drain()
            act.activation(ws, ws, ACT.Ln, bias=1.0).then_inc(e1, 1)
            act.wait_ge(e2, 1)
            act.activation(ws, ws, ACT.Exp)
            act.activation(wp, wp, ACT.Exp)
            act.activation(wc_row[0:H, :], wc_row[0:H, :], ACT.Exp)
            act.activation(lf, lf, ACT.Exp, scale=-1.0).then_inc(e2, 1)

        @block.vector
        def _(dve):
            dve.wait_ge(m_in, 16)
            dve.wait_ge(ends, 1)
            dve.tensor_scalar(ig, m.psum[0:4, 0, 0:T], bg[0:4, :], None, ALU.add)
            dve.tensor_scalar(lf, m.psum[0:4, 1, 0:T], bgf[0:4, :], None, ALU.add)
            dve.drain()
            dve.scalar_tensor_tensor(ws, lf, -1.0, lf, ALU.mult, ALU.max)
            dve.drain().then_inc(e1, 1)
            dve.wait_ge(e1, 2)
            dve.scalar_tensor_tensor(lf, lf, 0.0, ws, ALU.min, ALU.subtract)
            dve.drain()
            dve.tensor_tensor_scan(big, keep, lf, 0.0, ALU.mult, ALU.add)
            dve.drain()
            dve.tensor_tensor(ig, ig, big, ALU.subtract)
            dve.drain().then_inc(u_done, 1)
            dve.tensor_copy(wp, ig)
            dve.drain()
            dve.tensor_scalar(wp[:, 0:1], wp[:, 0:1], 0.0, None, ALU.max)
            dve.tensor_tensor(seqs(wp)[:, :, 0:1], seqs(wp)[:, :, 0:1], m0[0:H, :].unsqueeze(2), ALU.max)
            dve.drain()
            dve.tensor_tensor_scan(lf, cut, wp, 0.0, ALU.add, ALU.max)
            dve.drain()
            dve.tensor_copy(keep, lf)
            ends_m = lf[:, T_P + T_S - 1:T:T_S]
            dve.tensor_tensor(ws[:, 0:T_P], ig[:, 0:T_P], lf[:, T_P - 1:T_P].to_broadcast([4, T_P]), ALU.subtract)
            dve.tensor_tensor(seqs(ws), seqs(ig), ends_m.unsqueeze(2).to_broadcast([4, B, T_S]), ALU.subtract)
            dve.tensor_scalar(wp[:, 0:T_P], lf[:, 0:T_P], -1.0, None, ALU.mult)
            dve.tensor_tensor(seqs(wp), m0[0:H, :].unsqueeze(2).to_broadcast([4, B, T_S]), seqs(lf), ALU.subtract)
            dve.tensor_tensor(wc_row[0:H, :], m0[0:H, :], ends_m, ALU.subtract)
            dve.drain()
            dve.tensor_tensor(lf, lf, big, ALU.add)
            dve.drain()
            dve.tensor_copy(ml[0:H, 0:1], lf[:, T_P - 1:T_P])
            dve.tensor_copy(ml[0:H, 1:9], lf[:, T_P + T_S - 1:T:T_S])
            dve.drain().then_inc(m_done, 1)
            dve.drain().then_inc(e2, 1)
            dve.wait_ge(e2, 2)
            dve.drain().then_inc(u_done, 1)
            dve.wait_ge(turned, 2)
            for j, (t0, n) in enumerate(TILES):
                dve.tensor_copy(u_col[0:n, j, :], m.psum[0:n, 2, 4 * j:4 * j + 4])
            dve.tensor_copy(wcol.rearrange("p h b -> p (h b)"), m.psum[:, 3, 0:H * B])
    big_m = keep
    em = lf


    n0 = view(m.small, 528, B, H, HC)
    n_new = view(m.small, 784, 1 + B, H, HC)
    n_rows = view(m.arena, 20480, 2, P)
    rden = view(m.arena, 20480 + 2 * P, T)
    with signal(m, "n_in") as n_in, signal(m, "turned") as turned, nc.Block() as block:
        @block.sync
        def _(sp):
            src = I["state_mlstm_n"].rearrange("a b h (c p) -> (a b h c) p", p=P)
            for i in range(2):
                sp.dma_start(n_rows[:, i, :], src[i * P:(i + 1) * P, :]).then_inc(n_in, 16)

        @block.tensor
        def _(pe):
            pe.wait_ge(n_in, 32)
            for i in range(2):
                mm = pe.transpose(m.psum[:, 0, i * P:(i + 1) * P], n_rows[:, i, :], m.ident[:, :])
            mm.then_inc(turned, 1)

        @block.vector
        def _(dve):
            dve.wait_ge(turned, 1)
            dve.tensor_copy(n0.rearrange("p b h c -> p (b h c)"), m.psum[:, 0, 0:2 * P])

    c_slot = view(m.ring, 8192, HC, DH)
    s_t = [view(m.ring, 7424, T_P), view(m.ring, 7424 + T_P, P), view(m.ring, 7424 + T_P + P, 64)]
    vt = view(m.xn, 0, 3, DH)
    kt = view(m.xn, 3 * DH, 2, DH)
    k72, v72 = ([q_f[:, :, at + i * 64:at + (i + 1) * 64].bitcast(BF16) for i in range(2)] for at in (0, 128))
    q_one = [view(m.xn, 2 * DH + 512 * i, HC, 64) for i in range(2)]
    columns = m.ring[:, 4864:5120].bitcast(BF16).rearrange("p (b t) -> p b t", b=B)
    ones_at = view(m.arena, 21056, B, 64)
    num_tok = view(m.xn, 2 * DH, DH)
    k_one = [view(m.ring, 7936, 2, P), view(m.arena, 20480, 2, P)]
    c_stage = [view(m.ring, 7424, 512), view(m.arena, 21056, 512)]
    rep_words = HC * B * ROWS72 // 2
    krep = m.ring[:, 5120:5120 + rep_words].bitcast(BF16).rearrange("p (c b r) -> p c b r", c=HC, b=B)
    vrep = m.ring[:, 2560:2560 + rep_words].bitcast(BF16).rearrange("p (c b r) -> p c b r", c=HC, b=B)
    qn = view(m.ring, 14336, HC, 64)
    rest = view(m.ring, 14848, HC, 64)
    p16 = m.ring[:, 15360:15360 + HC * 32].bitcast(BF16).rearrange("p (c t) -> p c t", c=HC)
    wn = view(m.ring, 15872, HC, B)
    for h in range(H):
        xm_h, xc_h = xm[:, h * HC:(h + 1) * HC], xc[:, h * HC:(h + 1) * HC]
        with ExitStack() as ctx:
            expanded, prod, kept, v_kept, summed, centred, sqd, root = (ctx.enter_context(signal(m, n)) for n in (
                "expanded", "prod", "kept", "v_kept", "summed", "centred", "sqd", "root"))
            norm = HeadNorm(m, xm, xc, h - 1, summed, centred, sqd, root) if h else None
            block = ctx.enter_context(nc.Block())

            @block.vector
            def _(dve):
                def keep_v(chunks):
                    for c in chunks:
                        dve.wait_ge(prod, 3 * c + 3)
                        dve.tensor_copy(xm_h[:, c, :], m.psum[:, 3 * (c % 2) + 2, 0:T]).then_inc(v_kept, 1)

                expand(dve, h, range(0, 4), expanded)
                if norm:
                    norm.centre(dve)
                expand(dve, h, range(4, HC), expanded)
                keep_v(range(HC))
                if norm:
                    norm.variance(dve)
                    norm.invert(dve)

            @block.scalar
            def _(act):
                def keep_qk(chunks):
                    for c in chunks:
                        for i, dst in enumerate((q_f, k_f)):
                            act.wait_ge(prod, 3 * c + i + 1)
                            act.activation(dst[:, c, :], m.psum[:, 3 * (c % 2) + i, 0:T], ACT.Copy,
                                           scale=1.0 if i == 0 else DH ** -0.5).then_inc(kept, 1)

                keep_qk(range(0, 3))
                if norm:
                    norm.square(act)
                keep_qk(range(3, HC))
                if norm:
                    norm.take_root(act)

            @block.tensor
            def _(pe):
                def project(chunks):
                    for c in chunks:
                        if c >= 2:
                            pe.wait_ge(kept, 2 * (c - 1))
                            pe.wait_ge(v_kept, c - 1)
                        for i, src in enumerate((xc_h, xc_h, xm_h)):
                            pe.wait_ge(expanded, 3 * c + i + 1)
                            pe.matmul(m.psum[:, 3 * (c % 2) + i, 0:T], bd[:, i, c, :], src[:, c, :], start=True,
                                      stop=True).then_inc(prod, 1)

                if norm:
                    norm.sum(pe)
                project(range(0, 4))
                if norm:
                    norm.sum_squares(pe)
                project(range(4, HC))
        with signal(m, "scored") as scored, signal(m, "spread") as spread, signal(m, "arg") as arg, \
                signal(m, "weight") as weight, signal(m, "st_done") as st_done, signal(m, "den") as den, \
                nc.Block() as block:
            @block.tensor
            def _(pe):
                for i, row in enumerate((big_m, em, ws, wp)):
                    mm = pe.matmul(m.psum[:, 3 + i, 0:T], m.ident[0:H, h:h + 1].to_broadcast([H, P]), row, start=True,
                                   stop=True)
                mm.then_inc(spread, 1)
                for c in range(HC):
                    mm = pe.matmul(m.psum[0:64, 2, 0:64], k_f[:, c, T_P:T], q_f[:, c, T_P:T], start=(c == 0),
                                   stop=(c == HC - 1))
                mm.then_inc(scored, 1)
                for a in range(2):
                    for c in range(HC):
                        mm = pe.matmul(m.psum[:, a, 0:T_P - a * P], k_f[:, c, a * P:(a + 1) * P], q_f[:, c, a * P:T_P],
                                       start=(c == 0), stop=(c == HC - 1))
                mm.then_inc(scored, 1)
                pe.wait_ge(st_done, 1)
                pe.matmul(m.psum[:, 7, 0:T_P], m.ones[:, :], s_t[0], start=True, stop=False, skip_group_check=True)
                pe.matmul(m.psum[:, 7, P:T_P], m.ones[:, :], s_t[1], start=False, stop=False, skip_group_check=True)
                pe.matmul(m.psum[:, 7, T_P:T], m.ones[0:64, :], s_t[2][0:64, :], start=False, stop=False,
                          skip_group_check=True)
                for c in range(HC):
                    mm = pe.matmul(m.psum[:, 7, T_P:T], m.ones[:, :], qn[:, c, :], start=False, stop=(c == HC - 1),
                                   skip_group_check=True)
                mm.then_inc(den, 1)

            @block.scalar
            def _(act):
                for a in range(3):
                    n = TILES[a][1]
                    act.wait_ge(arg, a + 1)
                    act.activation(s_t[a][0:n, :], s_t[a][0:n, :], ACT.Exp, scale=-1.0).then_inc(weight, 1)

            @block.vector
            def _(dve):
                dve.wait_ge(spread, 1)
                for a, (t0, n) in enumerate(TILES):
                    end = T_P if a < 2 else T
                    dve.tensor_scalar(s_t[a][0:n, :], m.psum[0:n, 3, t0:end], u_col[0:n, a, h:h + 1], 0.0, ALU.subtract,
                                      ALU.max).then_inc(arg, 1)
                dve.wait_ge(scored, 1)
                q_s = q_f[:, :, T_P:T]
                dve.tensor_tensor(q_s, q_s, m.psum[:, 6, T_P:T].unsqueeze(1).to_broadcast([P, HC, 64]), ALU.mult)
                dve.drain()
                for b in range(B):
                    dve.tensor_tensor(qn[:, :, b * T_S:(b + 1) * T_S], q_s[:, :, b * T_S:(b + 1) * T_S],
                                      n0[:, b, h, :].unsqueeze(2).to_broadcast([P, HC, T_S]), ALU.mult)
                if norm:
                    norm.apply(dve)
                dve.wait_ge(scored, 2)
                for a, (t0, n) in enumerate(TILES):
                    dve.wait_ge(weight, a + 1)
                    dve.tensor_tensor(s_t[a][0:n, :], s_t[a][0:n, :], m.psum[0:n, a, 0:s_t[a].shape[1]], ALU.mult)
                dve.drain()
                for a, mask in enumerate((m.causal, m.causal, m.causal8)):
                    n = TILES[a][1]
                    dve.tensor_tensor(s_t[a][0:n, 0:n], s_t[a][0:n, 0:n], mask[0:n, 0:n], ALU.mult)
                dve.drain().then_inc(st_done, 1)
                dve.tensor_tensor(k_f, k_f, m.psum[:, 5, 0:T].unsqueeze(1).to_broadcast([P, HC, T]), ALU.mult)
                dve.wait_ge(den, 1)
                dve.tensor_copy(rden, m.psum[:, 7, 0:T])
                dve.drain()
                dve.scalar_tensor_tensor(rden, rden, -1.0, rden, ALU.mult, ALU.max)
                dve.drain()
                dve.tensor_tensor(rden, rden, m.psum[:, 4, 0:T], ALU.max)
                dve.drain()
                dve.reciprocal(rden, rden)
        states = ExitStack()
        landed = [states.enter_context(signal(m, f"state_landed{c}")) for c in range(HC)]
        c_in = I["state_mlstm_C"][0].rearrange("b h (c p) e -> b h c p e", p=P)
        LAG = 3
        with signal(m, "turned") as turned, signal(m, "copied") as copied, signal(m, "prompt_num") as prompt_num, \
                nc.Block() as block:
            @block.sync
            def _(sp):
                for c in range(HC - LAG):
                    sp.dma_start(c_slot[:, c, :], c_in[0, h, c]).then_inc(landed[c], 16)

            @block.tensor
            def _(pe):
                for j, (t0, n) in enumerate(TILES):
                    for c in range(HC):
                        mm = pe.transpose(m.psum[0:n, 2 * j + c // 4, (c % 4) * P:(c % 4 + 1) * P], xm_h[:, c, t0:t0 + n],
                                          m.ident[:, :])
                    mm.then_inc(turned, 1)
                for j, (t0, n) in enumerate(TILES[0:2]):
                    if j:
                        pe.wait_ge(copied, 1)
                    for c in range(HC):
                        bank = (6, 0)[j] + c // 4
                        mm = pe.transpose(m.psum[0:n, bank, (c % 4) * P:(c % 4 + 1) * P], k_f[:, c, t0:t0 + n],
                                          m.ident[:, :])
                    mm.then_inc(turned, 1)
                pe.wait_ge(copied, 3)
                for c in range(HC):
                    ps = m.psum[:, 2 + c // 2, (c % 2) * T_P:(c % 2 + 1) * T_P]
                    pe.matmul(ps, vt[:, 0, c * P:(c + 1) * P], s_t[0], start=True, stop=False, skip_group_check=True)
                    pe.matmul(ps[:, P:T_P], vt[:, 1, c * P:(c + 1) * P], s_t[1], start=False, stop=True,
                              skip_group_check=True).then_inc(prompt_num, 1)

            @block.gpsimd
            def _(pool):
                pool.memset(ones_at, 1.0)
                pool.drain()
                pool.affine_select(ones_at, ones_at, [[-T_S, B], [1, 64]], ALU.is_ge, 0.0, base=0, channel_multiplier=0)
                pool.drain()
                pool.affine_select(ones_at, ones_at, [[T_S, B], [-1, 64]], ALU.is_ge, 0.0, base=T_S - 1,
                                   channel_multiplier=0)

            @block.scalar
            def _(act):
                for j, (t0, n) in enumerate(TILES):
                    act.wait_ge(turned, j + 1)
                    act.copy(vt[0:n, j, :], m.psum[0:n, 2 * j:2 * j + 2, :].rearrange("p a b -> p (a b)")).then_inc(copied, 1)
                for j in range(2):
                    bank = (6, 0)[j]
                    act.wait_ge(turned, 4 + j)
                    act.copy(kt[:, j, :], m.psum[:, bank:bank + 2, :].rearrange("p a b -> p (a b)")).then_inc(copied, 1)

            @block.vector
            def _(dve):
                dve.tensor_reduce(n_new[:, 0, h, :].unsqueeze(2), k_f[:, :, 0:T_P], AX_X, ALU.add)
                for b in range(B):
                    dve.tensor_reduce(n_new[:, 1 + b, h, :].unsqueeze(2), k_f[:, :, T_P + b * T_S:T_P + (b + 1) * T_S],
                                      AX_X, ALU.add)
                    dve.tensor_scalar(wn[:, :, b], n0[:, b, h, :], wcol[:, h, b:b + 1], None, ALU.mult)
                dve.drain()
                dve.tensor_tensor(n_new[:, 1:1 + B, h, :], n_new[:, 1:1 + B, h, :], wn.rearrange("p c b -> p b c"), ALU.add)

                def split(source, rep, outer):
                    for i in range(SPL):
                        dve.tensor_copy(p16, source if i == 0 else rest)
                        dve.drain()
                        if i < SPL - 1:
                            dve.tensor_tensor(rest, source if i == 0 else rest, p16, ALU.subtract)
                        for j in range(SPL):
                            r = (i * SPL + j if outer else j * SPL + i) * T_S
                            dve.tensor_copy(rep[:, :, :, r:r + T_S], p16.rearrange("p c (b t) -> p c b t", b=B))
                        dve.drain()
                split(k_f[:, :, T_P:T], krep, True)
                dve.wait_ge(turned, 5)
                split(xm_h[:, :, T_P:T], vrep, False)
                for c in range(HC):
                    if c % 2 == 0:
                        dve.wait_ge(prompt_num, c + 2)
                    dve.tensor_tensor(xm_h[:, c, 0:T_P], m.psum[:, 2 + c // 2, (c % 2) * T_P:(c % 2 + 1) * T_P],
                                      rden[:, 0:T_P], ALU.mult)
        c_out = O["s_m_C"][0].rearrange("b h (c p) e -> b h c p e", p=P)
        c_prompt = O["p_m_C"][0, 0, h].rearrange("(c p) e -> c p e", p=P)
        with states as ctx:
            stored = [ctx.enter_context(signal(m, f"state_stored{c}")) for c in range(HC)]
            turned = ctx.enter_context(signal(m, "turned"))
            k_kept = ctx.enter_context(signal(m, "k_kept"))
            v_kept = ctx.enter_context(signal(m, "v_kept"))
            queries = ctx.enter_context(signal(m, "queries"))
            read = ctx.enter_context(signal(m, "read"))
            outer = ctx.enter_context(signal(m, "outer"))
            updated = ctx.enter_context(signal(m, "updated"))
            num = ctx.enter_context(signal(m, "num"))
            num_kept = ctx.enter_context(signal(m, "num_kept"))
            keys = ctx.enter_context(signal(m, "keys"))
            c_done = ctx.enter_context(signal(m, "c_done"))
            c_kept = ctx.enter_context(signal(m, "c_kept"))
            c_stored = [ctx.enter_context(signal(m, f"c_stored{e}")) for e in range(2)]
            block = ctx.enter_context(nc.Block())

            def one(v, i):
                return v[i] if isinstance(i, int) else v[bass.ds(i, 1)].squeeze(0)

            def at(i, odd, each, more=0):
                return i * (2 * each) + (odd * each + more)

            @block.sync
            def _(sp):
                def load(b, c):
                    sp.dma_start(c_slot[:, c, :], one(c_in, b)[h, c]).then_inc(landed[c], 16)

                def sequence(b, more):
                    for c in range(HC):
                        sp.wait_ge(updated, b * (2 * HC) + (2 * c + 4))
                        sp.dma_start(one(c_out, b)[h, c], c_slot[:, c, :]).then_inc(stored[c], 16)
                        if c < LAG:
                            if not (isinstance(b, int) and b == 0):
                                sp.wait_ge(stored[c - LAG + HC], b * 16)
                            load(b, c - LAG + HC)
                        elif more:
                            sp.wait_ge(stored[c - LAG], b * 16 + 16)
                            load(b + 1, c - LAG)
                        if c == HC // 2:
                            for e in range(2):
                                sp.wait_ge(c_kept, b * 2 + (e + 1))
                                sp.dma_start(one(c_prompt, b)[:, e * 512:(e + 1) * 512],
                                             c_stage[e]).then_inc(c_stored[e], 16)

                sequence(0, True)
                with sp.Fori(1, B - 1) as b:
                    sequence(b, True)
                sequence(B - 1, False)
                for c in range(HC):
                    sp.wait_ge(stored[c], 16 * B)
                for e in range(2):
                    sp.wait_ge(c_stored[e], 16 + 16 * B)

            @block.gpsimd
            def _(pool):
                def one_sequence(i, odd):
                    mask = columns[:, bass.ds(at(i, odd, 1), 1), :].to_broadcast([P, HC, 64])
                    pool.tensor_tensor(q_one[odd], q_f[:, :, T_P:T], mask, ALU.mult).then_inc(queries, 1)

                pool.tensor_copy(columns, ones_at)
                pool.drain()
                pool.wait_ge(read, 1)
                for odd in range(2):
                    one_sequence(0, odd)
                with pool.Fori(1, B // 2) as i:
                    for odd in range(2):
                        pool.wait_ge(read, at(i, odd, 1, 0))
                        one_sequence(i, odd)

            @block.tensor
            def _(pe):
                def turn(i, odd):
                    for j, rep in enumerate((krep, vrep)):
                        for c in range(HC):
                            mm = pe.matmul(m.psum[0:ROWS72, 1 + 2 * j + c // 4, (c % 4) * P:(c % 4 + 1) * P],
                                           rep[:, c, bass.ds(at(i, odd, 1), 1), :].squeeze(1), m.identb[:, :],
                                           start=True, stop=True)
                        mm.then_inc(turned, 1)

                def sequence(i, odd, last=False):
                    pe.wait_ge(queries, at(i, odd, 1, 1))
                    for c in range(HC):
                        pe.wait_ge(landed[c], at(i, odd, 16, 16))
                        for e in range(2):
                            mm = pe.matmul(m.psum[0:64, 7 * e, :], q_one[odd][:, c, :],
                                           c_slot[:, c, e * 512:(e + 1) * 512], start=False, stop=last and c == HC - 1,
                                           skip_group_check=True)
                        if c == HC - 1:
                            mm.then_inc(read, 1)
                        if c == 0:
                            pe.wait_ge(k_kept, at(i, odd, 1, 1))
                            pe.wait_ge(v_kept, at(i, odd, 1, 1))
                        for e in range(2):
                            pe.wait_ge(updated, at(i, odd, 2 * HC, 2 * c + e + 1))
                            pe.matmul(m.psum[:, 5 + e, :], k72[odd][0:ROWS72, c, :],
                                      v72[odd][0:ROWS72, 4 * e:4 * e + 4, :], start=True, stop=True).then_inc(outer, 1)
                        if c in (1, 2):
                            pe.wait_ge(keys, at(i, odd, 1, 1))
                            for a in range(2):
                                mm = pe.matmul(m.psum[:, c, :], k_one[odd][:, a, :],
                                               vt[:, a, (c - 1) * 512:c * 512], start=(a == 0), stop=(a == 1))
                            mm.then_inc(c_done, 1)
                        if c == HC // 2 and not last:
                            pe.wait_ge(c_kept, at(i, odd, 2, 2))
                            turn(i if odd == 0 else i + 1, 1 - odd)

                for e in range(2):
                    mm = pe.matmul(m.psum[0:64, 7 * e, :], s_t[2][0:64, :], vt[0:64, 2, e * 512:(e + 1) * 512], start=True,
                              stop=False, skip_group_check=True)
                mm.then_inc(read, 1)
                turn(0, 0)
                with pe.Fori(0, B // 2 - 1) as i:
                    sequence(i, 0)
                    sequence(i, 1)
                sequence(B // 2 - 1, 0)
                sequence(B // 2 - 1, 1, last=True)
                pe.drain().then_inc(num, 1)
                pe.wait_ge(num_kept, 2)
                for c in range(HC):
                    mm = pe.transpose(m.psum[:, 0, c * 64:(c + 1) * 64], num_tok[0:64, c * P:(c + 1) * P],
                                      m.ident[0:64, 0:64])
                mm.then_inc(num, 1)

            @block.scalar
            def _(act):
                for e in range(2):
                    act.sem_inc(c_stored[e], 16)
                act.wait_ge(read, 1)
                act.wait_ge(queries, 1)
                with act.Fori(0, B // 2) as i:
                    for odd in range(2):
                        act.copy(k_one[odd], kt[:, :, bass.ds(at(i, odd, P), P)]).then_inc(keys, 1)
                        act.wait_ge(turned, at(i, odd, 2, 1))
                        act.copy(k72[odd][0:ROWS72, :, :],
                                 m.psum[0:ROWS72, 1:3, :].rearrange("p a (c d) -> p (a c) d", d=P)).then_inc(k_kept, 1)
                        act.wait_ge(turned, at(i, odd, 2, 2))
                        act.copy(v72[odd][0:ROWS72, :, :],
                                 m.psum[0:ROWS72, 3:5, :].rearrange("p a (c d) -> p (a c) d", d=P)).then_inc(v_kept, 1)
                        for e in range(2):
                            act.wait_ge(c_done, at(i, odd, 2, e + 1))
                            act.wait_ge(c_stored[e], at(i, odd, 16, 16))
                            act.copy(c_stage[e], m.psum[:, 1 + e, :]).then_inc(c_kept, 1)
                act.wait_ge(num, 1)
                act.copy(num_tok[0:64, 0:512], m.psum[0:64, 0, :]).then_inc(num_kept, 1)

            @block.vector
            def _(dve):
                dve.sem_inc(updated, 2)
                with dve.Fori(0, B) as b:
                    for c in range(HC):
                        for e in range(2):
                            dve.wait_ge(outer, b * (2 * HC) + (2 * c + e + 1))
                            part_c = c_slot[:, c, e * 512:(e + 1) * 512]
                            dve.scalar_tensor_tensor(part_c, part_c, wcol[:, h, bass.ds(b, 1)], m.psum[:, 5 + e, :],
                                                     ALU.mult, ALU.add).then_inc(updated, 1)
                dve.wait_ge(num, 1)
                dve.tensor_copy(num_tok[0:64, 512:1024], m.psum[0:64, 7, :]).then_inc(num_kept, 1)
                dve.wait_ge(num, 2)
                dve.tensor_tensor(xm_h[:, :, T_P:T], m.psum[:, 0, :].rearrange("p (c t) -> p c t", c=HC),
                                  rden[:, T_P:T].unsqueeze(1).to_broadcast([P, HC, 64]), ALU.mult)
    with signal(m, "summed") as summed, signal(m, "centred") as centred, signal(m, "sqd") as sqd, \
            signal(m, "root") as root, nc.Block() as block:
        norm = HeadNorm(m, xm, xc, H - 1, summed, centred, sqd, root)

        @block.tensor
        def _(pe):
            norm.sum(pe)
            norm.sum_squares(pe)

        @block.scalar
        def _(act):
            norm.square(act)
            norm.take_root(act)

        @block.vector
        def _(dve):
            norm.centre(dve)
            norm.variance(dve)
            norm.invert(dve)
            norm.apply(dve)
    store_columns(nc, m, n_new.rearrange("p b h c -> p (b h c)"), 9 * H * HC, [
        (0, H * HC, O["p_m_n"].rearrange("a b h (c p) -> (a b h c) p", p=P)),
        (H * HC, 9 * H * HC, O["s_m_n"].rearrange("a b h (c p) -> (a b h c) p", p=P))])

    def gate_with_z(dve, e, n):
        y = xm[:, bass.ds(n, 1), :].squeeze(1)
        return dve.tensor_tensor(y, y, e, ALU.mult)

    linear(nc, m, I["l1_w_up"][0][:, DI:2 * DI], DC, lambda k: m.XN[:, k, :], gate=gate_with_z,
           norm=("norm_mix_g", DC))
    linear(nc, m, I["l1_w_down"][0], IC, lambda k: xm[:, k, :])


def build(nc, I, O):
    with ExitStack() as ctx:
        m = Mem(nc, ctx)
        proj = view(m.arena, 0, IN0C + 1, T)
        setup(nc, m, I)
        first_projection(nc, m, I)
        rg_lru(nc, m, I, O)
        gla(nc, m, I, O)
        linear(nc, m, I["l0_w_out"][0], DC, lambda k: proj[:, GA + k if k < 8 else GG + k - 8, :])
        moe(nc, m, I, 0)
        mlstm(nc, m, I, O)
        moe(nc, m, I, 1)
        final_norm(nc, m, O)


INS = """x_prompt x_sample state_lru_conv state_lru_h state_gla_S state_mlstm_conv state_mlstm_C state_mlstm_n
state_mlstm_m norm_mix_g norm_ffn_g norm_final_g l0_w_in l0_lru_conv_w l0_lru_conv_b l0_lru_wa l0_lru_ba l0_lru_wx
l0_lru_bx l0_lru_lam l0_gla_wa2 l0_gla_ba2 l0_gla_norm_g l0_w_out l1_w_up l1_conv_w l1_conv_b l1_wq l1_wk l1_wv l1_w_ig
l1_b_ig l1_w_fg l1_b_fg l1_skip l1_norm_g l1_w_down moe_w_rg moe_b_rg moe_w_re moe_b_re moe_w_gate moe_w_up
moe_w_down""".split()
OUTS = [("y_prompt", (1, T_P, D)), ("y_sample", (B, T_S, D))] + [
    (f"{g}_{name}", (1, n) + shape) for g, n in (("p", 1), ("s", B)) for name, shape in (
        ("lru_conv", (CW - 1, W_LRU)), ("lru_h", (W_LRU,)), ("gla_S", (H, DK, DV)), ("m_conv", (CW - 1, DI)),
        ("m_C", (H, DH, DH)), ("m_n", (H, DH)), ("m_m", (H,)))]


def kernel(**inputs):
    import numpy as np
    import concourse.bacc as bacc
    from concourse.bass_utils import run_bass_kernel_spmd

    nc = bacc.Bacc("TRN2", target_bir_lowering=False, num_devices=1)
    arrays, ins, outs = {}, {}, {}
    for name in INS:
        a = np.ascontiguousarray(inputs[name])
        arrays[f"in_{name}"] = a
        ins[name] = nc.dram_tensor(f"in_{name}", a.shape, mybir.dt.from_np(a.dtype), kind="ExternalInput").ap()
    for name, shape in OUTS:
        outs[name] = nc.dram_tensor(f"out_{name}", shape, F32, kind="ExternalOutput").ap()
    build(nc, ins, outs)
    r = run_bass_kernel_spmd(nc, [arrays], core_ids=[0])
    return tuple(r.results[0][f"out_{name}"] for name, _ in OUTS)
```
